# Optimizing a Trainium2 kernel written in Bass

```python
import jax, jax.numpy as jnp
from jax import lax
import numpy as np
import math

D_MODEL = 1024
BATCH = 1
SEQ = 1024
DEPTH = 1

CHUNK = 64
D_MIX = D_MODEL
HEAD_DIM = 64
N_HEADS_A = 8
N_HEADS_B = 8
D_A = N_HEADS_A * HEAD_DIM
D_B = N_HEADS_B * HEAD_DIM
SG_BLOCK = 128
Q_BLOCK = 128
D_FF = 2816
CONV_W = 3
EPS = 1e-6
D_IN = 2 * D_A + 3 * D_B + N_HEADS_B


def rms_norm(x, g):
    xf = x.astype(jnp.float32)
    y = xf * lax.rsqrt(jnp.mean(xf * xf, axis=-1, keepdims=True) + EPS)
    return (y * g.astype(jnp.float32)).astype(x.dtype)

def spatial_gating(u, v, ln_g, w_s, b_s):
    B, S, _ = u.shape
    n = S // SG_BLOCK
    v = v.reshape(B, n, SG_BLOCK, N_HEADS_A, HEAD_DIM)
    vf = v.astype(jnp.float32)
    mu = jnp.mean(vf, axis=-1, keepdims=True)
    var = jnp.mean(jnp.square(vf - mu), axis=-1, keepdims=True)
    vn = ((vf - mu) * lax.rsqrt(var + EPS) * ln_g.astype(jnp.float32)).astype(u.dtype)
    pos_chunk = jnp.arange(SG_BLOCK) // CHUNK
    mask = pos_chunk[:, None] >= pos_chunk[None, :]
    w = jnp.where(mask[None], w_s, 0).astype(u.dtype)
    mixed = jnp.einsum('hts,bnshd->bnthd', w, vn) + b_s.T.astype(u.dtype)[None, None, :, :, None]
    out = u.reshape(B, n, SG_BLOCK, N_HEADS_A, HEAD_DIM) * mixed
    return out.reshape(B, S, D_A)

def forgetting_attention(q, k, v, f_logit):
    B, S, H, Dh = q.shape
    n = S // Q_BLOCK
    scale = Dh ** -0.5
    c = jnp.cumsum(jax.nn.log_sigmoid(f_logit.astype(jnp.float32)), axis=1)
    c = c.transpose(0, 2, 1)
    qb = q.reshape(B, n, Q_BLOCK, H, Dh).transpose(1, 0, 3, 2, 4)
    cb = c.reshape(B, H, n, Q_BLOCK).transpose(2, 0, 1, 3)
    kpos = jnp.arange(S)

    def block(args):
        i, qi, ci = args
        s = jnp.einsum('bhtd,bshd->bhts', qi, k, preferred_element_type=jnp.float32) * scale
        s = s + ci[..., :, None] - c[:, :, None, :]
        qpos = i * Q_BLOCK + jnp.arange(Q_BLOCK)
        s = jnp.where(kpos[None, :] <= qpos[:, None], s, -jnp.inf)
        p = jax.nn.softmax(s, axis=-1)
        return jnp.einsum('bhts,bshd->bthd', p.astype(v.dtype), v)

    out = lax.map(block, (jnp.arange(n), qb, cb))
    return out.transpose(1, 0, 2, 3, 4).reshape(B, S, H * Dh)

def conv_ffn(h, w_up, w_conv, b_conv, w_down):
    a = h @ w_up
    C = a.shape[-1]
    a = lax.conv_general_dilated(
        a, w_conv[:, None, :].astype(a.dtype), window_strides=(1,),
        padding=[(CONV_W - 1, 0)], dimension_numbers=('NWC', 'WIO', 'NWC'),
        feature_group_count=C) + b_conv.astype(a.dtype)
    g, val = jnp.split(a, 2, axis=-1)
    return (jax.nn.silu(g) * val) @ w_down

def first_inputs(seed: int = 0) -> dict:
    key = jax.random.key(seed)
    ks = jax.random.split(key, 14)
    L = DEPTH
    nrm = jax.random.normal
    return {
        "x": nrm(ks[0], (BATCH, SEQ, D_MODEL), jnp.float32),
        "norm_mix_g": 1.0 + 0.02 * nrm(ks[1], (L, D_MODEL), jnp.float32),
        "w_in": nrm(ks[2], (L, D_MODEL, D_IN), jnp.float32) * D_MODEL ** -0.5,
        "f_bias": 3.0 + 0.5 * nrm(ks[3], (L, N_HEADS_B), jnp.float32),
        "sg_ln_g": 1.0 + 0.02 * nrm(ks[4], (L, N_HEADS_A, HEAD_DIM), jnp.float32),
        "sg_w": nrm(ks[5], (L, N_HEADS_A, SG_BLOCK, SG_BLOCK), jnp.float32) * SG_BLOCK ** -0.5,
        "sg_b": 1.0 + 0.1 * nrm(ks[6], (L, N_HEADS_A, SG_BLOCK), jnp.float32),
        "w_out": nrm(ks[7], (L, D_MIX, D_MODEL), jnp.float32) * D_MIX ** -0.5,
        "norm_ffn_g": 1.0 + 0.02 * nrm(ks[8], (L, D_MODEL), jnp.float32),
        "w_up": nrm(ks[9], (L, D_MODEL, 2 * D_FF), jnp.float32) * D_MODEL ** -0.5,
        "w_conv": nrm(ks[10], (L, CONV_W, 2 * D_FF), jnp.float32) * CONV_W ** -0.5,
        "b_conv": 0.02 * nrm(ks[11], (L, 2 * D_FF), jnp.float32),
        "w_down": nrm(ks[12], (L, D_FF, D_MODEL), jnp.float32) * D_FF ** -0.5,
        "norm_final_g": 1.0 + 0.02 * nrm(ks[13], (D_MODEL,), jnp.float32),
    }

def first_block(x, norm_mix_g, w_in, f_bias, sg_ln_g, sg_w, sg_b, w_out,
              norm_ffn_g, w_up, w_conv, b_conv, w_down, norm_final_g):
    B, S, _ = x.shape
    for l in range(DEPTH):
        h = rms_norm(x, norm_mix_g[l])
        z = h @ w_in[l]
        o = 0
        u_a = jax.nn.gelu(z[..., o:o + D_A], approximate=False); o += D_A
        v_a = jax.nn.gelu(z[..., o:o + D_A], approximate=False); o += D_A
        q_b = z[..., o:o + D_B].reshape(B, S, N_HEADS_B, HEAD_DIM); o += D_B
        k_b = z[..., o:o + D_B].reshape(B, S, N_HEADS_B, HEAD_DIM); o += D_B
        v_b = z[..., o:o + D_B].reshape(B, S, N_HEADS_B, HEAD_DIM); o += D_B
        f_logit = z[..., o:o + N_HEADS_B] + f_bias[l].astype(z.dtype)
        out_a = spatial_gating(u_a, v_a, sg_ln_g[l], sg_w[l], sg_b[l])
        out_b = forgetting_attention(q_b, k_b, v_b, f_logit)
        x = x + jnp.concatenate([out_a, out_b], axis=-1) @ w_out[l]
        x = x + conv_ffn(rms_norm(x, norm_ffn_g[l]), w_up[l], w_conv[l], b_conv[l], w_down[l])
    return rms_norm(x, norm_final_g)


DEPTH_2 = 2

GRID_W = 64
CTX_LEN = 256
A_HEADS = D_MODEL // (2 * HEAD_DIM)
A_WIDTH = A_HEADS * 2 * HEAD_DIM
A_IN_WIDTH = 4 * A_WIDTH
B_HEADS = D_MODEL // HEAD_DIM
B_KV_HEADS = 4
B_GROUP = B_HEADS // B_KV_HEADS
B_WIDTH = B_HEADS * HEAD_DIM
B_KV_WIDTH = B_KV_HEADS * HEAD_DIM
B_IN_WIDTH = 2 * B_WIDTH + 2 * B_KV_WIDTH
MIX_WIDTH = A_WIDTH
WINDOW = 128
BAND = Q_BLOCK + 2 * WINDOW
ROPE_THETA = 10000.0
NORM_EPS = 1e-6
SUBLN_EPS = 1e-5
NEG_INF = -1e30
ATTN_SCALE = HEAD_DIM ** -0.5
N_A_LAYERS = (DEPTH_2 + 1) // 2
N_B_LAYERS = DEPTH_2 // 2


def rms_norm_2(x, g, eps=NORM_EPS):
    x32 = x.astype(jnp.float32)
    y = x32 * lax.rsqrt(jnp.mean(x32 * x32, axis=-1, keepdims=True) + eps)
    return (y * g.astype(jnp.float32)).astype(x.dtype)

def modulate(h, shift, scale):
    return h * (1.0 + scale) + shift

def axial_angles(rows, rot_dim=HEAD_DIM):
    row = jnp.repeat(jnp.arange(rows, dtype=jnp.int32), GRID_W).astype(jnp.float32)
    col = jnp.tile(jnp.arange(GRID_W, dtype=jnp.int32), rows).astype(jnp.float32)
    axis_dim = rot_dim // 2
    inv_freq = ROPE_THETA ** (-jnp.arange(0, axis_dim, 2, dtype=jnp.float32) / axis_dim)
    return row[:, None] * inv_freq, col[:, None] * inv_freq

def rope_1d(x, ang):
    ang = ang.reshape(ang.shape[:1] + (1,) * (x.ndim - 3) + ang.shape[1:])
    cos, sin = jnp.cos(ang), jnp.sin(ang)
    x1, x2 = jnp.split(x.astype(jnp.float32), 2, axis=-1)
    return jnp.concatenate([x1 * cos - x2 * sin, x2 * cos + x1 * sin], axis=-1).astype(x.dtype)

def rope_axial(x, ang_r, ang_c):
    xr, xc = jnp.split(x, 2, axis=-1)
    return jnp.concatenate([rope_1d(xr, ang_r), rope_1d(xc, ang_c)], axis=-1)

def diff_attention_mixer(hx, hc, w_in, lq1, lk1, lq2, lk2, subln_g, layer_idx, with_ctx_out, ang_r, ang_c):
    B, S, _ = hx.shape
    nblk = S // Q_BLOCK
    lam_init = 0.8 - 0.6 * math.exp(-0.3 * layer_idx)
    f32 = jnp.float32
    lam = (jnp.exp(jnp.sum(lq1.astype(f32) * lk1.astype(f32)))
           - jnp.exp(jnp.sum(lq2.astype(f32) * lk2.astype(f32))) + lam_init)

    def split(p):
        q, k, v, g = jnp.split(p, [A_WIDTH, 2 * A_WIDTH, 3 * A_WIDTH], axis=-1)
        lead = p.shape[:2]
        return (q.reshape(lead + (A_HEADS, 2, HEAD_DIM)),
                k.reshape(lead + (A_HEADS, 2, HEAD_DIM)),
                v.reshape(lead + (A_HEADS, 2 * HEAD_DIM)), g)

    qx, kx, vx, gx = split(hx @ w_in)
    qc, kc, vc, gc = split(hc @ w_in)
    qx = rope_axial(qx, ang_r, ang_c)
    kx = rope_axial(kx, ang_r, ang_c)
    k_all = jnp.concatenate([kc, kx], axis=1)
    v_all = jnp.concatenate([vc, vx], axis=1)

    def attend(qb, keys, vals):
        s = jnp.einsum('bqhmd,bkhmd->bhmqk', qb, keys).astype(f32) * ATTN_SCALE
        p = jax.nn.softmax(s, axis=-1)
        a = p[:, :, 0] - lam * p[:, :, 1]
        return jnp.einsum('bhqk,bkhe->bqhe', a.astype(vals.dtype), vals)

    q_blocks = qx.reshape(B, nblk, Q_BLOCK, A_HEADS, 2, HEAD_DIM).swapaxes(0, 1)
    ox = lax.map(lambda qb: attend(qb, k_all, v_all), q_blocks)
    ox = ox.swapaxes(0, 1).reshape(B, S, A_HEADS, 2 * HEAD_DIM)

    def finish(o, g):
        o = rms_norm_2(o, subln_g, SUBLN_EPS) * (1.0 - lam_init)
        return o.reshape(o.shape[:2] + (A_WIDTH,)) * jax.nn.silu(g)

    out_x = finish(ox, gx)
    out_c = finish(attend(qc, kc, vc), gc) if with_ctx_out else None
    return out_x, out_c

def window_gqa_mixer(hx, hc, w_in, sink, with_ctx_out, ang_r, ang_c):
    B, S, _ = hx.shape
    nblk = S // Q_BLOCK
    f32 = jnp.float32

    def split(p):
        q, k, v, g = jnp.split(p, [B_WIDTH, B_WIDTH + B_KV_WIDTH, B_WIDTH + 2 * B_KV_WIDTH], axis=-1)
        lead = p.shape[:2]
        return (q.reshape(lead + (B_KV_HEADS, B_GROUP, HEAD_DIM)),
                k.reshape(lead + (B_KV_HEADS, HEAD_DIM)),
                v.reshape(lead + (B_KV_HEADS, HEAD_DIM)), g)

    qx, kx, vx, gx = split(hx @ w_in)
    qc, kc, vc, gc = split(hc @ w_in)
    qx = rope_axial(qx, ang_r, ang_c)
    kx = rope_axial(kx, ang_r, ang_c)
    n_ctx = kc.shape[1]
    sink_f = sink.astype(f32).reshape(B_KV_HEADS, B_GROUP)[None, :, :, None, None]

    def sink_softmax(s):
        sb = jnp.broadcast_to(sink_f, s.shape[:-1] + (1,))
        return jax.nn.softmax(jnp.concatenate([s, sb], axis=-1), axis=-1)[..., :-1]

    pad = ((0, 0), (WINDOW, WINDOW), (0, 0), (0, 0))
    kp = jnp.pad(kx, pad)
    vp = jnp.pad(vx, pad)
    q_blocks = qx.reshape(B, nblk, Q_BLOCK, B_KV_HEADS, B_GROUP, HEAD_DIM).swapaxes(0, 1)

    def block(args):
        qb, i = args
        start = i * Q_BLOCK
        kb = lax.dynamic_slice_in_dim(kp, start, BAND, axis=1)
        vb = lax.dynamic_slice_in_dim(vp, start, BAND, axis=1)
        qpos = start + jnp.arange(Q_BLOCK)
        kpos = start - WINDOW + jnp.arange(BAND)
        mask = ((jnp.abs(qpos[:, None] - kpos[None, :]) <= WINDOW)
                & (kpos >= 0)[None, :] & (kpos < S)[None, :])
        s_band = jnp.einsum('bqhgd,bjhd->bhgqj', qb, kb).astype(f32) * ATTN_SCALE
        s_band = jnp.where(mask, s_band, NEG_INF)
        s_ctx = jnp.einsum('bqhgd,bjhd->bhgqj', qb, kc).astype(f32) * ATTN_SCALE
        p = sink_softmax(jnp.concatenate([s_ctx, s_band], axis=-1)).astype(vb.dtype)
        return (jnp.einsum('bhgqj,bjhd->bqhgd', p[..., :n_ctx], vc)
                + jnp.einsum('bhgqj,bjhd->bqhgd', p[..., n_ctx:], vb))

    ox = lax.map(block, (q_blocks, jnp.arange(nblk)))
    out_x = ox.swapaxes(0, 1).reshape(B, S, B_WIDTH) * jax.nn.silu(gx)
    out_c = None
    if with_ctx_out:
        s = jnp.einsum('bqhgd,bjhd->bhgqj', qc, kc).astype(f32) * ATTN_SCALE
        p = sink_softmax(s).astype(vc.dtype)
        oc = jnp.einsum('bhgqj,bjhd->bqhgd', p, vc)
        out_c = oc.reshape(oc.shape[:2] + (B_WIDTH,)) * jax.nn.silu(gc)
    return out_x, out_c

def second_inputs(seed: int = 0) -> dict:
    key = jax.random.key(seed)
    ks = jax.random.split(key, 17)
    nrm = jax.random.normal
    f32 = jnp.float32
    return {
        'x': nrm(ks[0], (BATCH, SEQ, D_MODEL), f32),
        'c': nrm(ks[1], (BATCH, D_MODEL), f32),
        'ctx': nrm(ks[2], (BATCH, CTX_LEN, D_MODEL), f32),
        'c_ctx': nrm(ks[3], (D_MODEL,), f32),
        'w_mod': nrm(ks[4], (DEPTH_2, D_MODEL, 3 * D_MODEL), f32) * D_MODEL ** -0.5,
        'b_mod': 0.01 * nrm(ks[5], (DEPTH_2, 3 * D_MODEL), f32),
        'norm_g': 1.0 + 0.02 * nrm(ks[6], (DEPTH_2, D_MODEL), f32),
        'w_o': nrm(ks[7], (DEPTH_2, MIX_WIDTH, D_MODEL), f32) * MIX_WIDTH ** -0.5,
        'a_w_in': nrm(ks[8], (N_A_LAYERS, D_MODEL, A_IN_WIDTH), f32) * D_MODEL ** -0.5,
        'a_lambda_q1': 0.1 * nrm(ks[9], (N_A_LAYERS, HEAD_DIM), f32),
        'a_lambda_k1': 0.1 * nrm(ks[10], (N_A_LAYERS, HEAD_DIM), f32),
        'a_lambda_q2': 0.1 * nrm(ks[11], (N_A_LAYERS, HEAD_DIM), f32),
        'a_lambda_k2': 0.1 * nrm(ks[12], (N_A_LAYERS, HEAD_DIM), f32),
        'a_subln_g': 1.0 + 0.02 * nrm(ks[13], (N_A_LAYERS, 2 * HEAD_DIM), f32),
        'b_w_in': nrm(ks[14], (N_B_LAYERS, D_MODEL, B_IN_WIDTH), f32) * D_MODEL ** -0.5,
        'b_sink': 0.5 * nrm(ks[15], (N_B_LAYERS, B_HEADS), f32),
        'final_g': 1.0 + 0.02 * nrm(ks[16], (D_MODEL,), f32),
    }

def second_block(x, c, ctx, c_ctx, w_mod, b_mod, norm_g, w_o, a_w_in, a_lambda_q1, a_lambda_k1,
              a_lambda_q2, a_lambda_k2, a_subln_g, b_w_in, b_sink, final_g):
    n_tokens = x.shape[1]
    rows = n_tokens // GRID_W
    ang_r, ang_c = axial_angles(rows)
    sc = jax.nn.silu(c)
    sctx = jax.nn.silu(c_ctx)
    for i in range(DEPTH_2):
        last = i == DEPTH_2 - 1
        shift_x, scale_x, gate_x = jnp.split(sc @ w_mod[i] + b_mod[i], 3, axis=-1)
        shift_c, scale_c, gate_c = jnp.split(sctx @ w_mod[i] + b_mod[i], 3, axis=-1)
        hx = modulate(rms_norm_2(x, norm_g[i]), shift_x[:, None], scale_x[:, None])
        hc = modulate(rms_norm_2(ctx, norm_g[i]), shift_c, scale_c)
        j = i // 2
        if i % 2 == 0:
            ox, oc = diff_attention_mixer(hx, hc, a_w_in[j], a_lambda_q1[j], a_lambda_k1[j],
                                          a_lambda_q2[j], a_lambda_k2[j], a_subln_g[j], i,
                                          not last, ang_r, ang_c)
        else:
            ox, oc = window_gqa_mixer(hx, hc, b_w_in[j], b_sink[j], not last, ang_r, ang_c)
        x = x + gate_x[:, None] * (ox @ w_o[i])
        if not last:
            ctx = ctx + gate_c * (oc @ w_o[i])
    return rms_norm_2(x, final_g)


def setup_inputs(seed=0):
    out = dict(first_inputs(seed))
    for name, value in second_inputs(seed + 1).items():
        if name != "x":
            out[name + "_2"] = value
    return out


def reference(
    x, norm_mix_g, w_in, f_bias, sg_ln_g, sg_w, sg_b, w_out, norm_ffn_g, w_up, w_conv, b_conv,
    w_down, norm_final_g, c_2, ctx_2, c_ctx_2, w_mod_2, b_mod_2, norm_g_2, w_o_2, a_w_in_2,
    a_lambda_q1_2, a_lambda_k1_2, a_lambda_q2_2, a_lambda_k2_2, a_subln_g_2, b_w_in_2, b_sink_2,
    final_g_2,
):
    x = first_block(
        x, norm_mix_g, w_in, f_bias, sg_ln_g, sg_w, sg_b, w_out, norm_ffn_g, w_up, w_conv,
        b_conv, w_down, norm_final_g,
    )
    return second_block(
        x, c_2, ctx_2, c_ctx_2, w_mod_2, b_mod_2, norm_g_2, w_o_2, a_w_in_2, a_lambda_q1_2,
        a_lambda_k1_2, a_lambda_q2_2, a_lambda_k2_2, a_subln_g_2, b_w_in_2, b_sink_2, final_g_2,
    )


_drawn_inputs = setup_inputs


def setup_inputs(seed=0):
    import zlib

    import numpy as np

    out = dict(_drawn_inputs(seed))
    spreads = {}
    factors = {'norm_mix_g': 3.295,
     'sg_ln_g': 7.86,
     'norm_ffn_g': 4.504,
     'b_conv': 4.303,
     'norm_final_g': 2.705,
     'b_mod_2': 4.468,
     'norm_g_2': 5.507,
     'a_lambda_q1_2': 7.545,
     'a_lambda_k1_2': 8.0,
     'a_subln_g_2': 7.719,
     'b_sink_2': 8.0,
     'final_g_2': 2.742}
    for name, (base, spread) in spreads.items():
        noise = np.random.default_rng([zlib.crc32(name.encode()), seed]).standard_normal(out[name].shape)
        drawn = base * np.exp(spread * noise) if base else spread * noise
        out[name] = __import__('jax').numpy.asarray(drawn.astype(out[name].dtype))
    for name, factor in factors.items():
        out[name] = (out[name] * factor).astype(out[name].dtype)
    return out
```

```python
from contextlib import ExitStack

import concourse.bass as bass
from concourse import mybir

F32 = mybir.dt.float32
F32R = mybir.dt.float32r
ALU = mybir.AluOpType
ACT = mybir.ActivationFunctionType
AX = mybir.AxisListType.X

P = 128
D = 1024
KT = D // P
CTX = 256
SEQ = 1024
TOK = CTX + SEQ
BANK = 512
DH = 64
D_FF = 2816
FT = D_FF // P
CHUNKS = FT // 2
QB = SEQ // P
EPS = 1e-6
SUB_EPS = 1e-5
LAM_INIT = 0.8 - 0.6
SCALE = DH ** -0.5
LOWEST = -3.0e38

V_MIX, V_FFN, V_FIN, V_G2, V_FG2, V_BMOD, V_SUB, V_LNG, V_C, V_END = 0, 8, 16, 24, 40, 48, 96, 97, 101, 117

X_COLS = slice(CTX, TOK)
LEAD = 2


def batches(blocks):
    return [range(n, min(n + 4, blocks)) for n in range(0, blocks, 4)]


def da_tiles(u):
    return CTX // P if u < CTX // P else TOK // P


def da_plan():
    turns = [("v", n) for n in range(len(batches(TOK // P)))]
    for u in range(TOK // P):
        turns += [("p", u, n) for n in range(len(batches(da_tiles(u))))]
        if u >= 2 and u % 2 == 0:
            turns.append(("sum", u // 2 - 1))
        if u % 2 == 1:
            turns.append(("out", u // 2))
    turns.append(("sum", TOK // P // 2 - 1))
    return {key: (n % 2, n // 2) for n, key in enumerate(turns)}


DA_PLAN = da_plan()
DA_TURNS = [sum(b == n for b, _ in DA_PLAN.values()) for n in range(2)]


def da_turned(u):
    return len(batches(TOK // P)) + sum(len(batches(da_tiles(v))) for v in range(u + 1))


DA_BATCHES = da_turned(TOK // P - 1)


def window_tiles(i):
    return [2 + i - 1] * (i > 0) + [0, 1, 2 + i] + [2 + i + 1] * (i < QB - 1)


def two_block_kernel(
    nc, x, norm_mix_g, w_in, f_bias, sg_ln_g, sg_w, sg_b, w_out, norm_ffn_g, w_up, w_conv, b_conv, w_down,
    norm_final_g, c_2, ctx_2, c_ctx_2, w_mod_2, b_mod_2, norm_g_2, w_o_2, a_w_in_2, a_lambda_q1_2, a_lambda_k1_2,
    a_lambda_q2_2, a_lambda_k2_2, a_subln_g_2, b_w_in_2, b_sink_2, final_g_2,
    const_ident, const_swap, const_causal, const_before, const_cos, const_sin, out,
):
    z1 = nc.dram_tensor("z1", (20 * P, SEQ), F32, kind="Internal").ap()
    forget_rows = nc.dram_tensor("forget_rows", (2, 8, SEQ), F32, kind="Internal").ap()
    za = nc.dram_tensor("za", (32 * P, TOK), F32, kind="Internal").ap()
    zb = nc.dram_tensor("zb", (20 * P, TOK), F32, kind="Internal").ap()

    with ExitStack() as ctx:
        def alloc(scope, name, shape, dt=F32):
            return scope.enter_context(nc.sbuf_tensor(name, shape, dt))

        def sb(name, shape, dt=F32):
            return alloc(ctx, name, shape, dt)

        def sem(name):
            return ctx.enter_context(nc.semaphore(name))

        def sem2(name):
            return [sem(f"{name}{s}") for s in range(2)]

        res = sb("res", [P, KT, TOK])
        hh = sb("hh", [P, KT, TOK], F32R)
        hl = sb("hl", [P, KT, TOK], F32R)
        w_raw = sb("w_raw", [P, 2, KT * P])
        wh = sb("wh", [P, 2, KT * P], F32R)
        wl = sb("wl", [P, 2, KT * P], F32R)
        ident = sb("ident", [P, P])
        ones = sb("ones", [P, P])
        swap = sb("swap", [P, P])
        masks = sb("masks", [P, 3, P], F32R)
        ones_r = sb("ones_r", [2, P], F32R)
        vec = sb("vec", [P, V_END])
        vec32 = sb("vec32", [P, V_BMOD])
        convv = sb("convv", [P, 4 * 2 * FT])
        mod = sb("mod", [P, 48, 2])
        modg = sb("modg", [P, 2, 2, KT])
        zero = sb("zero", [P, 1])
        eps_d = sb("eps_d", [P, 1])
        eps_sub = sb("eps_sub", [P, 1])
        one = sb("one", [P, 1])
        eps_1 = sb("eps_1", [P, 1])
        lam = sb("lam", [P, 1])
        subg = sb("subg", [P, 1])
        sinks = sb("sinks", [P, 16])
        fb = sb("fb", [8, 1])
        s_wt = sb("s_wt", [P, 2, P])
        ps = ctx.enter_context(nc.psum_tensor("ps", [P, 8 * BANK], F32))

        def bank(b, n=1):
            return ps[:, b * BANK:(b + n) * BANK]

        acc = [bank(0, 3), bank(3, 3)]

        scope = ExitStack()
        tokrows = alloc(scope, "tokrows", [P, 2, D])
        rows = alloc(scope, "rows", [P, P])
        convrows = alloc(scope, "convrows", [88, 2, P])
        w_mod_sb = alloc(scope, "w_mod_sb", [P, 2, KT, 2 * P])
        cond = alloc(scope, "cond", [P, KT, 2])
        lamrows = alloc(scope, "lamrows", [P, 4, DH])
        maskrows = alloc(scope, "maskrows", [P, 2, P])
        lamt = alloc(scope, "lamt", [P, 4])
        scope.close()
        scope = ExitStack()
        n_sq = alloc(scope, "n_sq", [P, 2, SEQ])
        n_sum = alloc(scope, "n_sum", [P, SEQ])
        n_rs = alloc(scope, "n_rs", [P, SEQ])
        n_t = alloc(scope, "n_t", [P, 2, SEQ])
        n_h = alloc(scope, "n_h", [P, 2, SEQ])
        tok_out = alloc(scope, "tok_out", [P, 2, KT, P])
        scope.close()
        scope = ExitStack()
        z_out = alloc(scope, "z_out", [P, 2, TOK])
        f_x = alloc(scope, "f_x", [8, SEQ])
        f_a = alloc(scope, "f_a", [8, SEQ])
        inner = ExitStack()
        f_s = alloc(inner, "f_s", [8, 2, SEQ])
        inner.close()
        f_parts = alloc(scope, "f_parts", [8, 2, SEQ], F32R)
        scope.close()
        scope = ExitStack()
        s_keep = alloc(scope, "s_keep", [P, 7 * SEQ])
        s_u = alloc(scope, "s_u", [P, SEQ])
        s_v = alloc(scope, "s_v", [P, SEQ])
        s_w = alloc(scope, "s_w", [P, 2, P])
        s_b = alloc(scope, "s_b", [P, P])
        s_ctr = alloc(scope, "s_ctr", [P, 16, DH])
        s_sq = alloc(scope, "s_sq", [P, 16, DH])
        s_stat = alloc(scope, "s_stat", [P, 4, 16])
        s_y = alloc(scope, "s_y", [P, SEQ])
        scope.close()
        scope = ExitStack()
        a_q = alloc(scope, "a_q", [P, SEQ])
        a_k = alloc(scope, "a_k", [P, SEQ])
        a_vt = alloc(scope, "a_vt", [P, SEQ])
        a_c = alloc(scope, "a_c", [2, 2, SEQ], F32R)
        a_v = alloc(scope, "a_v", [P, QB, P])
        a_s = alloc(scope, "a_s", [P, 3, SEQ])
        a_pt = alloc(scope, "a_pt", [P, QB, 4 * P])
        a_small = alloc(scope, "a_small", [P, 4, 3])
        scope.close()
        scope = ExitStack()
        f_y = alloc(scope, "f_y", [P, 2, SEQ])
        f_g = alloc(scope, "f_g", [P, SEQ])
        f_act = alloc(scope, "f_act", [P, SEQ])
        f_hi = alloc(scope, "f_hi", [P, 2, SEQ], F32R)
        f_lo = alloc(scope, "f_lo", [P, 2, SEQ], F32R)
        d_raw = alloc(scope, "d_raw", [P, 2, D])
        d_hi = alloc(scope, "d_hi", [P, 2, D], F32R)
        d_lo = alloc(scope, "d_lo", [P, 2, D], F32R)
        scope.close()
        scope = ExitStack()
        d_q = alloc(scope, "d_q", [P, TOK])
        d_k = alloc(scope, "d_k", [P, TOK])
        d_g = alloc(scope, "d_g", [P, TOK])
        d_v = alloc(scope, "d_v", [P, TOK // P, P])
        d_p0 = alloc(scope, "d_p0", [P, 3, TOK])
        d_p1 = alloc(scope, "d_p1", [P, 2, TOK])
        d_pt = alloc(scope, "d_pt", [P, TOK // P, 2 * P])
        d_vt = d_pt[:].rearrange("p k q -> p (k q)")[:, 0:TOK]
        d_o = alloc(scope, "d_o", [P, 2, 2 * P])
        d_small = alloc(scope, "d_small", [P, 3, 8])
        scope.close()
        scope = ExitStack()
        b_q = alloc(scope, "b_q", [P, 2, SEQ])
        b_k = alloc(scope, "b_k", [P, TOK])
        b_vt = alloc(scope, "b_vt", [P, TOK])
        b_v = alloc(scope, "b_v", [P, TOK // P, P])
        b_g = alloc(scope, "b_g", [P, 2, SEQ])
        b_s = alloc(scope, "b_s", [P, 3, 5 * P])
        b_pt = alloc(scope, "b_pt", [P, 5, 4 * P])
        b_y = alloc(scope, "b_y", [P, 2, P])
        b_small = alloc(scope, "b_small", [P, 6, 3])
        scope.close()
        scope = ExitStack()
        r_keep = alloc(scope, "r_keep", [P, 2 * TOK])
        r_cos = alloc(scope, "r_cos", [P, SEQ])
        r_sin = alloc(scope, "r_sin", [P, SEQ])
        r_rot = alloc(scope, "r_rot", [P, SEQ])
        scope.close()

        consts_in = sem("consts_in")
        rows_in = sem("rows_in")
        zeroed = sem("zeroed")
        rows_turned, vec_ready = sem("rows_turned"), sem("vec_ready")
        vec32_ready, cond_ready = sem("vec32_ready"), sem("cond_ready")
        tok_in, tok_turned, tok_kept = sem2("tok_in"), sem2("tok_turned"), sem2("tok_kept")
        lam_step = sem("lam_step")
        lam_exp = sem("lam_exp")
        mod_in, mod_summed, mod_kept = sem2("mod_in"), sem2("mod_summed"), sem2("mod_kept")
        modg_ready = sem("modg_ready")
        w_landed, w_high, w_split, w_used = sem2("w_landed"), sem2("w_high"), sem2("w_split"), sem2("w_used")
        acc_free, stored = sem2("acc_free"), sem2("stored")
        res_added = sem("res_added")
        n_squared, n_added = sem2("n_squared"), sem2("n_added")
        n_zeroed, n_summed, n_root, n_scaled = sem("n_zeroed"), sem("n_summed"), sem("n_root"), sem("n_scaled")
        n_times, n_gained = sem2("n_times"), sem2("n_gained")
        n_high, n_low = sem2("n_high"), sem2("n_low")
        out_turned, out_kept, out_stored = sem2("out_turned"), sem2("out_kept"), sem2("out_stored")
        f_biased, f_soft, f_scan, f_stored = sem("f_biased"), sem("f_soft"), sem("f_scan"), sem("f_stored")
        s_in, s_turned, s_stats, s_squared, s_std = sem("s_in"), sem("s_turned"), sem("s_stats"), sem("s_squared"), sem("s_std")
        s_wt_ready, s_mixed, s_gated, s_low = sem("s_wt_ready"), sem("s_mixed"), sem("s_gated"), sem("s_low")
        f_based, f_tapped, f_gate, f_mult = sem2("f_based"), sem2("f_tapped"), sem("f_gate"), sem("f_mult")
        f_high, f_low, f_down = sem("f_high"), sem("f_low"), sem("f_down")
        d_landed, d_high, d_split, d_used = sem2("d_landed"), sem2("d_high"), sem2("d_split"), sem("d_used")
        r_swapped, r_read, r_turned, r_roped = sem("r_swapped"), sem("r_read"), sem("r_turned"), sem("r_roped")
        masks_ready = sem("masks_ready")

        class Mixer:
            def __init__(self, name):
                self.loaded, self.biased = sem(name + "_loaded"), sem(name + "_biased")
                self.scored, self.maxed, self.exped, self.weighed = (
                    sem(name + "_scored"), sem(name + "_maxed"), sem(name + "_exped"), sem(name + "_weighed"))
                self.turned, self.pt_kept, self.mixed, self.kept = (
                    sem(name + "_turned"), sem(name + "_pt_kept"), sem(name + "_mixed"), sem(name + "_kept"))
                self.low = sem(name + "_low")

        fa, da, ba = Mixer("fa"), Mixer("da"), Mixer("ba")
        da_scored1, da_maxed1, da_exped1 = sem("da_scored1"), sem("da_maxed1"), sem("da_exped1")
        da_vloaded, da_gloaded, ba_gloaded = sem("da_vloaded"), sem("da_gloaded"), sem("ba_gloaded")
        da_sq, da_ssq, da_rms = sem("da_sq"), sem("da_ssq"), sem("da_rms")
        da_free = sem2("da_free")

        W0, A0, Z0 = {}, {}, {}
        w_n, a_n, z_n = [0, 0], [0, 0], [0, 0]
        for name, w_uses, a_uses, z_uses in (
            ("gelu", (4, 4), (4, 4), (4, 4)), ("plain", (6, 6), (6, 6), (6, 6)), ("forget", (1, 0), (1, 0), (0, 0)),
            ("w_out", (4, 4), (4, 4), (0, 0)),
            ("ffn", (2 * CHUNKS, 2 * CHUNKS), (6 * CHUNKS, 6 * CHUNKS), (0, 0)),
            ("a_qk", (8, 8), (8, 8), (8, 8)), ("a_v", (4, 4), (4, 4), (4, 4)), ("a_gate", (4, 4), (4, 4), (4, 4)), ("a_out", (4, 4), (4, 4), (0, 0)),
            ("b_q", (4, 4), (4, 4), (4, 4)), ("b_k", (1, 1), (1, 1), (1, 1)), ("b_v", (1, 1), (1, 1), (1, 1)), ("b_gate", (4, 4), (4, 4), (4, 4)),
            ("b_out", (4, 4), (4, 4), (0, 0)),
        ):
            W0[name], A0[name], Z0[name] = tuple(w_n), tuple(a_n), tuple(z_n)
            for s in range(2):
                w_n[s] += w_uses[s]
                a_n[s] += a_uses[s]
                z_n[s] += z_uses[s]
        R0 = {"a_qk": 0, "b_q": 16, "b_k": 24}
        NORMS = {name: n for n, name in enumerate(("mix", "ffn", "fin", "a_x", "a_ctx", "b_x", "b_ctx", "out"))}
        SPLITS = {name: n for n, name in enumerate(("mix", "ffn", "a_x", "a_ctx", "b_x", "b_ctx"))}

        LATENT_SEGS = [(CTX, BANK, 0), (CTX + BANK, BANK, BANK)]
        ALL_SEGS = [(0, BANK, 0), (BANK, BANK, BANK), (2 * BANK, TOK - 2 * BANK, 2 * BANK)]

        block = ctx.enter_context(nc.Block())

        def weight_tiles(sp, name, w, col0, tiles, tables=None):
            view = w.rearrange("(k p) n -> p k n", p=P)

            def tile_pair(i):
                for s in range(2):
                    sp.wait_ge(w_split[s], i + W0[name][s] + 1)
                    sp.dma_start(w_raw[:, s].rearrange("p (k n) -> p k n", k=KT),
                                 view[:, :, bass.ds((2 * i + s) * P + col0, P)]).then_inc(w_landed[s], 16)

            tile_pair(0)
            if tables:
                (free, count), *loads = tables
                for s in range(2):
                    sp.wait_ge(free[s], count)
                for dst, src in loads:
                    sp.dma_start(dst[:], src).then_inc(consts_in, 16)
            if tiles > 2:
                with sp.Fori(1, tiles // 2) as i:
                    tile_pair(i)

        @block.sync
        def _(sp):
            for dst, src in ((ident[:], const_ident), (swap[:], const_swap),
                             (maskrows[:, 0], const_causal), (maskrows[:, 1], const_before),
                             (lamrows[:, 0], a_lambda_q1_2.broadcast_to([P, DH])),
                             (lamrows[:, 1], a_lambda_k1_2.broadcast_to([P, DH])),
                             (lamrows[:, 2], a_lambda_q2_2.broadcast_to([P, DH])),
                             (lamrows[:, 3], a_lambda_k2_2.broadcast_to([P, DH])),
                             (sinks[:], b_sink_2.broadcast_to([P, 16])),
                             (fb[:], f_bias.rearrange("o h -> h o"))):
                sp.dma_start(dst, src).then_inc(consts_in, 16)
            for at, v in ((V_MIX, norm_mix_g), (V_FFN, norm_ffn_g), (V_G2, norm_g_2), (V_BMOD, b_mod_2),
                          (V_SUB, a_subln_g_2), (V_C, c_2)):
                n = v.shape[0] * v.shape[1] // P
                sp.dma_start(rows[at:at + n, :], v.rearrange("o (t p) -> (o t) p", p=P)).then_inc(rows_in, 16)
            for at, v in ((V_FIN, norm_final_g), (V_FG2, final_g_2), (V_C + KT, c_ctx_2)):
                sp.dma_start(rows[at:at + KT, :], v.rearrange("(t p) -> t p", p=P)).then_inc(rows_in, 16)
            sp.dma_start(rows[V_LNG:V_LNG + 4, :],
                         sg_ln_g[0].rearrange("(j e) d -> j (e d)", e=2)).then_inc(rows_in, 16)
            for tap, (slot, at) in enumerate(((0, 0), (0, 44), (1, 0))):
                sp.dma_start(convrows[at:at + 2 * FT, slot, :],
                             w_conv[0, tap].rearrange("(t p) -> t p", p=P)).then_inc(rows_in, 16)
            sp.dma_start(convrows[44:88, 1, :], b_conv[0].rearrange("(t p) -> t p", p=P)).then_inc(rows_in, 16)
            for s in range(2):
                sp.dma_start(tokrows[:, s], ctx_2[0, s * P:(s + 1) * P, :]).then_inc(tok_in[s], 16)
            with sp.Fori(0, QB // 2) as i:
                for s in range(2):
                    sp.wait_ge(tok_turned[s], i + 1)
                    sp.dma_start(tokrows[:, s], x[0, bass.ds((2 * i + s) * P, P), :]).then_inc(tok_in[s], 16)
            for layer in range(2):
                view = w_mod_2[layer].rearrange("(k p) n -> p k n", p=P)
                with sp.Fori(0, 6) as i:
                    for s in range(2):
                        sp.wait_ge(mod_summed[s], i + 6 * layer + 1)
                        sp.dma_start(w_mod_sb[:, s], view[:, :, bass.ds((2 * i + s) * 2 * P, 2 * P)]).then_inc(mod_in[s], 16)
            weight_tiles(sp, "gelu", w_in[0], 0, 8)
            weight_tiles(sp, "plain", w_in[0], 8 * P, 12)
            sp.wait_ge(w_split[0], W0["forget"][0] + 1)
            with nc.allow_non_contiguous_dma(reason="eight columns"):
                sp.dma_start(w_raw[:, 0].rearrange("p (k n) -> p k n", k=KT)[:, :, 0:8],
                             w_in[0].rearrange("(k p) n -> p k n", p=P)[:, :, 20 * P:20 * P + 8]).then_inc(w_landed[0], 16)
            for s in range(2):
                sp.wait_ge(stored[s], 16 * (Z0["plain"][s] + 6) + 16)
            with sp.Fori(0, 4) as j:
                sp.wait_ge(s_low, j + 1)
                sp.dma_start(s_v[:], z1[bass.ds(j * P + 4 * P, P), :]).then_inc(s_in, 16)
                sp.dma_start(s_u[:], z1[bass.ds(j * P, P), :]).then_inc(s_in, 16)
                sp.dma_start(s_w[:], sg_w[0, bass.ds(2 * j, 2)].rearrange("h t s -> t h s")).then_inc(s_in, 16)
                for e in range(2):
                    sp.dma_start(s_b[e * DH:(e + 1) * DH, :],
                                 sg_b[0, bass.ds(2 * j + e, 1), :].broadcast_to([DH, P])).then_inc(s_in, 16)
            sp.wait_ge(f_stored, 32)
            sp.wait_ge(s_low, 4 + 1)
            with sp.Fori(0, 4) as j:
                sp.wait_ge(fa.scored, 16 * j + 1)
                sp.dma_start(a_q[:], z1[bass.ds(j * P + 8 * P, P), :]).then_inc(fa.loaded, 16)
                sp.dma_start(a_k[:], z1[bass.ds(j * P + 12 * P, P), :]).then_inc(fa.loaded, 16)
                for part in range(2):
                    sp.dma_start(a_c[part:part + 1].bitcast(F32), forget_rows[part:part + 1, bass.ds(2 * j, 2), :]).then_inc(fa.loaded, 16)
                sp.dma_start(a_vt[:], z1[bass.ds(j * P + 16 * P, P), :]).then_inc(fa.loaded, 16)
            weight_tiles(sp, "w_out", w_out[0], 0, 8)
            up = w_up[0].rearrange("(k p) n -> p k n", p=P)

            def up_tiles(chunk, e):
                for s in range(2):
                    sp.wait_ge(w_split[s], 2 * chunk + (W0["ffn"][s] + e) + 1)
                    sp.dma_start(w_raw[:, s].rearrange("p (k n) -> p k n", k=KT),
                                 up[:, :, bass.ds((2 * chunk + (s * FT + e)) * P, P)]).then_inc(w_landed[s], 16)

            def down_rows(chunk):
                for s in range(2):
                    sp.wait_ge(d_split[s], chunk + 1)
                    sp.dma_start(d_raw[:, s], w_down[0, bass.ds((2 * chunk + s) * P, P), :]).then_inc(d_landed[s], 16)

            up_tiles(0, 0)
            for s in range(2):
                sp.wait_ge(n_low[s], 4 * (SPLITS["ffn"] + 1) + 1)
            with sp.Fori(0, CHUNKS - 1) as c:
                up_tiles(c, 1)
                down_rows(c)
                up_tiles(c + 1, 0)
            up_tiles(CHUNKS - 1, 1)
            down_rows(CHUNKS - 1)
            weight_tiles(sp, "a_qk", a_w_in_2[0], 0, 16, ((n_low, 4 * (SPLITS["a_ctx"] + 1) + 1), (r_cos, const_cos), (r_sin, const_sin)))
            weight_tiles(sp, "a_v", a_w_in_2[0], 16 * P, 8)
            weight_tiles(sp, "a_gate", a_w_in_2[0], 24 * P, 8)
            for s in range(2):
                sp.wait_ge(stored[s], 16 * (Z0["a_gate"][s] + 4) + 16)
            with sp.Fori(0, 8) as h:
                sp.wait_ge(da_scored1, 10 * h + 1)
                sp.dma_start(d_q[:], za[bass.ds(h * P, P), :]).then_inc(da.loaded, 16)
                sp.dma_start(d_k[:], za[bass.ds(h * P + 8 * P, P), :]).then_inc(da.loaded, 16)
                sp.wait_ge(da.mixed, 5 * h + 1)
                sp.dma_start(d_vt, za[bass.ds(h * P + 16 * P, P), :]).then_inc(da_vloaded, 16)
                sp.wait_ge(da.low, 5 * h + 1)
                sp.dma_start(d_g[:], za[bass.ds(h * P + 24 * P, P), :]).then_inc(da_gloaded, 16)
            weight_tiles(sp, "a_out", w_o_2[0], 0, 8)
            weight_tiles(sp, "b_q", b_w_in_2[0], 0, 8, ((n_low, 4 * (SPLITS["b_ctx"] + 1) + 1), (r_cos, const_cos), (r_sin, const_sin)))
            weight_tiles(sp, "b_k", b_w_in_2[0], 8 * P, 2)
            weight_tiles(sp, "b_v", b_w_in_2[0], 10 * P, 2)
            weight_tiles(sp, "b_gate", b_w_in_2[0], 12 * P, 8)
            for s in range(2):
                sp.wait_ge(stored[s], 16 * (Z0["b_gate"][s] + 4) + 16)
            with sp.Fori(0, 4) as h:
                sp.wait_ge(ba.scored, 32 * h + 1)
                sp.dma_start(b_q[:], zb[bass.ds(h * 2 * P, 2 * P), X_COLS].rearrange("(t p) n -> p t n", p=P)).then_inc(ba.loaded, 16)
                for e in range(2):
                    sp.dma_start(b_k[e * DH:(e + 1) * DH, :], zb[bass.ds(h * DH + 8 * P, DH), :]).then_inc(ba.loaded, 16)
                    sp.dma_start(b_vt[e * DH:(e + 1) * DH, :], zb[bass.ds(h * DH + 10 * P, DH), :]).then_inc(ba.loaded, 16)
                sp.wait_ge(ba.low, 8 * h + 1)
                sp.dma_start(b_g[:], zb[bass.ds(h * 2 * P + 12 * P, 2 * P), X_COLS].rearrange("(t p) n -> p t n", p=P)).then_inc(ba_gloaded, 16)
            weight_tiles(sp, "b_out", w_o_2[1], 0, 8)
            rows_of_out = out[0].rearrange("(t p) n -> p t n", p=P)
            with sp.Fori(0, KT // 2) as i:
                for s in range(2):
                    sp.wait_ge(out_kept[s], i + 1 + 1)
                    sp.dma_start(rows_of_out[:, :, bass.ds((2 * i + s) * P, P)], tok_out[:, s]).then_inc(out_stored[s], 16)
            for s in range(2):
                sp.wait_ge(out_stored[s], 16 * (KT // 2) + 16)

        def split(pool, base, use, s):
            pool.wait_ge(w_landed[s], 16 * use + 16 * (base[s] + 1))
            pool.wait_ge(w_used[s], use + base[s] + 1)
            pool.tensor_tensor(wh[:, s], w_raw[:, s], zero[:].broadcast_to([P, KT * P]), ALU.add).then_inc(w_high[s], 1)
            pool.wait_ge(w_high[s], use + (base[s] + 1))
            pool.tensor_tensor(wl[:, s], w_raw[:, s], wh[:, s].bitcast(F32), ALU.subtract).then_inc(w_split[s], 1)

        def split_tiles(pool, name, tiles):
            with pool.Fori(0, tiles // 2) as i:
                for s in range(2):
                    split(pool, W0[name], i, s)

        def norm_rests(pool, name, cols):
            n = 4 * SPLITS[name]
            with pool.Fori(0, KT // 2) as i:
                for s in range(2):
                    pool.wait_ge(n_high[s], i + (n + 1))
                    pool.tensor_tensor(hl[:, bass.ds(2 * i + s, 1), cols], n_h[:, s:s + 1, 0:cols.stop - cols.start],
                                       hh[:, bass.ds(2 * i + s, 1), cols].bitcast(F32), ALU.subtract).then_inc(n_low[s], 1)

        @block.gpsimd
        def _(pool):
            for opened in (*w_split, *w_used, *acc_free, *mod_summed, *mod_kept, *n_added, *n_low, *n_gained, *out_turned, *out_kept,
                           s_low, *d_split, d_used, r_read, r_roped, fa.kept, fa.mixed, fa.scored, fa.pt_kept, da.low, da.mixed, da.maxed,
                           da_maxed1, da_scored1, da_ssq, *da_free, ba.low, ba.mixed, ba.pt_kept, ba.scored):
                pool.sem_inc(opened, 1)
            for opened in (*stored, *out_stored):
                pool.sem_inc(opened, 16)
            pool.memset(ones[:], 1.0).then_inc(zeroed, 1)
            pool.memset(zero[:], 0.0).then_inc(zeroed, 1)
            pool.memset(ones_r[:].bitcast(F32), 1.0).then_inc(zeroed, 1)
            pool.memset(one[:], 1.0).then_inc(zeroed, 1)
            pool.memset(eps_d[:], D * EPS).then_inc(zeroed, 1)
            pool.memset(eps_1[:], EPS).then_inc(zeroed, 1)
            pool.memset(eps_sub[:], SUB_EPS).then_inc(zeroed, 1)
            pool.memset(s_wt[:], 0.0).then_inc(zeroed, 1)
            pool.wait_ge(zeroed, 2)
            norm_rests(pool, "mix", X_COLS)
            split_tiles(pool, "gelu", 8)
            split_tiles(pool, "plain", 12)
            split(pool, W0["forget"], 0, 0)
            with pool.Fori(0, 4) as j:
                pool.wait_ge(s_gated, 4 * j + 4)
                pool.tensor_tensor(hl[:, bass.ds(j, 1), X_COLS], s_y[:].unsqueeze(1),
                                   hh[:, bass.ds(j, 1), X_COLS].bitcast(F32), ALU.subtract).then_inc(s_low, 1)
            split_tiles(pool, "w_out", 8)
            norm_rests(pool, "ffn", X_COLS)

            def split_up(chunk, e):
                for s in range(2):
                    split(pool, W0["ffn"], 2 * chunk + e, s)

            def split_down(chunk):
                for s in range(2):
                    pool.wait_ge(d_landed[s], 16 * chunk + 16)
                    pool.wait_ge(d_used, chunk + 1)
                    pool.tensor_tensor(d_hi[:, s], d_raw[:, s], zero[:].broadcast_to([P, D]), ALU.add).then_inc(d_high[s], 1)
                    pool.wait_ge(d_high[s], chunk + 1)
                    pool.tensor_tensor(d_lo[:, s], d_raw[:, s], d_hi[:, s].bitcast(F32), ALU.subtract).then_inc(d_split[s], 1)

            def act_rest(chunk, e):
                pool.wait_ge(f_high, 2 * chunk + (e + 1))
                pool.tensor_tensor(f_lo[:, e], f_act[:], f_hi[:, e].bitcast(F32), ALU.subtract).then_inc(f_low, 1)

            split_up(0, 0)
            with pool.Fori(0, CHUNKS - 1) as c:
                split_up(c, 1)
                act_rest(c, 0)
                split_down(c)
                split_up(c + 1, 0)
                act_rest(c, 1)
            split_up(CHUNKS - 1, 1)
            act_rest(CHUNKS - 1, 0)
            split_down(CHUNKS - 1)
            act_rest(CHUNKS - 1, 1)
            norm_rests(pool, "a_x", X_COLS)
            norm_rests(pool, "a_ctx", slice(0, CTX))
            split_tiles(pool, "a_qk", 16)
            split_tiles(pool, "a_v", 8)
            split_tiles(pool, "a_gate", 8)
            with pool.Fori(0, 8) as h:
                for g in range(5):
                    pool.wait_ge(da.kept, 15 * h + (3 * g + 3))
                    pool.tensor_tensor(hl[:, bass.ds(h, 1), g * 2 * P:(g + 1) * 2 * P], d_o[:, 0:1, :],
                                       hh[:, bass.ds(h, 1), g * 2 * P:(g + 1) * 2 * P].bitcast(F32),
                                       ALU.subtract).then_inc(da.low, 1)
            split_tiles(pool, "a_out", 8)
            norm_rests(pool, "b_x", X_COLS)
            norm_rests(pool, "b_ctx", slice(0, CTX))
            split_tiles(pool, "b_q", 8)
            split_tiles(pool, "b_k", 2)
            split_tiles(pool, "b_v", 2)
            split_tiles(pool, "b_gate", 8)
            with pool.Fori(0, 4) as h:
                for i in range(QB):
                    cols = slice(CTX + i * P, CTX + (i + 1) * P)
                    pool.wait_ge(ba.kept, 24 * h + (3 * i + 3))
                    pool.tensor_tensor(hl[:, bass.ds(2 * h, 2), cols], b_y[:], hh[:, bass.ds(2 * h, 2), cols].bitcast(F32),
                                       ALU.subtract).then_inc(ba.low, 1)
            split_tiles(pool, "b_out", 8)

        def product(pe, out_, w_hi, w_lo, x_hi, x_lo, start, stop):
            pe.matmul(out_, w_hi, x_hi, start=start, stop=False)
            pe.matmul(out_, w_hi, x_lo, start=False, stop=False)
            return pe.matmul(out_, w_lo, x_hi, start=False, stop=stop)

        def project_tile(pe, name, i, s, segs):
            pe.wait_ge(w_split[s], i + (W0[name][s] + 1) + 1)
            pe.wait_ge(acc_free[s], i + A0[name][s] + 1)
            for k in range(KT):
                wk = slice(k * P, (k + 1) * P)
                for c0, w, p0 in segs:
                    last = product(pe, acc[s][:, p0:p0 + w], wh[:, s, wk], wl[:, s, wk],
                                   hh[:, k, c0:c0 + w], hl[:, k, c0:c0 + w], k == 0, k == KT - 1)
            last.then_inc(w_used[s], 1)

        def project(pe, name, tiles, segs):
            with pe.Fori(0, tiles // 2) as i:
                for s in range(2):
                    project_tile(pe, name, i, s, segs)

        def project_rotated(pe, name, tiles, segs):
            def swap_tile(i, s):
                pe.wait_ge(acc_free[s], i + A0[name][s] + 1 + 1)
                pe.wait_ge(r_read, 2 * i + (R0[name] + s) + 1)
                first = segs[-1][2] + segs[-1][1] - SEQ
                for c in range(0, SEQ, BANK):
                    last = pe.matmul(ps[:, 6 * BANK + c:7 * BANK + c], swap[:], z_out[:, s, first + c:first + c + BANK], start=True, stop=True)
                last.then_inc(r_swapped, 1)

            project_tile(pe, name, 0, 0, segs)
            project_tile(pe, name, 0, 1, segs)
            swap_tile(0, 0)
            if tiles > 2:
                with pe.Fori(1, tiles // 2) as i:
                    project_tile(pe, name, i, 0, segs)
                    swap_tile(i - 1, 1)
                    project_tile(pe, name, i, 1, segs)
                    swap_tile(i, 0)
            swap_tile(tiles // 2 - 1, 1)

        def wait_split_norm(pe, *names):
            for name in names:
                for s in range(2):
                    pe.wait_ge(n_low[s], 4 * (SPLITS[name] + 1) + 1)

        def norm_sum(pe, name, width):
            n = NORMS[name]
            for s in range(2):
                pe.wait_ge(n_added[s], 4 * (n + 1) + 1)
            for c in range(0, width, BANK):
                w = min(BANK, width - c)
                last = pe.matmul(ps[:, 6 * BANK + c:6 * BANK + c + w], ones[:], n_sum[:, c:c + w], start=True, stop=True)
            last.then_inc(n_summed, 1)

        @block.tensor
        def _(pe):
            pe.wait_ge(consts_in, 16 * 10)

            def turn_tokens(s, use):
                pe.wait_ge(tok_in[s], 16 * use + 16)
                pe.wait_ge(tok_kept[s], use)
                for k in range(KT):
                    last = pe.transpose(acc[s][:, k * P:(k + 1) * P], tokrows[:, s, k * P:(k + 1) * P], ident[:])
                last.then_inc(tok_turned[s], 1)

            for s in range(2):
                turn_tokens(s, 0)
            with pe.Fori(0, QB // 2) as i:
                for s in range(2):
                    turn_tokens(s, i + 1)
            pe.wait_ge(rows_in, 16 * 14)
            pe.transpose(bank(6)[:, 0:V_END], rows[0:V_END, :], ident[0:V_END, 0:V_END])
            for n in range(2):
                last = pe.transpose(bank(7)[:, n * 88:(n + 1) * 88], convrows[:, n, :], ident[0:88, 0:88])
            last.then_inc(rows_turned, 1)
            pe.wait_ge(cond_ready, 2)
            for layer in range(2):
                with pe.Fori(0, 6) as i:
                    for s in range(2):
                        pe.wait_ge(mod_in[s], 16 * i + 16 * (6 * layer + 1))
                        pe.wait_ge(mod_kept[s], 2 * i + 12 * layer + 1)
                        for n in range(2):
                            for k in range(KT):
                                last = pe.matmul(acc[s][:, 2 * n:2 * n + 2], w_mod_sb[:, s, k, n * P:(n + 1) * P],
                                                 cond[:, k, :], start=(k == 0), stop=(k == KT - 1))
                        last.then_inc(mod_summed[s], 1)
            norm_sum(pe, "mix", SEQ)
            wait_split_norm(pe, "mix")
            project(pe, "gelu", 8, LATENT_SEGS)
            project(pe, "plain", 12, LATENT_SEGS)
            project_tile(pe, "forget", 0, 0, LATENT_SEGS)
            for s in range(2):
                pe.wait_ge(acc_free[s], A0["w_out"][s] + 1)
            with pe.Fori(0, 4) as j:
                pe.wait_ge(s_in, 80 * j + 80)
                for n in range(QB):
                    pe.transpose(ps[:, n * P:(n + 1) * P], s_v[:, n * P:(n + 1) * P], ident[:])
                for e in range(2):
                    last = pe.transpose(bank(2)[:, e * P:(e + 1) * P], s_w[:, e], ident[:])
                last.then_inc(s_turned, 1)
                pe.wait_ge(s_wt_ready, 2 * j + 2)
                pe.wait_ge(s_stats, 6 * j + 6)
                for n in range(QB):
                    last = pe.matmul(ps[:, 4 * BANK + n * 2 * P:4 * BANK + (n + 1) * 2 * P],
                                     s_ctr[:].rearrange("p (n e) d -> p n (e d)", e=2)[:, n],
                                     s_wt[:].rearrange("p e t -> p (e t)"), start=True, stop=True)
                last.then_inc(s_mixed, 1)
            pe.wait_ge(masks_ready, 3)
            pe.wait_ge(s_low, 4 + 1)
            with pe.Fori(0, 4) as j:
                pe.wait_ge(fa.loaded, 80 * j + 80)

                def fa_scores(u):
                    a, i = divmod(u, QB)
                    h, at, width = slice(a * DH, (a + 1) * DH), 2 * (u % 2) * BANK, (i + 1) * P
                    if u >= 2:
                        pe.wait_ge(fa.maxed, 16 * j + (u - 1))
                    for c in range(0, width, BANK):
                        w = min(BANK, width - c)
                        got = ps[:, at + c:at + c + w]
                        pe.matmul(got, a_q[h, i * P:(i + 1) * P], a_k[h, c:c + w], start=True, stop=False)
                        last = pe.matmul(got, ones_r[:], a_c[:, a, c:c + w], start=False, stop=(c + w < width))
                    last = pe.matmul(ps[:, at + i * P:at + width], masks[:, 0], masks[:, 1], start=False, stop=True)
                    last.then_inc(fa.scored, 1)

                for u in range(LEAD):
                    fa_scores(u)
                pe.wait_ge(fa.pt_kept, 17 * j + 1)
                for n in range(QB):
                    last = pe.transpose(ps[:, 4 * BANK + n * P:4 * BANK + (n + 1) * P], a_vt[:, n * P:(n + 1) * P], ident[:])
                last.then_inc(fa.turned, 1)
                for u in range(2 * QB):
                    a, i = divmod(u, QB)
                    pe.wait_ge(fa.weighed, 32 * j + (2 * u + 2))
                    pe.wait_ge(fa.pt_kept, 17 * j + (u + 1) + 1)
                    for kt in range(i + 1):
                        last = pe.transpose(ps[:, 4 * BANK + kt * P:4 * BANK + (kt + 1) * P],
                                            a_s[:, u % 3, kt * P:(kt + 1) * P], ident[:])
                    last.then_inc(fa.turned, 1)
                    if u + LEAD < 2 * QB:
                        fa_scores(u + LEAD)
                    if u % 4 == 3:
                        g, first = u // 4, 4 * (i // 4)
                        pe.wait_ge(fa.pt_kept, 17 * j + (u + 2) + 1)
                        pe.wait_ge(fa.kept, 8 * j + 2 * g + 1)
                        for kt in range(i + 1):
                            c = max(0, kt - first) * P
                            last = pe.matmul(bank(6)[:, c:], a_v[:, kt, :], a_pt[:, kt, c:], start=(kt == 0), stop=(kt == i))
                        last.then_inc(fa.mixed, 1)
            pe.wait_ge(fa.kept, 32 + 1)
            project(pe, "w_out", 8, LATENT_SEGS)
            norm_sum(pe, "ffn", SEQ)
            wait_split_norm(pe, "ffn")

            def ffn_up(chunk, e, acc_use):
                for s in range(2):
                    pe.wait_ge(w_split[s], 2 * chunk + (W0["ffn"][s] + e + 1) + 1)
                    pe.wait_ge(acc_free[s], acc_use + A0["ffn"][s] + 1)
                    for k in range(KT):
                        wk = slice(k * P, (k + 1) * P)
                        for c0, w, p0 in LATENT_SEGS:
                            last = product(pe, acc[s][:, p0:p0 + w], wh[:, s, wk], wl[:, s, wk],
                                           hh[:, k, c0:c0 + w], hl[:, k, c0:c0 + w], k == 0, k == KT - 1)
                    last.then_inc(w_used[s], 1)

            def ffn_down(chunk, acc_use):
                pe.wait_ge(f_low, 2 * chunk + 2)
                for s in range(2):
                    pe.wait_ge(d_split[s], chunk + 1 + 1)
                for m in range(KT):
                    s, wm = m % 2, slice(m * P, (m + 1) * P)
                    pe.wait_ge(acc_free[s], acc_use + (A0["ffn"][s] + m // 2) + 1)
                    for e in range(2):
                        for c in range(0, SEQ, BANK):
                            last = product(pe, acc[s][:, c:c + BANK], d_hi[:, e, wm], d_lo[:, e, wm],
                                           f_hi[:, e, c:c + BANK], f_lo[:, e, c:c + BANK], e == 0, e == 1)
                    last.then_inc(f_down if m < KT - 1 else d_used, 1)

            ffn_up(0, 0, 0)
            ffn_up(0, 1, 1)
            with pe.Fori(1, CHUNKS) as c:
                ffn_up(c, 0, 6 * c - 4)
                ffn_down(c - 1, 6 * c - 3)
                ffn_up(c, 1, 6 * c + 1)
            ffn_down(CHUNKS - 1, 6 * CHUNKS - 4)
            norm_sum(pe, "fin", SEQ)
            norm_sum(pe, "a_x", SEQ)
            norm_sum(pe, "a_ctx", CTX)
            wait_split_norm(pe, "a_x", "a_ctx")
            project_rotated(pe, "a_qk", 16, ALL_SEGS)
            project(pe, "a_v", 8, ALL_SEGS)
            project(pe, "a_gate", 8, ALL_SEGS)
            for s in range(2):
                pe.wait_ge(acc_free[s], A0["a_out"][s] + 1)
            with pe.Fori(0, 8) as h:
                def da_take(*key):
                    b, n = DA_PLAN[key]
                    pe.wait_ge(da_free[b], DA_TURNS[b] * h + n + 1)
                    return b

                def da_turn(src, blocks, *key):
                    b = da_take(*key)
                    for n, kt in enumerate(blocks):
                        last = pe.transpose(bank(6 + b)[:, n * P:(n + 1) * P], src(kt), ident[:])
                    last.then_inc(da.turned, 1)

                def da_scores(u, m):
                    done, read = ((da.scored, da.maxed), (da_scored1, da_maxed1))[m]
                    pe.wait_ge(read, 10 * h + u + 1)
                    r, width = slice(m * DH, (m + 1) * DH), da_tiles(u) * P
                    for c in range(0, width, BANK):
                        w = min(BANK, width - c)
                        last = pe.matmul(acc[m][:, c:c + w], d_q[r, u * P:(u + 1) * P], d_k[r, c:c + w], start=True, stop=True)
                    last.then_inc(done, 1)

                def da_sum(g):
                    b = da_take("sum", g)
                    pe.wait_ge(da_sq, 5 * h + (g + 1))
                    pe.matmul(bank(6 + b)[:, 0:2 * P], ones[:], d_o[:, 1, :], start=True, stop=True).then_inc(da_ssq, 1)

                pe.wait_ge(da.loaded, 32 * h + 32)
                for u in range(LEAD):
                    for m in range(2):
                        da_scores(u, m)
                pe.wait_ge(da_vloaded, 16 * h + 16)
                for n, blocks in enumerate(batches(TOK // P)):
                    da_turn(lambda kt: d_vt[:, kt * P:(kt + 1) * P], blocks, "v", n)
                for u in range(10):
                    nk = da_tiles(u)
                    ahead = [m for m in range(2) if u + LEAD < 10]
                    pe.wait_ge(da.weighed, 40 * h + (4 * u + 4))
                    for n, blocks in enumerate(batches(nk)):
                        da_turn(lambda kt: d_p0[:, u % 3, kt * P:(kt + 1) * P], blocks, "p", u, n)
                        if n and ahead:
                            da_scores(u + LEAD, ahead.pop(0))
                    for m in ahead:
                        da_scores(u + LEAD, m)
                    if u >= 2 and u % 2 == 0:
                        da_sum(u // 2 - 1)
                    if u % 2 == 1:
                        b = da_take("out", u // 2)
                        last_b, last_n = DA_PLAN["p", u, len(batches(nk)) - 1]
                        pe.wait_ge(da_free[last_b], DA_TURNS[last_b] * h + (last_n + 1) + 1)
                        for kt in range(nk):
                            last = pe.matmul(bank(6 + b)[:, 0:2 * P], d_v[:, kt, :], d_pt[:, kt, :], start=(kt == 0), stop=(kt == nk - 1))
                        last.then_inc(da.mixed, 1)
                da_sum(4)
            pe.wait_ge(da.low, 40 + 1)
            project(pe, "a_out", 8, ALL_SEGS)
            norm_sum(pe, "b_x", SEQ)
            norm_sum(pe, "b_ctx", CTX)
            wait_split_norm(pe, "b_x", "b_ctx")
            project_rotated(pe, "b_q", 8, LATENT_SEGS)
            project_rotated(pe, "b_k", 2, ALL_SEGS)
            project(pe, "b_v", 2, ALL_SEGS)
            project(pe, "b_gate", 8, LATENT_SEGS)
            for s in range(2):
                pe.wait_ge(acc_free[s], A0["b_out"][s] + 1)
            with pe.Fori(0, 4) as h:
                def ba_scores(u):
                    i, a = divmod(u, 4)
                    r, t, at = slice((a % 2) * DH, (a % 2 + 1) * DH), a // 2, 2 * (u % 2) * BANK
                    if u >= 2:
                        pe.wait_ge(ba.maxed, 32 * h + (u - 1))
                    for n, kt in enumerate(window_tiles(i)):
                        if kt == 1:
                            continue
                        w, side = CTX if kt == 0 else P, kt - (2 + i) if kt else 0
                        got = ps[:, at + n * P:at + n * P + w]
                        last = pe.matmul(got, b_q[r, t, i * P:(i + 1) * P], b_k[r, kt * P:kt * P + w], start=True, stop=(side == 0))
                        if side:
                            last = pe.matmul(got, masks[:, 0], masks[:, 2 if side < 0 else 1], start=False, stop=True)
                    last.then_inc(ba.scored, 1)

                pe.wait_ge(ba.loaded, 80 * h + 80)
                for u in range(LEAD):
                    ba_scores(u)
                for n, blocks in enumerate((range(8), range(8, 10))):
                    pe.wait_ge(ba.pt_kept, 34 * h + n + 1)
                    for m, kt in enumerate(blocks):
                        last = pe.transpose(ps[:, 4 * BANK + m * P:4 * BANK + (m + 1) * P], b_vt[:, kt * P:(kt + 1) * P], ident[:])
                    last.then_inc(ba.turned, 1)
                for u in range(4 * QB):
                    i, a = divmod(u, 4)
                    tiles = window_tiles(i)
                    pe.wait_ge(ba.weighed, 96 * h + (3 * u + 3))
                    pe.wait_ge(ba.pt_kept, 34 * h + (u + 2) + 1)
                    for n in range(len(tiles)):
                        last = pe.transpose(ps[:, 4 * BANK + n * P:4 * BANK + (n + 1) * P], b_s[:, u % 3, n * P:(n + 1) * P], ident[:])
                    last.then_inc(ba.turned, 1)
                    if u + LEAD < 4 * QB:
                        ba_scores(u + LEAD)
                    if a == 3:
                        pe.wait_ge(ba.pt_kept, 34 * h + (u + 3) + 1)
                        pe.wait_ge(ba.low, 8 * h + i + 1)
                        for n, kt in enumerate(tiles):
                            last = pe.matmul(bank(6), b_v[:, kt, :], b_pt[:, n, :], start=(n == 0), stop=(n == len(tiles) - 1))
                        last.then_inc(ba.mixed, 1)
            pe.wait_ge(ba.low, 32 + 1)
            project(pe, "b_out", 8, LATENT_SEGS)
            norm_sum(pe, "out", SEQ)
            with pe.Fori(0, KT // 2) as i:
                for s in range(2):
                    pe.wait_ge(n_gained[s], i + 4 * NORMS["out"] + 1 + 1)
                    pe.wait_ge(out_kept[s], i + 1)
                    for t in range(QB):
                        last = pe.transpose(acc[s][:, t * P:(t + 1) * P], n_h[:, s, t * P:(t + 1) * P], ident[:])
                    last.then_inc(out_turned[s], 1)

        def norm_root(act, name, cols):
            n, w = NORMS[name], cols.stop - cols.start
            with act.Fori(0, KT // 2) as i:
                for s in range(2):
                    act.wait_ge(n_added[s], i + 4 * n + 1)
                    act.activation(n_sq[:, s:s + 1, 0:w], res[:, bass.ds(2 * i + s, 1), cols], ACT.Square).then_inc(n_squared[s], 1)
            act.wait_ge(n_summed, n + 1)
            act.activation(n_rs[:, 0:w], ps[:, 6 * BANK:6 * BANK + w], ACT.Sqrt, bias=eps_d[:]).then_inc(n_root, 1)

        def norm_gain(act, name, cols, gain, shift):
            n, w = NORMS[name], cols.stop - cols.start
            with act.Fori(0, KT // 2) as i:
                for s in range(2):
                    k = 2 * i + s
                    act.wait_ge(n_times[s], i + (4 * n + 1))
                    to = n_h[:, s:s + 1, 0:w]
                    if name in SPLITS:
                        act.wait_ge(n_low[s], i + 4 * SPLITS[name] + 1)
                    elif name == "out":
                        act.wait_ge(out_turned[s], i + 1)
                    else:
                        to = res[:, bass.ds(k, 1), cols]
                    act.activation(to, n_t[:, s:s + 1, 0:w], ACT.Identity, bias=shift(k), scale=gain(k)).then_inc(n_gained[s], 1)

        def keep(act, name, rows, row0, tiles, cols, func):
            w = cols.stop - cols.start
            with act.Fori(0, tiles // 2) as i:
                for s in range(2):
                    act.wait_ge(w_used[s], i + (W0[name][s] + 1) + 1)
                    act.wait_ge(stored[s], 16 * i + 16 * Z0[name][s] + 16)
                    act.activation(z_out[:, s, 0:w], acc[s][:, 0:w], func).then_inc(acc_free[s], 1)
                    act.wait_ge(acc_free[s], i + (A0[name][s] + 1) + 1)
                    act.dma_start(rows[bass.ds((2 * i + s) * P + row0, P), cols], z_out[:, s, 0:w]).then_inc(stored[s], 16)

        def keep_rotated(act, name, rows, row0, tiles, cols):
            w = cols.stop - cols.start

            def copy(i, s):
                act.wait_ge(w_used[s], i + (W0[name][s] + 1) + 1)
                act.wait_ge(stored[s], 16 * i + 16 * Z0[name][s] + 16)
                act.activation(z_out[:, s, 0:w], acc[s][:, 0:w], ACT.Copy).then_inc(acc_free[s], 1)

            def store(i, s):
                act.wait_ge(r_roped, 2 * i + (R0[name] + s + 1) + 1)
                act.dma_start(rows[bass.ds((2 * i + s) * P + row0, P), cols], z_out[:, s, 0:w]).then_inc(stored[s], 16)

            copy(0, 0)
            copy(0, 1)
            store(0, 0)
            if tiles > 2:
                with act.Fori(1, tiles // 2) as i:
                    copy(i, 0)
                    store(i - 1, 1)
                    copy(i, 1)
                    store(i, 0)
            store(tiles // 2 - 1, 1)

        def vec_gain(at):
            return lambda k: vec32[:, bass.ds(k + at, 1)]

        def no_shift(k):
            return zero[:]

        def mod_gain(layer, v):
            return lambda k: modg[:, layer, v, bass.ds(k, 1)]

        def mod_shift(layer, v):
            return lambda k: mod[:, bass.ds(k + 24 * layer, 1), v]

        @block.scalar
        def _(act):
            act.wait_ge(zeroed, 8)
            act.wait_ge(vec_ready, 2)
            for v in range(2):
                act.activation(cond[:, :, v], vec[:, V_C + v * KT:V_C + (v + 1) * KT], ACT.Silu).then_inc(cond_ready, 1)
            act.wait_ge(lam_step, 2)
            act.activation(lamt[:, 2:4], lamt[:, 0:2], ACT.Exp).then_inc(lam_exp, 1)
            act.wait_ge(modg_ready, 4)
            norm_root(act, "mix", X_COLS)
            norm_gain(act, "mix", X_COLS, vec_gain(V_MIX), no_shift)
            for s in range(2):
                act.wait_ge(n_low[s], 4 * (SPLITS["mix"] + 1) + 1)
            keep(act, "gelu", z1, 0, 8, slice(0, SEQ), ACT.Gelu)
            keep(act, "plain", z1, 8 * P, 12, slice(0, SEQ), ACT.Copy)
            act.wait_ge(w_used[0], W0["forget"][0] + 1 + 1)
            act.activation(f_x[:], acc[0][0:8, 0:SEQ], ACT.Identity, bias=fb[:]).then_inc(acc_free[0], 1)
            act.wait_ge(acc_free[0], A0["forget"][0] + 1 + 1)
            act.activation(f_a[:], f_x[:], ACT.Abs).then_inc(f_soft, 1)
            act.wait_ge(f_soft, 1)
            act.activation(f_a[:], f_a[:], ACT.Exp, scale=-1.0).then_inc(f_soft, 1)
            act.wait_ge(f_soft, 2)
            act.activation(f_a[:], f_a[:], ACT.Ln, bias=one[0:8, :]).then_inc(f_soft, 1)
            act.wait_ge(f_scan, 24)
            for part in range(2):
                act.dma_start(forget_rows[part], f_parts[:, part].bitcast(F32)).then_inc(f_stored, 16)
            with act.Fori(0, 4) as j:
                act.wait_ge(s_turned, j + 1)
                turned = bank(2)[:, 0:2 * P].rearrange("p (e t) -> p e t", e=2)
                act.activation(s_wt[0:64, :, :], turned[0:64], ACT.Copy).then_inc(s_wt_ready, 1)
                act.activation(s_wt[64:P, :, 64:P], turned[64:P, :, 64:P], ACT.Copy).then_inc(s_wt_ready, 1)
                act.wait_ge(s_stats, 6 * j + 3)
                act.activation(s_sq[:], s_ctr[:], ACT.Square).then_inc(s_squared, 1)
                act.wait_ge(s_stats, 6 * j + 4)
                act.activation(s_stat[:, 3], s_stat[:, 2], ACT.Sqrt, bias=eps_1[:], scale=1.0 / DH).then_inc(s_std, 1)
            with act.Fori(0, 4) as j:
                def fa_exp(u):
                    s, w = u % 3, (u % QB + 1) * P
                    act.wait_ge(fa.biased, 16 * j + (u + 1))
                    act.activation(a_s[:, s, 0:w], a_s[:, s, 0:w], ACT.Exp, bias=a_small[:, 1, s:s + 1],
                                   accum_out=a_small[:, 2, s:s + 1]).then_inc(fa.exped, 1)

                for u in range(LEAD):
                    fa_exp(u)
                act.wait_ge(fa.turned, 17 * j + 1)
                act.wait_ge(fa.mixed, 4 * j + 1)
                act.activation(a_v[:].rearrange("p k d -> p (k d)"), bank(4, 2), ACT.Copy).then_inc(fa.pt_kept, 1)
                for u in range(2 * QB):
                    i, q = u % QB, u % 4
                    act.wait_ge(fa.turned, 17 * j + (u + 2))
                    if q == 0:
                        act.wait_ge(fa.mixed, 4 * j + u // 4 + 1)
                    act.activation(a_pt[:, 0:i + 1, q * P:(q + 1) * P],
                                   ps[:, 4 * BANK:4 * BANK + (i + 1) * P].rearrange("p (k q) -> p k q", q=P),
                                   ACT.Copy).then_inc(fa.pt_kept, 1)
                    if u + LEAD < 2 * QB:
                        fa_exp(u + LEAD)
            for s in range(2):
                act.wait_ge(acc_free[s], A0["ffn"][s] + 1)
            norm_root(act, "ffn", X_COLS)
            norm_gain(act, "ffn", X_COLS, vec_gain(V_FFN), no_shift)
            for s in range(2):
                act.wait_ge(n_low[s], 4 * (SPLITS["ffn"] + 1) + 1)

            def ffn_up(chunk, e, acc_use):
                for s in range(2):
                    tile = 2 * chunk + (s * FT + e)
                    act.wait_ge(w_used[s], 2 * chunk + (W0["ffn"][s] + e + 1) + 1)
                    act.wait_ge(f_mult, 2 * chunk + e)
                    act.activation(f_y[:, s], acc[s][:, 0:SEQ], ACT.Identity, bias=convv[:, bass.ds(tile + 6 * FT, 1)],
                                   scale=convv[:, bass.ds(tile + 4 * FT, 1)]).then_inc(f_based[s], 1)
                act.wait_ge(acc_free[0], acc_use + (A0["ffn"][0] + 1) + 1)
                act.activation(f_g[:], f_y[:, 0], ACT.Silu).then_inc(f_gate, 1)

            ffn_up(0, 0, 0)
            ffn_up(0, 1, 1)
            with act.Fori(1, CHUNKS) as c:
                ffn_up(c, 0, 6 * c - 4)
                ffn_up(c, 1, 6 * c + 1)
            for s in range(2):
                act.wait_ge(acc_free[s], A0["a_qk"][s] + 1)
            norm_root(act, "fin", X_COLS)
            norm_gain(act, "fin", X_COLS, vec_gain(V_FIN), no_shift)
            for s in range(2):
                act.wait_ge(n_gained[s], 4 * (NORMS["fin"] + 1) + 1)
            for name, cols, v in (("a_x", X_COLS, 0), ("a_ctx", slice(0, CTX), 1)):
                norm_root(act, name, cols)
                norm_gain(act, name, cols, mod_gain(0, v), mod_shift(0, v))
            for s in range(2):
                act.wait_ge(n_low[s], 4 * (SPLITS["a_ctx"] + 1) + 1)
            keep_rotated(act, "a_qk", za, 0, 16, slice(0, TOK))
            keep(act, "a_v", za, 16 * P, 8, slice(0, TOK), ACT.Copy)
            keep(act, "a_gate", za, 24 * P, 8, slice(0, TOK), ACT.Silu)
            with act.Fori(0, 8) as h:
                def da_freed(*key):
                    b, n = DA_PLAN[key]
                    return b, DA_TURNS[b] * h + (n + 1)

                def da_exp(u):
                    w, s = da_tiles(u) * P, u % 3
                    act.wait_ge(da.biased, 10 * h + (u + 1))
                    act.activation(d_p0[:, s, 0:w], d_p0[:, s, 0:w], ACT.Exp, bias=d_small[:, s, 2:3],
                                   accum_out=d_small[:, s, 4:5]).then_inc(da.exped, 1)
                    act.activation(d_p1[:, u % 2, 0:w], d_p1[:, u % 2, 0:w], ACT.Exp, bias=d_small[:, s, 3:4],
                                   accum_out=d_small[:, s, 5:6]).then_inc(da_exped1, 1)

                def da_rms_of(g):
                    b, n = da_freed("out", g)
                    act.wait_ge(da_free[b], n + 1)
                    act.wait_ge(da_ssq, 5 * h + g + 1)
                    act.activation(d_o[:, 1], d_o[:, 0], ACT.Square).then_inc(da_sq, 1)
                    b, n = da_freed("sum", g)
                    act.wait_ge(da_ssq, 5 * h + (g + 1) + 1)
                    act.wait_ge(da.low, 5 * h + g + 1)
                    act.activation(d_o[:, 1], bank(6 + b)[:, 0:2 * P], ACT.Ln, bias=eps_sub[:], scale=1.0 / P).then_inc(da_free[b], 1)
                    act.wait_ge(da_free[b], n + 1)
                    act.activation(d_o[:, 1], d_o[:, 1], ACT.Exp, scale=-0.5).then_inc(da_rms, 1)

                for u in range(LEAD):
                    da_exp(u)
                for n, blocks in enumerate(batches(TOK // P)):
                    b, _ = da_freed("v", n)
                    act.wait_ge(da.turned, DA_BATCHES * h + (n + 1))
                    act.wait_ge(da.mixed, 5 * h + 1)
                    act.activation(d_v[:, blocks.start:blocks.stop, :],
                                   bank(6 + b)[:, 0:len(blocks) * P].rearrange("p (k d) -> p k d", d=P), ACT.Copy).then_inc(da_free[b], 1)
                for u in range(10):
                    for n, blocks in enumerate(batches(da_tiles(u))):
                        b, _ = da_freed("p", u, n)
                        act.wait_ge(da.turned, DA_BATCHES * h + (da_turned(u - 1) + n + 1))
                        if u % 2 == 0:
                            act.wait_ge(da.mixed, 5 * h + u // 2 + 1)
                        act.activation(d_pt[:, blocks.start:blocks.stop, (u % 2) * P:(u % 2 + 1) * P],
                                       bank(6 + b)[:, 0:len(blocks) * P].rearrange("p (k q) -> p k q", q=P),
                                       ACT.Copy).then_inc(da_free[b], 1)
                    if u >= 2 and u % 2 == 0:
                        da_rms_of(u // 2 - 1)
                    if u + LEAD < 10:
                        da_exp(u + LEAD)
                da_rms_of(4)
            for s in range(2):
                act.wait_ge(acc_free[s], A0["b_q"][s] + 1)
            for name, cols, v in (("b_x", X_COLS, 0), ("b_ctx", slice(0, CTX), 1)):
                norm_root(act, name, cols)
                norm_gain(act, name, cols, mod_gain(1, v), mod_shift(1, v))
            for s in range(2):
                act.wait_ge(n_low[s], 4 * (SPLITS["b_ctx"] + 1) + 1)
            keep_rotated(act, "b_q", zb[:, X_COLS], 0, 8, slice(0, SEQ))
            keep_rotated(act, "b_k", zb, 8 * P, 2, slice(0, TOK))
            keep(act, "b_v", zb, 10 * P, 2, slice(0, TOK), ACT.Copy)
            keep(act, "b_gate", zb[:, X_COLS], 12 * P, 8, slice(0, SEQ), ACT.Silu)
            with act.Fori(0, 4) as h:
                def ba_exp(u):
                    i, a = divmod(u, 4)
                    s, w = u % 3, len(window_tiles(i)) * P
                    act.wait_ge(ba.biased, 32 * h + (u + 1))
                    act.activation(b_s[:, s, 0:w], b_s[:, s, 0:w], ACT.Exp, bias=b_small[:, 1, s:s + 1],
                                   accum_out=b_small[:, 2, s:s + 1]).then_inc(ba.exped, 1)
                    act.activation(b_small[:, 5, s:s + 1], sinks[:, bass.ds(4 * h + a, 1)], ACT.Exp,
                                   bias=b_small[:, 1, s:s + 1]).then_inc(ba.exped, 1)

                for u in range(LEAD):
                    ba_exp(u)
                for n, (k0, k1) in enumerate(((0, 8), (8, 10))):
                    act.wait_ge(ba.turned, 34 * h + (n + 1))
                    act.wait_ge(ba.mixed, 8 * h + 1)
                    act.activation(b_v[:, k0:k1, :], ps[:, 4 * BANK:4 * BANK + (k1 - k0) * P].rearrange("p (k d) -> p k d", d=P),
                                   ACT.Copy).then_inc(ba.pt_kept, 1)
                for u in range(4 * QB):
                    i, a = divmod(u, 4)
                    nk = len(window_tiles(i))
                    act.wait_ge(ba.turned, 34 * h + (u + 3))
                    if a == 0:
                        act.wait_ge(ba.mixed, 8 * h + i + 1)
                    act.activation(b_pt[:, 0:nk, a * P:(a + 1) * P],
                                   ps[:, 4 * BANK:4 * BANK + nk * P].rearrange("p (k q) -> p k q", q=P),
                                   ACT.Copy).then_inc(ba.pt_kept, 1)
                    if u + LEAD < 4 * QB:
                        ba_exp(u + LEAD)
            for s in range(2):
                act.wait_ge(acc_free[s], A0["b_out"][s] + 4 + 1)
            norm_root(act, "out", X_COLS)
            norm_gain(act, "out", X_COLS, vec_gain(V_FG2), no_shift)

        def norm_scale(dve, name, cols):
            n, w = NORMS[name], cols.stop - cols.start
            dve.memset(n_sum[:, 0:w], 0.0).then_inc(n_zeroed, 1)
            dve.wait_ge(n_zeroed, n + 1)
            with dve.Fori(0, KT // 2) as i:
                for s in range(2):
                    dve.wait_ge(n_squared[s], i + (4 * n + 1))
                    dve.wait_ge(n_added[1 - s], i + (4 * n + s) + 1)
                    dve.tensor_tensor(n_sum[:, 0:w], n_sum[:, 0:w], n_sq[:, s, 0:w], ALU.add).then_inc(n_added[s], 1)
            dve.wait_ge(n_root, n + 1)
            dve.reciprocal(n_rs[:, 0:w], n_rs[:, 0:w]).then_inc(n_scaled, 1)
            dve.wait_ge(n_scaled, n + 1)
            with dve.Fori(0, KT // 2) as i:
                for s in range(2):
                    dve.wait_ge(n_gained[s], i + 4 * n + 1)
                    dve.tensor_tensor(n_t[:, s:s + 1, 0:w], res[:, bass.ds(2 * i + s, 1), cols], n_rs[:, 0:w].unsqueeze(1),
                                      ALU.mult).then_inc(n_times[s], 1)
                if name in SPLITS:
                    for s in range(2):
                        dve.wait_ge(n_gained[s], i + (4 * n + 1) + 1)
                        dve.tensor_copy(hh[:, bass.ds(2 * i + s, 1), cols], n_h[:, s:s + 1, 0:w]).then_inc(n_high[s], 1)
                elif name == "out":
                    for s in range(2):
                        dve.wait_ge(out_turned[s], i + 1 + 1)
                        dve.wait_ge(out_stored[s], 16 * i + 16)
                        dve.tensor_copy(tok_out[:, s], acc[s][:, 0:SEQ].rearrange("p (t n) -> p t n", n=P)).then_inc(out_kept[s], 1)

        def add_to_residual(dve, name, parts):
            with dve.Fori(0, KT // 2) as i:
                for s in range(2):
                    dve.wait_ge(w_used[s], i + (W0[name][s] + 1) + 1)
                    for n, (cols, p0, gate) in enumerate(parts):
                        at = res[:, bass.ds(2 * i + s, 1), cols]
                        got = acc[s][:, p0:p0 + cols.stop - cols.start].unsqueeze(1)
                        if gate is None:
                            ins = dve.tensor_tensor(at, got, at, ALU.add)
                        else:
                            layer, v = gate
                            ins = dve.scalar_tensor_tensor(at, got, mod[:, bass.ds(2 * i + (s + 24 * layer + 16), 1), v], at,
                                                           ALU.mult, ALU.add)
                        if n == len(parts) - 1:
                            ins.then_inc(acc_free[s], 1)

        def rotate(dve, name, tiles, first):
            cols = slice(first, first + SEQ)
            with dve.Fori(0, tiles // 2) as i:
                for s in range(2):
                    n = 2 * i + (R0[name] + s)
                    dve.wait_ge(r_swapped, n + 1)
                    dve.wait_ge(r_roped, n + 1)
                    dve.tensor_tensor(r_rot[:], bank(6, 2), r_sin[:], ALU.mult).then_inc(r_read, 1)
                    dve.tensor_tensor(z_out[:, s, cols], z_out[:, s, cols], r_cos[:], ALU.mult).then_inc(r_turned, 1)
                    dve.wait_ge(r_read, n + 1 + 1)
                    dve.wait_ge(r_turned, n + 1)
                    dve.tensor_tensor(z_out[:, s, cols], z_out[:, s, cols], r_rot[:], ALU.add).then_inc(r_roped, 1)

        @block.vector
        def _(dve):
            def keep_tokens(s, use, col):
                dve.wait_ge(tok_turned[s], use + 1)
                dve.tensor_copy(res[:, :, bass.ds(col, P)],
                                acc[s][:, 0:KT * P].rearrange("p (k t) -> p k t", t=P)).then_inc(tok_kept[s], 1)

            for s in range(2):
                keep_tokens(s, 0, s * P)
            with dve.Fori(0, QB // 2) as i:
                for s in range(2):
                    keep_tokens(s, i + 1, (2 * i + s) * P + CTX)
            dve.wait_ge(rows_turned, 1)
            dve.tensor_copy(vec[:], bank(6)[:, 0:V_END]).then_inc(vec_ready, 1)
            dve.tensor_copy(convv[:], bank(7)[:, 0:4 * 2 * FT]).then_inc(vec_ready, 1)
            dve.wait_ge(consts_in, 16 * 10)
            for n in range(2):
                dve.tensor_tensor_reduce(lamrows[:, 2 * n], lamrows[:, 2 * n], lamrows[:, 2 * n + 1], 1.0, 0.0, ALU.mult,
                                         ALU.add, lamt[:, n:n + 1]).then_inc(lam_step, 1)
            for n, rows_ in enumerate((ident[:], maskrows[:, 0], maskrows[:, 1])):
                dve.tensor_copy(masks[:, n], rows_).then_inc(masks_ready, 1)
            dve.wait_ge(vec_ready, 2)
            dve.tensor_scalar(vec32[:], vec[:, 0:V_BMOD], float(D) ** 0.5, None, ALU.mult).then_inc(vec32_ready, 1)
            dve.tensor_scalar(subg[:], vec[:, V_SUB:V_SUB + 1], 1.0 - LAM_INIT, None, ALU.mult).then_inc(vec32_ready, 1)
            dve.wait_ge(lam_exp, 1)
            dve.scalar_tensor_tensor(lam[:], lamt[:, 2:3], LAM_INIT, lamt[:, 3:4], ALU.add, ALU.subtract).then_inc(lam_step, 1)
            for layer in range(2):
                with dve.Fori(0, 6) as i:
                    for s in range(2):
                        dve.wait_ge(mod_summed[s], i + (6 * layer + 1) + 1)
                        for n in range(2):
                            t = 4 * i + (2 * s + n + 24 * layer)
                            dve.tensor_scalar(mod[:, bass.ds(t, 1), :], acc[s][:, 2 * n:2 * n + 2].unsqueeze(1),
                                              vec[:, bass.ds(t + V_BMOD, 1)], None, ALU.add).then_inc(mod_kept[s], 1)
            for s in range(2):
                dve.wait_ge(mod_kept[s], 24 + 1)
            dve.wait_ge(vec32_ready, 2)
            for layer in range(2):
                for v in range(2):
                    dve.scalar_tensor_tensor(modg[:, layer, v], mod[:, 24 * layer + 8:24 * layer + 16, v], 1.0,
                                             vec32[:, V_G2 + KT * layer:V_G2 + KT * (layer + 1)], ALU.add,
                                             ALU.mult).then_inc(modg_ready, 1)
            norm_scale(dve, "mix", X_COLS)
            dve.wait_ge(f_soft, 3)
            dve.scalar_tensor_tensor(f_s[:, 0], f_x[:], 0.0, f_a[:], ALU.min, ALU.subtract).then_inc(f_scan, 1)
            for n in range(10):
                a, b, d = n % 2, 1 - n % 2, 1 << n
                dve.wait_ge(f_scan, 2 * n + 1)
                dve.tensor_copy(f_s[:, b, 0:d], f_s[:, a, 0:d]).then_inc(f_scan, 1)
                dve.tensor_tensor(f_s[:, b, d:], f_s[:, a, d:], f_s[:, a, 0:SEQ - d], ALU.add).then_inc(f_scan, 1)
            dve.wait_ge(f_scan, 21)
            dve.tensor_scalar(f_x[:], f_s[:, 0], -1.0 / SCALE, None, ALU.mult).then_inc(f_scan, 1)
            dve.wait_ge(f_scan, 22)
            dve.tensor_copy(f_parts[:, 0], f_x[:]).then_inc(f_scan, 1)
            dve.wait_ge(f_scan, 23)
            dve.tensor_tensor(f_parts[:, 1], f_x[:], f_parts[:, 0].bitcast(F32), ALU.subtract).then_inc(f_scan, 1)
            with dve.Fori(0, 4) as j:
                v = ps[:, 0:2 * BANK].rearrange("p (g d) -> p g d", d=DH)

                def by_head(n):
                    return s_stat[:, n].unsqueeze(2).broadcast_to([P, 16, DH])

                dve.wait_ge(s_turned, j + 1)
                dve.tensor_reduce(s_stat[:, 0], v, AX, ALU.add).then_inc(s_stats, 1)
                dve.wait_ge(s_stats, 6 * j + 1)
                dve.tensor_scalar(s_stat[:, 1], s_stat[:, 0], 1.0 / DH, None, ALU.mult).then_inc(s_stats, 1)
                dve.wait_ge(s_stats, 6 * j + 2)
                dve.tensor_tensor(s_ctr[:], v, by_head(1), ALU.subtract).then_inc(s_stats, 1)
                dve.wait_ge(s_squared, j + 1)
                dve.tensor_reduce(s_stat[:, 2], s_sq[:], AX, ALU.add).then_inc(s_stats, 1)
                dve.wait_ge(s_std, j + 1)
                dve.reciprocal(s_stat[:, 3], s_stat[:, 3]).then_inc(s_stats, 1)
                dve.wait_ge(s_stats, 6 * j + 5)
                dve.tensor_tensor(s_ctr[:], s_ctr[:], by_head(3), ALU.mult).then_inc(s_stats, 1)
                dve.wait_ge(s_in, 80 * j + 80)
                dve.wait_ge(s_mixed, j + 1)
                dve.wait_ge(s_low, j + 1)
                for e in range(2):
                    r = slice(e * DH, (e + 1) * DH)
                    got = ps[r, 4 * BANK:].rearrange("p (n e t) -> p n e t", e=2, t=P)[:, :, e]
                    dve.scalar_tensor_tensor(s_y[r].rearrange("p (n t) -> p n t", t=P), got, vec[r, bass.ds(j + V_LNG, 1)],
                                             s_b[r].unsqueeze(1).broadcast_to([DH, QB, P]), ALU.mult, ALU.add).then_inc(s_gated, 1)
                dve.wait_ge(s_gated, 4 * j + 2)
                dve.tensor_tensor(s_y[:], s_y[:], s_u[:], ALU.mult).then_inc(s_gated, 1)
                dve.wait_ge(s_gated, 4 * j + 3)
                dve.tensor_copy(hh[:, bass.ds(j, 1), X_COLS], s_y[:].unsqueeze(1)).then_inc(s_gated, 1)
            with dve.Fori(0, 4) as j:
                def fa_max(u):
                    s, at, w = u % 3, 2 * (u % 2) * BANK, (u % QB + 1) * P
                    dve.wait_ge(fa.scored, 16 * j + (u + 1) + 1)
                    if u >= 3:
                        dve.wait_ge(fa.turned, 17 * j + (u - 1))
                    dve.tensor_scalar(a_s[:, s, 0:w], ps[:, at:at + w], SCALE, LOWEST, ALU.mult, ALU.max,
                                      accum_out=a_small[:, 0, s:s + 1]).then_inc(fa.maxed, 1)
                    dve.wait_ge(fa.maxed, 16 * j + (u + 1))
                    dve.tensor_scalar(a_small[:, 1, s:s + 1], a_small[:, 0, s:s + 1], -1.0, None, ALU.mult).then_inc(fa.biased, 1)

                def fa_keep(g):
                    r, c0 = slice((g // 2) * DH, (g // 2 + 1) * DH), CTX + (g % 2) * BANK
                    to = (r, bass.ds(j + 4, 1), slice(c0, c0 + BANK))
                    dve.wait_ge(fa.mixed, 4 * j + (g + 1) + 1)
                    dve.tensor_copy(hh[to], bank(6)[r].unsqueeze(1)).then_inc(fa.kept, 1)
                    dve.wait_ge(fa.kept, 8 * j + (2 * g + 1) + 1)
                    dve.tensor_tensor(hl[to], bank(6)[r].unsqueeze(1), hh[to].bitcast(F32), ALU.subtract).then_inc(fa.kept, 1)

                for u in range(LEAD):
                    fa_max(u)
                for u in range(2 * QB):
                    s, w = u % 3, (u % QB + 1) * P
                    dve.wait_ge(fa.exped, 16 * j + (u + 1))
                    dve.reciprocal(a_small[:, 3, s:s + 1], a_small[:, 2, s:s + 1]).then_inc(fa.weighed, 1)
                    dve.wait_ge(fa.weighed, 32 * j + (2 * u + 1))
                    dve.tensor_scalar(a_s[:, s, 0:w], a_s[:, s, 0:w], a_small[:, 3, s:s + 1], None, ALU.mult).then_inc(fa.weighed, 1)
                    if u + LEAD < 2 * QB:
                        fa_max(u + LEAD)
                    if u and u % 4 == 0:
                        fa_keep(u // 4 - 1)
                fa_keep(3)
            add_to_residual(dve, "w_out", ((X_COLS, 0, None),))
            norm_scale(dve, "ffn", X_COLS)

            def ffn_taps(chunk, e, acc_use):
                for s in range(2):
                    tile = 2 * chunk + (s * FT + e)
                    dve.wait_ge(f_based[s], 2 * chunk + (e + 1))
                    dve.scalar_tensor_tensor(f_y[:, s, 1:], acc[s][:, 0:SEQ - 1], convv[:, bass.ds(tile + 2 * FT, 1)],
                                             f_y[:, s, 1:], ALU.mult, ALU.add).then_inc(f_tapped[s], 1)
                    dve.wait_ge(f_tapped[s], 2 * chunk + (e + 1))
                    dve.scalar_tensor_tensor(f_y[:, s, 2:], acc[s][:, 0:SEQ - 2], convv[:, bass.ds(tile, 1)],
                                             f_y[:, s, 2:], ALU.mult, ALU.add).then_inc(acc_free[s], 1)
                dve.wait_ge(f_gate, 2 * chunk + (e + 1))
                dve.wait_ge(acc_free[1], acc_use + (A0["ffn"][1] + 1) + 1)
                dve.wait_ge(f_low, 2 * chunk + e)
                dve.tensor_tensor(f_act[:], f_g[:], f_y[:, 1], ALU.mult).then_inc(f_mult, 1)

            def ffn_high(chunk, e):
                dve.wait_ge(f_mult, 2 * chunk + (e + 1))
                dve.wait_ge(d_used, chunk + 1)
                dve.tensor_copy(f_hi[:, e], f_act[:]).then_inc(f_high, 1)

            def ffn_down(chunk):
                for m in range(KT):
                    if m < KT - 1:
                        dve.wait_ge(f_down, 7 * chunk + (m + 1))
                    else:
                        dve.wait_ge(d_used, chunk + 1 + 1)
                    dve.tensor_tensor(res[:, m, X_COLS], acc[m % 2][:, 0:SEQ], res[:, m, X_COLS], ALU.add).then_inc(acc_free[m % 2], 1)

            ffn_taps(0, 0, 0)
            ffn_high(0, 0)
            ffn_taps(0, 1, 1)
            ffn_high(0, 1)
            with dve.Fori(1, CHUNKS) as c:
                ffn_taps(c, 0, 6 * c - 4)
                ffn_down(c - 1)
                ffn_high(c, 0)
                ffn_taps(c, 1, 6 * c + 1)
                ffn_high(c, 1)
            ffn_down(CHUNKS - 1)
            norm_scale(dve, "fin", X_COLS)
            for s in range(2):
                dve.wait_ge(n_gained[s], 4 * (NORMS["fin"] + 1) + 1)
            norm_scale(dve, "a_x", X_COLS)
            norm_scale(dve, "a_ctx", slice(0, CTX))
            for s in range(2):
                dve.wait_ge(n_low[s], 4 * (SPLITS["a_ctx"] + 1) + 1)
            dve.wait_ge(consts_in, 16 * 12)
            rotate(dve, "a_qk", 16, CTX)
            dve.wait_ge(lam_step, 3)
            with dve.Fori(0, 8) as h:
                def da_max(u):
                    s, w = u % 3, da_tiles(u) * P
                    if u >= 3:
                        dve.wait_ge(da.turned, DA_BATCHES * h + da_turned(u - 3))
                    dve.wait_ge(da.scored, 10 * h + (u + 1))
                    dve.tensor_scalar(d_p0[:, s, 0:w], acc[0][:, 0:w], SCALE, LOWEST, ALU.mult, ALU.max,
                                      accum_out=d_small[:, s, 0:1]).then_inc(da.maxed, 1)
                    dve.wait_ge(da_scored1, 10 * h + (u + 1) + 1)
                    dve.tensor_scalar(d_p1[:, u % 2, 0:w], acc[1][:, 0:w], SCALE, LOWEST, ALU.mult, ALU.max,
                                      accum_out=d_small[:, s, 1:2]).then_inc(da_maxed1, 1)
                    dve.wait_ge(da.maxed, 10 * h + (u + 1) + 1)
                    dve.wait_ge(da_maxed1, 10 * h + (u + 1) + 1)
                    dve.tensor_scalar(d_small[:, s, 2:4], d_small[:, s, 0:2], -1.0, None, ALU.mult).then_inc(da.biased, 1)

                def da_take_out(g):
                    b, _ = DA_PLAN["out", g]
                    dve.wait_ge(da.mixed, 5 * h + (g + 1) + 1)
                    dve.wait_ge(da.low, 5 * h + g + 1)
                    dve.tensor_copy(d_o[:, 0], bank(6 + b)[:, 0:2 * P]).then_inc(da_free[b], 1)

                def da_finish(g):
                    cols = slice(g * 2 * P, (g + 1) * 2 * P)
                    dve.wait_ge(da_gloaded, 16 * h + 16)
                    dve.wait_ge(da_rms, 5 * h + (g + 1))
                    dve.tensor_tensor(d_o[:, 0], d_o[:, 0], d_o[:, 1], ALU.mult).then_inc(da.kept, 1)
                    dve.wait_ge(da.kept, 15 * h + (3 * g + 1))
                    dve.scalar_tensor_tensor(d_o[:, 0], d_o[:, 0], subg[:], d_g[:, cols], ALU.mult, ALU.mult).then_inc(da.kept, 1)
                    dve.wait_ge(da.kept, 15 * h + (3 * g + 2))
                    dve.tensor_copy(hh[:, bass.ds(h, 1), cols], d_o[:, 0:1]).then_inc(da.kept, 1)

                for u in range(LEAD):
                    da_max(u)
                for u in range(10):
                    s, w = u % 3, da_tiles(u) * P
                    dve.wait_ge(da.exped, 10 * h + (u + 1))
                    dve.wait_ge(da_exped1, 10 * h + (u + 1))
                    dve.reciprocal(d_small[:, s, 6:8], d_small[:, s, 4:6]).then_inc(da.weighed, 1)
                    dve.wait_ge(da.weighed, 40 * h + (4 * u + 1))
                    dve.tensor_tensor(d_small[:, s, 7:8], d_small[:, s, 7:8], lam[:], ALU.mult).then_inc(da.weighed, 1)
                    dve.wait_ge(da.weighed, 40 * h + (4 * u + 2))
                    dve.tensor_scalar(d_p1[:, u % 2, 0:w], d_p1[:, u % 2, 0:w], d_small[:, s, 7:8], None, ALU.mult).then_inc(da.weighed, 1)
                    dve.wait_ge(da.weighed, 40 * h + (4 * u + 3))
                    dve.scalar_tensor_tensor(d_p0[:, s, 0:w], d_p0[:, s, 0:w], d_small[:, s, 6:7], d_p1[:, u % 2, 0:w], ALU.mult,
                                             ALU.subtract).then_inc(da.weighed, 1)
                    if u >= 2 and u % 2 == 0:
                        da_take_out(u // 2 - 1)
                    if u + LEAD < 10:
                        da_max(u + LEAD)
                    if u >= 2 and u % 2 == 0:
                        da_finish(u // 2 - 1)
                da_take_out(4)
                da_finish(4)
            add_to_residual(dve, "a_out", ((X_COLS, CTX, (0, 0)), (slice(0, CTX), 0, (0, 1))))
            norm_scale(dve, "b_x", X_COLS)
            norm_scale(dve, "b_ctx", slice(0, CTX))
            for s in range(2):
                dve.wait_ge(n_low[s], 4 * (SPLITS["b_ctx"] + 1) + 1)
            dve.wait_ge(consts_in, 16 * 14)
            rotate(dve, "b_q", 8, 0)
            rotate(dve, "b_k", 2, CTX)
            with dve.Fori(0, 4) as h:
                def ba_max(u):
                    i, a = divmod(u, 4)
                    s, at, w = u % 3, 2 * (u % 2) * BANK, len(window_tiles(i)) * P
                    dve.wait_ge(ba.scored, 32 * h + (u + 1) + 1)
                    if u >= 3:
                        dve.wait_ge(ba.turned, 34 * h + u)
                    dve.tensor_scalar(b_s[:, s, 0:w], ps[:, at:at + w], SCALE, LOWEST, ALU.mult, ALU.max,
                                      accum_out=b_small[:, 0, s:s + 1]).then_inc(ba.maxed, 1)
                    dve.wait_ge(ba.maxed, 32 * h + (u + 1))
                    dve.tensor_scalar(b_small[:, 1, s:s + 1], b_small[:, 0, s:s + 1], sinks[:, bass.ds(4 * h + a, 1)], -1.0,
                                      ALU.max, ALU.mult).then_inc(ba.biased, 1)

                def ba_keep(i):
                    cols = slice(CTX + i * P, CTX + (i + 1) * P)
                    got = bank(6).rearrange("p (t e q) -> p t e q", t=2, e=2)
                    dve.wait_ge(ba_gloaded, 16 * h + 16)
                    dve.wait_ge(ba.mixed, 8 * h + (i + 1) + 1)
                    dve.wait_ge(ba.low, 8 * h + i + 1)
                    for e in range(2):
                        r = slice(e * DH, (e + 1) * DH)
                        dve.tensor_tensor(b_y[r], got[r, :, e], b_g[r, :, i * P:(i + 1) * P], ALU.mult).then_inc(ba.kept, 1)
                    dve.wait_ge(ba.kept, 24 * h + (3 * i + 2))
                    dve.tensor_copy(hh[:, bass.ds(2 * h, 2), cols], b_y[:]).then_inc(ba.kept, 1)

                for u in range(LEAD):
                    ba_max(u)
                for u in range(4 * QB):
                    i, a = divmod(u, 4)
                    s, w = u % 3, len(window_tiles(i)) * P
                    dve.wait_ge(ba.exped, 64 * h + (2 * u + 2))
                    dve.tensor_tensor(b_small[:, 3, s:s + 1], b_small[:, 2, s:s + 1], b_small[:, 5, s:s + 1], ALU.add).then_inc(ba.weighed, 1)
                    dve.wait_ge(ba.weighed, 96 * h + (3 * u + 1))
                    dve.reciprocal(b_small[:, 4, s:s + 1], b_small[:, 3, s:s + 1]).then_inc(ba.weighed, 1)
                    dve.wait_ge(ba.weighed, 96 * h + (3 * u + 2))
                    dve.tensor_scalar(b_s[:, s, 0:w], b_s[:, s, 0:w], b_small[:, 4, s:s + 1], None, ALU.mult).then_inc(ba.weighed, 1)
                    if u + LEAD < 4 * QB:
                        ba_max(u + LEAD)
                    if u and a == 0:
                        ba_keep(i - 1)
                ba_keep(QB - 1)
            add_to_residual(dve, "b_out", ((X_COLS, 0, (1, 0)),))
            norm_scale(dve, "out", X_COLS)


_INS = [
    "x", "norm_mix_g", "w_in", "f_bias", "sg_ln_g", "sg_w", "sg_b", "w_out", "norm_ffn_g", "w_up", "w_conv", "b_conv", "w_down",
    "norm_final_g", "c_2", "ctx_2", "c_ctx_2", "w_mod_2", "b_mod_2", "norm_g_2", "w_o_2", "a_w_in_2", "a_lambda_q1_2",
    "a_lambda_k1_2", "a_lambda_q2_2", "a_lambda_k2_2", "a_subln_g_2", "b_w_in_2", "b_sink_2", "final_g_2",
]


def constants():
    import numpy as np

    n = np.arange(P)
    causal = np.where(n[None, :] <= n[:, None], 0.0, -1e30)
    before = np.where(n[None, :] >= n[:, None], 0.0, -1e30)
    half, grid = DH // 2, 64
    inv = (np.float32(10000.0) ** (-np.arange(0, half, 2, dtype=np.float32) / np.float32(half))).astype(np.float32)
    t = np.arange(SEQ)
    place = np.stack([t // grid, t % grid]).astype(np.float32)
    angle = np.stack([place[(f % DH) // half] * inv[f % 16] for f in range(P)]).astype(np.float32)
    sign = np.where(n % half < 16, -1.0, 1.0)[:, None]
    return {
        "const_ident": np.eye(P, dtype=np.float32), "const_swap": np.eye(P, dtype=np.float32)[n ^ 16],
        "const_causal": causal.astype(np.float32), "const_before": before.astype(np.float32), "const_cos": np.cos(angle).astype(np.float32),
        "const_sin": (sign * np.sin(angle)).astype(np.float32),
    }


def kernel(**inputs):
    import numpy as np
    import concourse.bacc as bacc
    from concourse.bass_utils import run_bass_kernel_spmd

    nc = bacc.Bacc("TRN2", target_bir_lowering=False, num_devices=1)
    arrays = {f"in_{name}": np.ascontiguousarray(inputs[name]) for name in _INS}
    arrays.update(constants())
    args = [nc.dram_tensor(name, a.shape, F32, kind="ExternalInput").ap() for name, a in arrays.items()]
    args.append(nc.dram_tensor("out_rows", (1, SEQ, D), F32, kind="ExternalOutput").ap())
    two_block_kernel(nc, *args)
    got = run_bass_kernel_spmd(nc, [arrays], core_ids=[0])
    return got.results[0]["out_rows"]
```

```python
from contextlib import ExitStack

import concourse.bass as bass
from concourse import mybir

F32 = mybir.dt.float32
F32R = mybir.dt.float32r
ALU = mybir.AluOpType
ACT = mybir.ActivationFunctionType
AX = mybir.AxisListType.X

P = 128
D = 1024
KT = D // P
CTX = 256
SEQ = 1024
TOK = CTX + SEQ
BANK = 512
DH = 64
D_FF = 2816
FT = D_FF // P
CHUNKS = FT // 2
QB = SEQ // P
EPS = 1e-6
SUB_EPS = 1e-5
LAM_INIT = 0.8 - 0.6
SCALE = DH ** -0.5

V_MIX, V_FFN, V_FIN, V_G2, V_FG2, V_BMOD, V_SUB, V_LNG, V_C, V_END = 0, 8, 16, 24, 40, 48, 96, 97, 101, 117

X_COLS = slice(CTX, TOK)
DA_HEADS = 8
LEAD = 2
HIGHEST = 3.0e38


def batches(blocks):
    return [range(n, min(n + 4, blocks)) for n in range(0, blocks, 4)]


def da_tiles(u):
    return CTX // P if u < CTX // P else TOK // P


def da_plan(heads_before):
    turns = [("v", n) for n in range(len(batches(TOK // P)))]
    for u in range(TOK // P):
        weights = [("p", u, n) for n in range(len(batches(da_tiles(u))))]
        output = [("o", n) for n in range(len(batches(TOK // P)))] if u == 1 and heads_before else []
        turns += weights[0:2] + output + [("m", u - 1)] * (u > 0) + weights[2:]
    turns.append(("m", TOK // P - 1))
    return {key: n for n, key in enumerate(turns)}


def da_turn(h, *key):
    mixes = TOK // P
    first, plan = da_plan(False), da_plan(True)
    per_head, short = len(plan), len(plan) - len(first)
    if isinstance(h, int) and h == 0:
        n = first[key]
        mixed = sum(k[0] == "m" for k in first if first[k] < n)
        return n % 2, n // 2, n + 1 - mixed
    last = isinstance(h, int) and h == DA_HEADS
    n = key[1] if last else plan[key]
    mixed = 0 if last else sum(k[0] == "m" for k in plan if plan[k] < n)
    return (n - short) % 2, per_head // 2 * h + (n - short) // 2, (per_head - mixes) * h + (n - short + 1 - mixed)


def window_tiles(i):
    return [2 + i - 1] * (i > 0) + [0, 1, 2 + i] + [2 + i + 1] * (i < QB - 1)


def two_block_kernel(
    nc, x, norm_mix_g, w_in, f_bias, sg_ln_g, sg_w, sg_b, w_out, norm_ffn_g, w_up, w_conv, b_conv, w_down,
    norm_final_g, c_2, ctx_2, c_ctx_2, w_mod_2, b_mod_2, norm_g_2, w_o_2, a_w_in_2, a_lambda_q1_2, a_lambda_k1_2,
    a_lambda_q2_2, a_lambda_k2_2, a_subln_g_2, b_w_in_2, b_sink_2, final_g_2,
    const_ident, const_swap, const_causal, const_before, const_cos, const_sin, out,
):
    z1 = nc.dram_tensor("z1", (20 * P, SEQ), F32, kind="Internal").ap()
    forget_rows = nc.dram_tensor("forget_rows", (2, 8, SEQ), F32, kind="Internal").ap()
    za = nc.dram_tensor("za", (32 * P, TOK), F32, kind="Internal").ap()
    zb = nc.dram_tensor("zb", (20 * P, TOK), F32, kind="Internal").ap()

    with ExitStack() as ctx:
        def alloc(scope, name, shape, dt=F32):
            return scope.enter_context(nc.sbuf_tensor(name, shape, dt))

        def sb(name, shape, dt=F32):
            return alloc(ctx, name, shape, dt)

        def sem(name):
            return ctx.enter_context(nc.semaphore(name))

        def sem2(name):
            return [sem(f"{name}{s}") for s in range(2)]

        res = sb("res", [P, KT, TOK])
        hh = sb("hh", [P, KT, TOK], F32R)
        hl = sb("hl", [P, KT, TOK], F32R)
        w_raw = sb("w_raw", [P, 2, KT * P])
        wh = sb("wh", [P, 2, KT * P], F32R)
        wl = sb("wl", [P, 2, KT * P], F32R)
        ident = sb("ident", [P, P])
        ones = sb("ones", [P, P])
        swap = sb("swap", [P, P])
        masks = sb("masks", [P, 3, P], F32R)
        ones_r = sb("ones_r", [2, P], F32R)
        vec = sb("vec", [P, V_END])
        vec32 = sb("vec32", [P, V_BMOD])
        convv = sb("convv", [P, 4 * 2 * FT])
        mod = sb("mod", [P, 48, 2])
        modg = sb("modg", [P, 2, 2, KT])
        zero = sb("zero", [P, 1])
        eps_d = sb("eps_d", [P, 1])
        one = sb("one", [P, 1])
        eps_1 = sb("eps_1", [P, 1])
        neg_lam = sb("neg_lam", [P, 1])
        subg = sb("subg", [P, 1])
        sinks = sb("sinks", [P, 16])
        fb = sb("fb", [8, 1])
        s_wt = sb("s_wt", [P, 2, P])
        ps = ctx.enter_context(nc.psum_tensor("ps", [P, 8 * BANK], F32))

        def bank(b, n=1):
            return ps[:, b * BANK:(b + n) * BANK]

        acc = [bank(0, 3), bank(3, 3)]

        scope = ExitStack()
        tokrows = alloc(scope, "tokrows", [P, 2, D])
        rows = alloc(scope, "rows", [P, P])
        convrows = alloc(scope, "convrows", [88, 2, P])
        w_mod_sb = alloc(scope, "w_mod_sb", [P, 2, KT, 2 * P])
        cond = alloc(scope, "cond", [P, KT, 2])
        lamrows = alloc(scope, "lamrows", [P, 4, DH])
        maskrows = alloc(scope, "maskrows", [P, 2, P])
        lamt = alloc(scope, "lamt", [P, 4])
        scope.close()
        scope = ExitStack()
        n_sq = alloc(scope, "n_sq", [P, 2, SEQ])
        n_sum = alloc(scope, "n_sum", [P, SEQ])
        n_rs = alloc(scope, "n_rs", [P, SEQ])
        n_t = alloc(scope, "n_t", [P, 2, SEQ])
        n_h = alloc(scope, "n_h", [P, 2, SEQ])
        tok_out = alloc(scope, "tok_out", [P, 2, KT, P])
        scope.close()
        scope = ExitStack()
        z_out = alloc(scope, "z_out", [P, 2, TOK])
        f_x = alloc(scope, "f_x", [8, SEQ])
        f_a = alloc(scope, "f_a", [8, SEQ])
        inner = ExitStack()
        f_s = alloc(inner, "f_s", [8, 2, SEQ])
        inner.close()
        f_parts = alloc(scope, "f_parts", [8, 2, SEQ], F32R)
        scope.close()
        scope = ExitStack()
        s_keep = alloc(scope, "s_keep", [P, 7 * SEQ])
        s_u = alloc(scope, "s_u", [P, SEQ])
        s_v = alloc(scope, "s_v", [P, SEQ])
        s_w = alloc(scope, "s_w", [P, 2, P])
        s_b = alloc(scope, "s_b", [P, P])
        s_ctr = alloc(scope, "s_ctr", [P, 16, DH])
        s_sq = alloc(scope, "s_sq", [P, 16, DH])
        s_stat = alloc(scope, "s_stat", [P, 4, 16])
        s_y = alloc(scope, "s_y", [P, SEQ])
        scope.close()
        scope = ExitStack()
        a_q = alloc(scope, "a_q", [P, SEQ])
        a_k = alloc(scope, "a_k", [P, SEQ])
        a_vt = alloc(scope, "a_vt", [P, SEQ])
        a_c = alloc(scope, "a_c", [2, 2, SEQ], F32R)
        a_v = alloc(scope, "a_v", [P, QB, P])
        a_s = alloc(scope, "a_s", [P, 3, SEQ])
        a_pt = alloc(scope, "a_pt", [P, 2, QB, P])
        a_o = alloc(scope, "a_o", [P, QB, 2, DH])
        a_low = alloc(scope, "a_low", [P, 3])
        a_sum = alloc(scope, "a_sum", [P, 2, QB])
        a_rec = alloc(scope, "a_rec", [P, 2, QB])
        scope.close()
        scope = ExitStack()
        f_y = alloc(scope, "f_y", [P, 2, SEQ])
        f_g = alloc(scope, "f_g", [P, SEQ])
        f_act = alloc(scope, "f_act", [P, SEQ])
        f_hi = alloc(scope, "f_hi", [P, 2, SEQ], F32R)
        f_lo = alloc(scope, "f_lo", [P, 2, SEQ], F32R)
        d_raw = alloc(scope, "d_raw", [P, 2, D])
        d_hi = alloc(scope, "d_hi", [P, 2, D], F32R)
        d_lo = alloc(scope, "d_lo", [P, 2, D], F32R)
        scope.close()
        scope = ExitStack()
        d_q = alloc(scope, "d_q", [P, TOK])
        d_k = alloc(scope, "d_k", [P, TOK])
        d_g = w_raw[:].rearrange("p s n -> p (s n)")[:, 0:TOK]
        d_v = alloc(scope, "d_v", [P, TOK // P, P])
        d_p0 = alloc(scope, "d_p0", [P, 3, TOK])
        d_p1 = alloc(scope, "d_p1", [P, 2, TOK])
        d_pt = alloc(scope, "d_pt", [P, 2, TOK // P, P])
        d_vt = d_pt[:, 0].rearrange("p k q -> p (k q)")
        d_o = alloc(scope, "d_o", [P, TOK // P, P])
        d_sq = alloc(scope, "d_sq", [P, P])
        d_low = alloc(scope, "d_low", [P, 3, 2])
        d_sum = alloc(scope, "d_sum", [P, 2, TOK // P])
        d_rec = alloc(scope, "d_rec", [P, 3, 2])
        d_ss = alloc(scope, "d_ss", [P, TOK // P])
        d_eps = alloc(scope, "d_eps", [P, TOK // P])
        d_rs = alloc(scope, "d_rs", [P, TOK // P])
        scope.close()
        scope = ExitStack()
        b_q = alloc(scope, "b_q", [P, 2, SEQ])
        b_k = alloc(scope, "b_k", [P, TOK])
        b_vt = alloc(scope, "b_vt", [P, TOK // 2])
        b_v = alloc(scope, "b_v", [P, TOK // 2 // P, 2, DH])
        b_g = alloc(scope, "b_g", [P, 2, SEQ])
        b_s = alloc(scope, "b_s", [P, 3, 5 * P])
        b_pt = alloc(scope, "b_pt", [P, 2, 5, P])
        b_o = alloc(scope, "b_o", [P, 2 * P])
        b_y = alloc(scope, "b_y", [P, 2, P])
        b_low = alloc(scope, "b_low", [P, 2, 3])
        b_sum = alloc(scope, "b_sum", [P, 2, 4])
        b_sink = alloc(scope, "b_sink", [P, 2, 4])
        b_rec = alloc(scope, "b_rec", [P, 2, 4])
        scope.close()
        scope = ExitStack()
        r_keep = alloc(scope, "r_keep", [P, 2 * TOK])
        r_cos = alloc(scope, "r_cos", [P, SEQ])
        r_sin = alloc(scope, "r_sin", [P, SEQ])
        r_rot = alloc(scope, "r_rot", [P, SEQ])
        scope.close()

        consts_in = sem("consts_in")
        rows_in = sem("rows_in")
        zeroed = sem("zeroed")
        rows_turned, vec_ready = sem("rows_turned"), sem("vec_ready")
        vec32_ready, cond_ready = sem("vec32_ready"), sem("cond_ready")
        tok_in, tok_turned, tok_kept = sem2("tok_in"), sem2("tok_turned"), sem2("tok_kept")
        lam_step = sem("lam_step")
        lam_exp = sem("lam_exp")
        mod_in, mod_summed, mod_kept = sem2("mod_in"), sem2("mod_summed"), sem2("mod_kept")
        modg_ready = sem("modg_ready")
        w_landed, w_high, w_split, w_used = sem2("w_landed"), sem2("w_high"), sem2("w_split"), sem2("w_used")
        acc_free, stored = sem2("acc_free"), sem2("stored")
        res_added = sem("res_added")
        n_squared, n_added = sem2("n_squared"), sem2("n_added")
        n_zeroed, n_summed, n_root, n_scaled = sem("n_zeroed"), sem("n_summed"), sem("n_root"), sem("n_scaled")
        n_times, n_gained = sem2("n_times"), sem2("n_gained")
        n_high, n_low = sem2("n_high"), sem2("n_low")
        out_turned, out_kept, out_stored = sem2("out_turned"), sem2("out_kept"), sem2("out_stored")
        f_biased, f_soft, f_scan, f_stored = sem("f_biased"), sem("f_soft"), sem("f_scan"), sem("f_stored")
        s_in, s_turned, s_stats, s_squared, s_std = sem("s_in"), sem("s_turned"), sem("s_stats"), sem("s_squared"), sem("s_std")
        s_wt_ready, s_mixed, s_gated, s_low = sem("s_wt_ready"), sem("s_mixed"), sem("s_gated"), sem("s_low")
        f_based, f_tapped, f_gate, f_mult = sem2("f_based"), sem2("f_tapped"), sem("f_gate"), sem("f_mult")
        f_high, f_low, f_down = sem("f_high"), sem("f_low"), sem("f_down")
        d_landed, d_high, d_split, d_used = sem2("d_landed"), sem2("d_high"), sem2("d_split"), sem("d_used")
        r_swapped, r_read, r_turned, r_roped = sem("r_swapped"), sem("r_read"), sem("r_turned"), sem("r_roped")
        masks_ready = sem("masks_ready")

        class Mixer:
            def __init__(self, name):
                self.loaded, self.scored = sem(name + "_loaded"), sem(name + "_scored")
                self.maxed, self.exped = sem(name + "_maxed"), sem(name + "_exped")
                self.turned, self.pt_kept, self.mixed = sem(name + "_turned"), sem(name + "_pt_kept"), sem(name + "_mixed")
                self.normed, self.kept, self.low = sem(name + "_normed"), sem(name + "_kept"), sem(name + "_low")

        fa, da, ba = Mixer("fa"), Mixer("da"), Mixer("ba")
        da_scored1, da_maxed1, da_exped1 = sem("da_scored1"), sem("da_maxed1"), sem("da_exped1")
        da_vloaded, da_gloaded, ba_gloaded = sem("da_vloaded"), sem("da_gloaded"), sem("ba_gloaded")
        da_weighed, da_rms, da_gated = sem("da_weighed"), sem("da_rms"), sem("da_gated")
        ba_biased, ba_o_turned = sem("ba_biased"), sem("ba_o_turned")
        da_free = sem2("da_free")

        W0, A0, Z0 = {}, {}, {}
        w_n, a_n, z_n = [0, 0], [0, 0], [0, 0]
        for name, w_uses, a_uses, z_uses in (
            ("gelu", (4, 4), (4, 4), (4, 4)), ("plain", (6, 6), (6, 6), (6, 6)), ("forget", (1, 0), (1, 0), (0, 0)),
            ("w_out", (4, 4), (4, 4), (0, 0)),
            ("ffn", (2 * CHUNKS, 2 * CHUNKS), (6 * CHUNKS, 6 * CHUNKS), (0, 0)),
            ("a_qk", (8, 8), (8, 8), (8, 8)), ("a_v", (4, 4), (4, 4), (4, 4)), ("a_gate", (4, 4), (4, 4), (4, 4)), ("a_out", (4, 4), (4, 4), (0, 0)),
            ("b_q", (4, 4), (4, 4), (4, 4)), ("b_k", (1, 1), (1, 1), (1, 1)), ("b_v", (1, 1), (1, 1), (1, 1)), ("b_gate", (4, 4), (4, 4), (4, 4)),
            ("b_out", (4, 4), (4, 4), (0, 0)),
        ):
            W0[name], A0[name], Z0[name] = tuple(w_n), tuple(a_n), tuple(z_n)
            for s in range(2):
                w_n[s] += w_uses[s]
                a_n[s] += a_uses[s]
                z_n[s] += z_uses[s]
        R0 = {"a_qk": 0, "b_q": 16, "b_k": 24}
        NORMS = {name: n for n, name in enumerate(("mix", "ffn", "fin", "a_x", "a_ctx", "b_x", "b_ctx", "out"))}
        SPLITS = {name: n for n, name in enumerate(("mix", "ffn", "a_x", "a_ctx", "b_x", "b_ctx"))}

        LATENT_SEGS = [(CTX, BANK, 0), (CTX + BANK, BANK, BANK)]
        ALL_SEGS = [(0, BANK, 0), (BANK, BANK, BANK), (2 * BANK, TOK - 2 * BANK, 2 * BANK)]

        block = ctx.enter_context(nc.Block())

        def weight_tiles(sp, name, w, col0, tiles, tables=None):
            view = w.rearrange("(k p) n -> p k n", p=P)

            def tile_pair(i):
                for s in range(2):
                    sp.wait_ge(w_split[s], i + W0[name][s] + 1)
                    sp.dma_start(w_raw[:, s].rearrange("p (k n) -> p k n", k=KT),
                                 view[:, :, bass.ds((2 * i + s) * P + col0, P)]).then_inc(w_landed[s], 16)

            tile_pair(0)
            if tables:
                (free, count), *loads = tables
                for s in range(2):
                    sp.wait_ge(free[s], count)
                for dst, src in loads:
                    sp.dma_start(dst[:], src).then_inc(consts_in, 16)
            if tiles > 2:
                with sp.Fori(1, tiles // 2) as i:
                    tile_pair(i)

        @block.sync
        def _(sp):
            for dst, src in ((ident[:], const_ident), (swap[:], const_swap),
                             (maskrows[:, 0], const_causal), (maskrows[:, 1], const_before),
                             (lamrows[:, 0], a_lambda_q1_2.broadcast_to([P, DH])),
                             (lamrows[:, 1], a_lambda_k1_2.broadcast_to([P, DH])),
                             (lamrows[:, 2], a_lambda_q2_2.broadcast_to([P, DH])),
                             (lamrows[:, 3], a_lambda_k2_2.broadcast_to([P, DH])),
                             (sinks[:], b_sink_2.broadcast_to([P, 16])),
                             (fb[:], f_bias.rearrange("o h -> h o"))):
                sp.dma_start(dst, src).then_inc(consts_in, 16)
            for at, v in ((V_MIX, norm_mix_g), (V_FFN, norm_ffn_g), (V_G2, norm_g_2), (V_BMOD, b_mod_2),
                          (V_SUB, a_subln_g_2), (V_C, c_2)):
                n = v.shape[0] * v.shape[1] // P
                sp.dma_start(rows[at:at + n, :], v.rearrange("o (t p) -> (o t) p", p=P)).then_inc(rows_in, 16)
            for at, v in ((V_FIN, norm_final_g), (V_FG2, final_g_2), (V_C + KT, c_ctx_2)):
                sp.dma_start(rows[at:at + KT, :], v.rearrange("(t p) -> t p", p=P)).then_inc(rows_in, 16)
            sp.dma_start(rows[V_LNG:V_LNG + 4, :],
                         sg_ln_g[0].rearrange("(j e) d -> j (e d)", e=2)).then_inc(rows_in, 16)
            for tap, (slot, at) in enumerate(((0, 0), (0, 44), (1, 0))):
                sp.dma_start(convrows[at:at + 2 * FT, slot, :],
                             w_conv[0, tap].rearrange("(t p) -> t p", p=P)).then_inc(rows_in, 16)
            sp.dma_start(convrows[44:88, 1, :], b_conv[0].rearrange("(t p) -> t p", p=P)).then_inc(rows_in, 16)
            for s in range(2):
                sp.dma_start(tokrows[:, s], ctx_2[0, s * P:(s + 1) * P, :]).then_inc(tok_in[s], 16)
            with sp.Fori(0, QB // 2) as i:
                for s in range(2):
                    sp.wait_ge(tok_turned[s], i + 1)
                    sp.dma_start(tokrows[:, s], x[0, bass.ds((2 * i + s) * P, P), :]).then_inc(tok_in[s], 16)
            for layer in range(2):
                view = w_mod_2[layer].rearrange("(k p) n -> p k n", p=P)
                with sp.Fori(0, 6) as i:
                    for s in range(2):
                        sp.wait_ge(mod_summed[s], i + 6 * layer + 1)
                        sp.dma_start(w_mod_sb[:, s], view[:, :, bass.ds((2 * i + s) * 2 * P, 2 * P)]).then_inc(mod_in[s], 16)
            weight_tiles(sp, "gelu", w_in[0], 0, 8)
            weight_tiles(sp, "plain", w_in[0], 8 * P, 12)
            sp.wait_ge(w_split[0], W0["forget"][0] + 1)
            with nc.allow_non_contiguous_dma(reason="eight columns"):
                sp.dma_start(w_raw[:, 0].rearrange("p (k n) -> p k n", k=KT)[:, :, 0:8],
                             w_in[0].rearrange("(k p) n -> p k n", p=P)[:, :, 20 * P:20 * P + 8]).then_inc(w_landed[0], 16)
            for s in range(2):
                sp.wait_ge(stored[s], 16 * (Z0["plain"][s] + 6) + 16)
            with sp.Fori(0, 4) as j:
                sp.wait_ge(s_low, j + 1)
                sp.dma_start(s_v[:], z1[bass.ds(j * P + 4 * P, P), :]).then_inc(s_in, 16)
                sp.dma_start(s_u[:], z1[bass.ds(j * P, P), :]).then_inc(s_in, 16)
                sp.dma_start(s_w[:], sg_w[0, bass.ds(2 * j, 2)].rearrange("h t s -> t h s")).then_inc(s_in, 16)
                for e in range(2):
                    sp.dma_start(s_b[e * DH:(e + 1) * DH, :],
                                 sg_b[0, bass.ds(2 * j + e, 1), :].broadcast_to([DH, P])).then_inc(s_in, 16)
            sp.wait_ge(f_stored, 32)
            sp.wait_ge(s_low, 4 + 1)
            with sp.Fori(0, 4) as j:
                sp.wait_ge(fa.scored, 16 * j + 1)
                sp.dma_start(a_q[:], z1[bass.ds(j * P + 8 * P, P), :]).then_inc(fa.loaded, 16)
                sp.dma_start(a_k[:], z1[bass.ds(j * P + 12 * P, P), :]).then_inc(fa.loaded, 16)
                for part in range(2):
                    sp.dma_start(a_c[part:part + 1].bitcast(F32), forget_rows[part:part + 1, bass.ds(2 * j, 2), :]).then_inc(fa.loaded, 16)
                sp.dma_start(a_vt[:], z1[bass.ds(j * P + 16 * P, P), :]).then_inc(fa.loaded, 16)
            weight_tiles(sp, "w_out", w_out[0], 0, 8)
            up = w_up[0].rearrange("(k p) n -> p k n", p=P)

            def up_tiles(chunk, e):
                for s in range(2):
                    sp.wait_ge(w_split[s], 2 * chunk + (W0["ffn"][s] + e) + 1)
                    sp.dma_start(w_raw[:, s].rearrange("p (k n) -> p k n", k=KT),
                                 up[:, :, bass.ds((2 * chunk + (s * FT + e)) * P, P)]).then_inc(w_landed[s], 16)

            def down_rows(chunk):
                for s in range(2):
                    sp.wait_ge(d_split[s], chunk + 1)
                    sp.dma_start(d_raw[:, s], w_down[0, bass.ds((2 * chunk + s) * P, P), :]).then_inc(d_landed[s], 16)

            up_tiles(0, 0)
            for s in range(2):
                sp.wait_ge(n_low[s], 4 * (SPLITS["ffn"] + 1) + 1)
            with sp.Fori(0, CHUNKS - 1) as c:
                up_tiles(c, 1)
                down_rows(c)
                up_tiles(c + 1, 0)
            up_tiles(CHUNKS - 1, 1)
            down_rows(CHUNKS - 1)
            weight_tiles(sp, "a_qk", a_w_in_2[0], 0, 16, ((n_low, 4 * (SPLITS["a_ctx"] + 1) + 1), (r_cos, const_cos), (r_sin, const_sin)))
            weight_tiles(sp, "a_v", a_w_in_2[0], 16 * P, 8)
            weight_tiles(sp, "a_gate", a_w_in_2[0], 24 * P, 8)
            for s in range(2):
                sp.wait_ge(stored[s], 16 * (Z0["a_gate"][s] + 4) + 16)
            with sp.Fori(0, DA_HEADS) as h:
                sp.wait_ge(da_scored1, 10 * h + 1)
                sp.dma_start(d_q[:], za[bass.ds(h * P, P), :]).then_inc(da.loaded, 16)
                sp.dma_start(d_k[:], za[bass.ds(h * P + 8 * P, P), :]).then_inc(da.loaded, 16)
                sp.wait_ge(da.mixed, 10 * h + 1)
                sp.dma_start(d_vt, za[bass.ds(h * P + 16 * P, P), :]).then_inc(da_vloaded, 16)
                sp.wait_ge(da.low, h + 1)
                sp.dma_start(d_g, za[bass.ds(h * P + 24 * P, P), :]).then_inc(da_gloaded, 16)
            sp.wait_ge(da.low, DA_HEADS + 1)
            weight_tiles(sp, "a_out", w_o_2[0], 0, 8)
            weight_tiles(sp, "b_q", b_w_in_2[0], 0, 8, ((n_low, 4 * (SPLITS["b_ctx"] + 1) + 1), (r_cos, const_cos), (r_sin, const_sin)))
            weight_tiles(sp, "b_k", b_w_in_2[0], 8 * P, 2)
            weight_tiles(sp, "b_v", b_w_in_2[0], 10 * P, 2)
            weight_tiles(sp, "b_gate", b_w_in_2[0], 12 * P, 8)
            for s in range(2):
                sp.wait_ge(stored[s], 16 * (Z0["b_gate"][s] + 4) + 16)
            with sp.Fori(0, 4) as h:
                sp.wait_ge(ba.scored, 32 * h + 1)
                sp.dma_start(b_q[:], zb[bass.ds(h * 2 * P, 2 * P), X_COLS].rearrange("(t p) n -> p t n", p=P)).then_inc(ba.loaded, 16)
                for e in range(2):
                    sp.dma_start(b_k[e * DH:(e + 1) * DH, :], zb[bass.ds(h * DH + 8 * P, DH), :]).then_inc(ba.loaded, 16)
                    sp.dma_start(b_vt[e * DH:(e + 1) * DH, :],
                                 zb[bass.ds(h * DH + 10 * P, DH), e * TOK // 2:(e + 1) * TOK // 2]).then_inc(ba.loaded, 16)
                sp.wait_ge(ba.low, 8 * h + 1)
                sp.dma_start(b_g[:], zb[bass.ds(h * 2 * P + 12 * P, 2 * P), X_COLS].rearrange("(t p) n -> p t n", p=P)).then_inc(ba_gloaded, 16)
            weight_tiles(sp, "b_out", w_o_2[1], 0, 8)
            rows_of_out = out[0].rearrange("(t p) n -> p t n", p=P)
            with sp.Fori(0, KT // 2) as i:
                for s in range(2):
                    sp.wait_ge(out_kept[s], i + 1 + 1)
                    sp.dma_start(rows_of_out[:, :, bass.ds((2 * i + s) * P, P)], tok_out[:, s]).then_inc(out_stored[s], 16)
            for s in range(2):
                sp.wait_ge(out_stored[s], 16 * (KT // 2) + 16)

        def split(pool, base, use, s):
            pool.wait_ge(w_landed[s], 16 * use + 16 * (base[s] + 1))
            pool.wait_ge(w_used[s], use + base[s] + 1)
            pool.tensor_tensor(wh[:, s], w_raw[:, s], zero[:].broadcast_to([P, KT * P]), ALU.add).then_inc(w_high[s], 1)
            pool.wait_ge(w_high[s], use + (base[s] + 1))
            pool.tensor_tensor(wl[:, s], w_raw[:, s], wh[:, s].bitcast(F32), ALU.subtract).then_inc(w_split[s], 1)

        def split_tiles(pool, name, tiles):
            with pool.Fori(0, tiles // 2) as i:
                for s in range(2):
                    split(pool, W0[name], i, s)

        def norm_rests(pool, name, cols):
            n = 4 * SPLITS[name]
            with pool.Fori(0, KT // 2) as i:
                for s in range(2):
                    pool.wait_ge(n_high[s], i + (n + 1))
                    pool.tensor_tensor(hl[:, bass.ds(2 * i + s, 1), cols], n_h[:, s:s + 1, 0:cols.stop - cols.start],
                                       hh[:, bass.ds(2 * i + s, 1), cols].bitcast(F32), ALU.subtract).then_inc(n_low[s], 1)

        @block.gpsimd
        def _(pool):
            for opened in (*w_split, *w_used, *acc_free, *mod_summed, *mod_kept, *n_added, *n_low, *n_gained, *out_turned, *out_kept,
                           s_low, *d_split, d_used, r_read, r_roped, fa.scored, fa.pt_kept, fa.mixed, fa.normed, fa.kept,
                           da.scored, da_scored1, da.maxed, da_maxed1, da.mixed, da.low, *da_free,
                           ba.scored, ba.pt_kept, ba.mixed, ba.low):
                pool.sem_inc(opened, 1)
            for opened in (*stored, *out_stored):
                pool.sem_inc(opened, 16)
            pool.memset(ones[:], 1.0).then_inc(zeroed, 1)
            pool.memset(zero[:], 0.0).then_inc(zeroed, 1)
            pool.memset(ones_r[:].bitcast(F32), 1.0).then_inc(zeroed, 1)
            pool.memset(one[:], 1.0).then_inc(zeroed, 1)
            pool.memset(eps_d[:], D * EPS).then_inc(zeroed, 1)
            pool.memset(eps_1[:], EPS).then_inc(zeroed, 1)
            pool.memset(s_wt[:], 0.0).then_inc(zeroed, 1)
            pool.wait_ge(zeroed, 2)
            norm_rests(pool, "mix", X_COLS)
            split_tiles(pool, "gelu", 8)
            split_tiles(pool, "plain", 12)
            split(pool, W0["forget"], 0, 0)
            with pool.Fori(0, 4) as j:
                pool.wait_ge(s_gated, 4 * j + 4)
                pool.tensor_tensor(hl[:, bass.ds(j, 1), X_COLS], s_y[:].unsqueeze(1),
                                   hh[:, bass.ds(j, 1), X_COLS].bitcast(F32), ALU.subtract).then_inc(s_low, 1)
            split_tiles(pool, "w_out", 8)
            norm_rests(pool, "ffn", X_COLS)

            def split_up(chunk, e):
                for s in range(2):
                    split(pool, W0["ffn"], 2 * chunk + e, s)

            def split_down(chunk):
                for s in range(2):
                    pool.wait_ge(d_landed[s], 16 * chunk + 16)
                    pool.wait_ge(d_used, chunk + 1)
                    pool.tensor_tensor(d_hi[:, s], d_raw[:, s], zero[:].broadcast_to([P, D]), ALU.add).then_inc(d_high[s], 1)
                    pool.wait_ge(d_high[s], chunk + 1)
                    pool.tensor_tensor(d_lo[:, s], d_raw[:, s], d_hi[:, s].bitcast(F32), ALU.subtract).then_inc(d_split[s], 1)

            def act_rest(chunk, e):
                pool.wait_ge(f_high, 2 * chunk + (e + 1))
                pool.tensor_tensor(f_lo[:, e], f_act[:], f_hi[:, e].bitcast(F32), ALU.subtract).then_inc(f_low, 1)

            split_up(0, 0)
            with pool.Fori(0, CHUNKS - 1) as c:
                split_up(c, 1)
                act_rest(c, 0)
                split_down(c)
                split_up(c + 1, 0)
                act_rest(c, 1)
            split_up(CHUNKS - 1, 1)
            act_rest(CHUNKS - 1, 0)
            split_down(CHUNKS - 1)
            act_rest(CHUNKS - 1, 1)
            norm_rests(pool, "a_x", X_COLS)
            norm_rests(pool, "a_ctx", slice(0, CTX))
            split_tiles(pool, "a_qk", 16)
            split_tiles(pool, "a_v", 8)
            split_tiles(pool, "a_gate", 8)
            with pool.Fori(0, DA_HEADS) as h:
                pool.wait_ge(da_gated, h + 1)
                pool.tensor_tensor(hl[:, bass.ds(h, 1)], d_g.unsqueeze(1), hh[:, bass.ds(h, 1)].bitcast(F32), ALU.subtract).then_inc(da.low, 1)
            split_tiles(pool, "a_out", 8)
            norm_rests(pool, "b_x", X_COLS)
            norm_rests(pool, "b_ctx", slice(0, CTX))
            split_tiles(pool, "b_q", 8)
            split_tiles(pool, "b_k", 2)
            split_tiles(pool, "b_v", 2)
            split_tiles(pool, "b_gate", 8)
            with pool.Fori(0, 4) as h:
                for i in range(QB):
                    cols = slice(CTX + i * P, CTX + (i + 1) * P)
                    pool.wait_ge(ba.kept, 16 * h + (2 * i + 2))
                    pool.tensor_tensor(hl[:, bass.ds(2 * h, 2), cols], b_y[:], hh[:, bass.ds(2 * h, 2), cols].bitcast(F32),
                                       ALU.subtract).then_inc(ba.low, 1)
            split_tiles(pool, "b_out", 8)

        def product(pe, out_, w_hi, w_lo, x_hi, x_lo, start, stop):
            pe.matmul(out_, w_hi, x_hi, start=start, stop=False)
            pe.matmul(out_, w_hi, x_lo, start=False, stop=False)
            return pe.matmul(out_, w_lo, x_hi, start=False, stop=stop)

        def project_tile(pe, name, i, s, segs):
            pe.wait_ge(w_split[s], i + (W0[name][s] + 1) + 1)
            pe.wait_ge(acc_free[s], i + A0[name][s] + 1)
            for k in range(KT):
                wk = slice(k * P, (k + 1) * P)
                for c0, w, p0 in segs:
                    last = product(pe, acc[s][:, p0:p0 + w], wh[:, s, wk], wl[:, s, wk],
                                   hh[:, k, c0:c0 + w], hl[:, k, c0:c0 + w], k == 0, k == KT - 1)
            last.then_inc(w_used[s], 1)

        def project(pe, name, tiles, segs):
            with pe.Fori(0, tiles // 2) as i:
                for s in range(2):
                    project_tile(pe, name, i, s, segs)

        def project_rotated(pe, name, tiles, segs):
            def swap_tile(i, s):
                pe.wait_ge(acc_free[s], i + A0[name][s] + 1 + 1)
                pe.wait_ge(r_read, 2 * i + (R0[name] + s) + 1)
                first = segs[-1][2] + segs[-1][1] - SEQ
                for c in range(0, SEQ, BANK):
                    last = pe.matmul(ps[:, 6 * BANK + c:7 * BANK + c], swap[:], z_out[:, s, first + c:first + c + BANK], start=True, stop=True)
                last.then_inc(r_swapped, 1)

            project_tile(pe, name, 0, 0, segs)
            project_tile(pe, name, 0, 1, segs)
            swap_tile(0, 0)
            if tiles > 2:
                with pe.Fori(1, tiles // 2) as i:
                    project_tile(pe, name, i, 0, segs)
                    swap_tile(i - 1, 1)
                    project_tile(pe, name, i, 1, segs)
                    swap_tile(i, 0)
            swap_tile(tiles // 2 - 1, 1)

        def wait_split_norm(pe, *names):
            for name in names:
                for s in range(2):
                    pe.wait_ge(n_low[s], 4 * (SPLITS[name] + 1) + 1)

        def norm_sum(pe, name, width):
            n = NORMS[name]
            for s in range(2):
                pe.wait_ge(n_added[s], 4 * (n + 1) + 1)
            for c in range(0, width, BANK):
                w = min(BANK, width - c)
                last = pe.matmul(ps[:, 6 * BANK + c:6 * BANK + c + w], ones[:], n_sum[:, c:c + w], start=True, stop=True)
            last.then_inc(n_summed, 1)

        @block.tensor
        def _(pe):
            pe.wait_ge(consts_in, 16 * 10)

            def turn_tokens(s, use):
                pe.wait_ge(tok_in[s], 16 * use + 16)
                pe.wait_ge(tok_kept[s], use)
                for k in range(KT):
                    last = pe.transpose(acc[s][:, k * P:(k + 1) * P], tokrows[:, s, k * P:(k + 1) * P], ident[:])
                last.then_inc(tok_turned[s], 1)

            for s in range(2):
                turn_tokens(s, 0)
            with pe.Fori(0, QB // 2) as i:
                for s in range(2):
                    turn_tokens(s, i + 1)
            pe.wait_ge(rows_in, 16 * 14)
            pe.transpose(bank(6)[:, 0:V_END], rows[0:V_END, :], ident[0:V_END, 0:V_END])
            for n in range(2):
                last = pe.transpose(bank(7)[:, n * 88:(n + 1) * 88], convrows[:, n, :], ident[0:88, 0:88])
            last.then_inc(rows_turned, 1)
            pe.wait_ge(cond_ready, 2)
            for layer in range(2):
                with pe.Fori(0, 6) as i:
                    for s in range(2):
                        pe.wait_ge(mod_in[s], 16 * i + 16 * (6 * layer + 1))
                        pe.wait_ge(mod_kept[s], 2 * i + 12 * layer + 1)
                        for n in range(2):
                            for k in range(KT):
                                last = pe.matmul(acc[s][:, 2 * n:2 * n + 2], w_mod_sb[:, s, k, n * P:(n + 1) * P],
                                                 cond[:, k, :], start=(k == 0), stop=(k == KT - 1))
                        last.then_inc(mod_summed[s], 1)
            norm_sum(pe, "mix", SEQ)
            wait_split_norm(pe, "mix")
            project(pe, "gelu", 8, LATENT_SEGS)
            project(pe, "plain", 12, LATENT_SEGS)
            project_tile(pe, "forget", 0, 0, LATENT_SEGS)
            for s in range(2):
                pe.wait_ge(acc_free[s], A0["w_out"][s] + 1)
            with pe.Fori(0, 4) as j:
                pe.wait_ge(s_in, 80 * j + 80)
                for n in range(QB):
                    pe.transpose(ps[:, n * P:(n + 1) * P], s_v[:, n * P:(n + 1) * P], ident[:])
                for e in range(2):
                    last = pe.transpose(bank(2)[:, e * P:(e + 1) * P], s_w[:, e], ident[:])
                last.then_inc(s_turned, 1)
                pe.wait_ge(s_wt_ready, 2 * j + 2)
                pe.wait_ge(s_stats, 6 * j + 6)
                for n in range(QB):
                    last = pe.matmul(ps[:, 4 * BANK + n * 2 * P:4 * BANK + (n + 1) * 2 * P],
                                     s_ctr[:].rearrange("p (n e) d -> p n (e d)", e=2)[:, n],
                                     s_wt[:].rearrange("p e t -> p (e t)"), start=True, stop=True)
                last.then_inc(s_mixed, 1)
            pe.wait_ge(masks_ready, 3)
            pe.wait_ge(s_low, 4 + 1)
            with pe.Fori(0, 4) as j:
                pe.wait_ge(fa.loaded, 80 * j + 80)

                def fa_scores(u):
                    a, i = divmod(u, QB)
                    h, at, width = slice(a * DH, (a + 1) * DH), 2 * (u % 2) * BANK, (i + 1) * P
                    if u >= 2:
                        pe.wait_ge(fa.maxed, 16 * j + (u - 1))
                    for c in range(0, width, BANK):
                        w = min(BANK, width - c)
                        got = ps[:, at + c:at + c + w]
                        pe.matmul(got, a_q[h, i * P:(i + 1) * P], a_k[h, c:c + w], start=True, stop=False)
                        last = pe.matmul(got, ones_r[:], a_c[:, a, c:c + w], start=False, stop=(c + w < width))
                    last = pe.matmul(ps[:, at + i * P:at + width], masks[:, 0], masks[:, 1], start=False, stop=True)
                    last.then_inc(fa.scored, 1)

                def fa_mix(u):
                    a, i = divmod(u, QB)
                    pe.wait_ge(fa.pt_kept, 17 * j + (u + 2) + 1)
                    if u == 0:
                        pe.wait_ge(fa.normed, 2 * j + 1)
                    got = ps[:, 6 * BANK + i * P + a * DH:6 * BANK + i * P + (a + 1) * DH]
                    for kt in range(i + 1):
                        last = pe.matmul(got, a_pt[:, u % 2, kt], a_v[:, kt, a * DH:(a + 1) * DH], start=(kt == 0), stop=(kt == i))
                    last.then_inc(fa.mixed, 1)

                for u in range(LEAD):
                    fa_scores(u)
                pe.wait_ge(fa.pt_kept, 17 * j + 1)
                pe.wait_ge(fa.kept, 2 * j + 1)
                for n in range(QB):
                    last = pe.transpose(ps[:, 4 * BANK + n * P:4 * BANK + (n + 1) * P], a_vt[:, n * P:(n + 1) * P], ident[:])
                last.then_inc(fa.turned, 1)
                for u in range(2 * QB):
                    if u + LEAD < 2 * QB:
                        fa_scores(u + LEAD)
                    pe.wait_ge(fa.exped, 16 * j + (u + 1))
                    pe.wait_ge(fa.pt_kept, 17 * j + (u + 1) + 1)
                    for kt in range(u % QB + 1):
                        last = pe.transpose(ps[:, 4 * BANK + kt * P:4 * BANK + (kt + 1) * P],
                                            a_s[:, u % 3, kt * P:(kt + 1) * P], ident[:])
                    last.then_inc(fa.turned, 1)
                    if u:
                        fa_mix(u - 1)
                fa_mix(2 * QB - 1)
                pe.wait_ge(fa.normed, 2 * j + 2 + 1)
                for i in range(QB):
                    last = pe.transpose(ps[:, 4 * BANK + i * P:4 * BANK + (i + 1) * P],
                                        a_o[:, i].rearrange("p a d -> p (a d)"), ident[:])
                last.then_inc(fa.turned, 1)
            pe.wait_ge(fa.kept, 8 + 1)
            project(pe, "w_out", 8, LATENT_SEGS)
            norm_sum(pe, "ffn", SEQ)
            wait_split_norm(pe, "ffn")

            def ffn_up(chunk, e, acc_use):
                for s in range(2):
                    pe.wait_ge(w_split[s], 2 * chunk + (W0["ffn"][s] + e + 1) + 1)
                    pe.wait_ge(acc_free[s], acc_use + A0["ffn"][s] + 1)
                    for k in range(KT):
                        wk = slice(k * P, (k + 1) * P)
                        for c0, w, p0 in LATENT_SEGS:
                            last = product(pe, acc[s][:, p0:p0 + w], wh[:, s, wk], wl[:, s, wk],
                                           hh[:, k, c0:c0 + w], hl[:, k, c0:c0 + w], k == 0, k == KT - 1)
                    last.then_inc(w_used[s], 1)

            def ffn_down(chunk, acc_use):
                pe.wait_ge(f_low, 2 * chunk + 2)
                for s in range(2):
                    pe.wait_ge(d_split[s], chunk + 1 + 1)
                for m in range(KT):
                    s, wm = m % 2, slice(m * P, (m + 1) * P)
                    pe.wait_ge(acc_free[s], acc_use + (A0["ffn"][s] + m // 2) + 1)
                    for e in range(2):
                        for c in range(0, SEQ, BANK):
                            last = product(pe, acc[s][:, c:c + BANK], d_hi[:, e, wm], d_lo[:, e, wm],
                                           f_hi[:, e, c:c + BANK], f_lo[:, e, c:c + BANK], e == 0, e == 1)
                    last.then_inc(f_down if m < KT - 1 else d_used, 1)

            ffn_up(0, 0, 0)
            ffn_up(0, 1, 1)
            with pe.Fori(1, CHUNKS) as c:
                ffn_up(c, 0, 6 * c - 4)
                ffn_down(c - 1, 6 * c - 3)
                ffn_up(c, 1, 6 * c + 1)
            ffn_down(CHUNKS - 1, 6 * CHUNKS - 4)
            norm_sum(pe, "fin", SEQ)
            norm_sum(pe, "a_x", SEQ)
            norm_sum(pe, "a_ctx", CTX)
            wait_split_norm(pe, "a_x", "a_ctx")
            project_rotated(pe, "a_qk", 16, ALL_SEGS)
            project(pe, "a_v", 8, ALL_SEGS)
            project(pe, "a_gate", 8, ALL_SEGS)
            for s in range(2):
                pe.wait_ge(acc_free[s], A0["a_out"][s] + 1)
            def da_turn_tiles(h, src, blocks, *key):
                b, before, _ = da_turn(h, *key)
                pe.wait_ge(da_free[b], before + 1)
                for n, kt in enumerate(blocks):
                    last = pe.transpose(bank(6 + b)[:, n * P:(n + 1) * P], src(kt), ident[:])
                last.then_inc(da.turned, 1)

            def da_scores(h, u, m):
                done, read = ((da.scored, da.maxed), (da_scored1, da_maxed1))[m]
                pe.wait_ge(read, 10 * h + u + 1)
                r, width = slice(m * DH, (m + 1) * DH), da_tiles(u) * P
                for c in range(0, width, BANK):
                    w = min(BANK, width - c)
                    last = pe.matmul(acc[m][:, c:c + w], d_q[r, u * P:(u + 1) * P], d_k[r, c:c + w], start=True, stop=True)
                last.then_inc(done, 1)

            def da_mix(h, u):
                nk = da_tiles(u)
                for n in range(len(batches(nk)))[-2:]:
                    b, before, _ = da_turn(h, "p", u, n)
                    pe.wait_ge(da_free[b], before + 1 + 1)
                b, before, _ = da_turn(h, "m", u)
                pe.wait_ge(da_free[b], before + 1)
                for kt in range(nk):
                    last = pe.matmul(bank(6 + b)[:, 0:P], d_pt[:, u % 2, kt, :], d_v[:, kt, :], start=(kt == 0), stop=(kt == nk - 1))
                last.then_inc(da.mixed, 1)

            def da_turn_output(h):
                pe.wait_ge(da.normed, 4 * h)
                for n, blocks in enumerate(batches(TOK // P)):
                    da_turn_tiles(h, lambda u: d_o[:, u], blocks, "o", n)

            def da_head(h, first):
                pe.wait_ge(da.loaded, 32 * h + 32)
                for u in range(LEAD):
                    for m in range(2):
                        da_scores(h, u, m)
                pe.wait_ge(da_vloaded, 16 * h + 16)
                for n, blocks in enumerate(batches(TOK // P)):
                    da_turn_tiles(h, lambda kt: d_vt[:, kt * P:(kt + 1) * P], blocks, "v", n)
                for u in range(TOK // P):
                    ahead = [m for m in range(2) if u + LEAD < TOK // P]
                    if ahead:
                        da_scores(h, u + LEAD, ahead.pop(0))
                    pe.wait_ge(da_weighed, 30 * h + (3 * u + 3))
                    for n, blocks in enumerate(batches(da_tiles(u))):
                        if n == 2:
                            da_mix(h, u - 1)
                        da_turn_tiles(h, lambda kt: d_p0[:, u % 3, kt * P:(kt + 1) * P], blocks, "p", u, n)
                        if ahead:
                            da_scores(h, u + LEAD, ahead.pop(0))
                    if u == 1 and not first:
                        da_turn_output(h)
                    if u == 1:
                        da_mix(h, 0)
                da_mix(h, TOK // P - 1)

            da_head(0, True)
            with pe.Fori(1, DA_HEADS) as h:
                da_head(h, False)
            da_turn_output(DA_HEADS)
            pe.wait_ge(da.low, DA_HEADS + 1)
            project(pe, "a_out", 8, ALL_SEGS)
            norm_sum(pe, "b_x", SEQ)
            norm_sum(pe, "b_ctx", CTX)
            wait_split_norm(pe, "b_x", "b_ctx")
            project_rotated(pe, "b_q", 8, LATENT_SEGS)
            project_rotated(pe, "b_k", 2, ALL_SEGS)
            project(pe, "b_v", 2, ALL_SEGS)
            project(pe, "b_gate", 8, LATENT_SEGS)
            for s in range(2):
                pe.wait_ge(acc_free[s], A0["b_out"][s] + 1)
            with pe.Fori(0, 4) as h:
                def ba_scores(u):
                    i, a = divmod(u, 4)
                    r, t, at = slice((a % 2) * DH, (a % 2 + 1) * DH), a // 2, 2 * (u % 2) * BANK
                    if u >= 2:
                        pe.wait_ge(ba.maxed, 32 * h + (u - 1))
                    for n, kt in enumerate(window_tiles(i)):
                        if kt == 1:
                            continue
                        w, side = CTX if kt == 0 else P, kt - (2 + i) if kt else 0
                        got = ps[:, at + n * P:at + n * P + w]
                        last = pe.matmul(got, b_q[r, t, i * P:(i + 1) * P], b_k[r, kt * P:kt * P + w], start=True, stop=(side == 0))
                        if side:
                            last = pe.matmul(got, masks[:, 0], masks[:, 2 if side < 0 else 1], start=False, stop=True)
                    last.then_inc(ba.scored, 1)

                def ba_mix(u):
                    i, a = divmod(u, 4)
                    tiles = window_tiles(i)
                    pe.wait_ge(ba.pt_kept, 33 * h + (u + 2) + 1)
                    for n, kt in enumerate(tiles):
                        last = pe.matmul(bank(6 + i % 2)[:, a * DH:(a + 1) * DH], b_pt[:, u % 2, n, :], b_v[:, kt % 5, kt // 5, :],
                                         start=(n == 0), stop=(n == len(tiles) - 1))
                    last.then_inc(ba.mixed, 1)

                def ba_turn_output(i):
                    pe.wait_ge(ba.normed, 24 * h + (3 * i + 3))
                    for t in range(2):
                        last = pe.transpose(bank(6 + i % 2)[:, (2 + t) * P:(3 + t) * P], b_o[:, t * P:(t + 1) * P], ident[:])
                    last.then_inc(ba_o_turned, 1)

                pe.wait_ge(ba.loaded, 80 * h + 80)
                for u in range(LEAD):
                    ba_scores(u)
                pe.wait_ge(ba.pt_kept, 33 * h + 1)
                for n in range(TOK // 2 // P):
                    last = pe.transpose(ps[:, 4 * BANK + n * P:4 * BANK + (n + 1) * P], b_vt[:, n * P:(n + 1) * P], ident[:])
                last.then_inc(ba.turned, 1)
                for u in range(4 * QB):
                    i, a = divmod(u, 4)
                    if u + LEAD < 4 * QB:
                        ba_scores(u + LEAD)
                    pe.wait_ge(ba.exped, 64 * h + (2 * u + 1))
                    pe.wait_ge(ba.pt_kept, 33 * h + (u + 1) + 1)
                    for n in range(len(window_tiles(i))):
                        last = pe.transpose(ps[:, 4 * BANK + n * P:4 * BANK + (n + 1) * P], b_s[:, u % 3, n * P:(n + 1) * P], ident[:])
                    last.then_inc(ba.turned, 1)
                    if i and a == 1:
                        ba_turn_output(i - 1)
                    if u:
                        ba_mix(u - 1)
                ba_mix(4 * QB - 1)
                ba_turn_output(QB - 1)
            pe.wait_ge(ba.low, 32 + 1)
            project(pe, "b_out", 8, LATENT_SEGS)
            norm_sum(pe, "out", SEQ)
            with pe.Fori(0, KT // 2) as i:
                for s in range(2):
                    pe.wait_ge(n_gained[s], i + 4 * NORMS["out"] + 1 + 1)
                    pe.wait_ge(out_kept[s], i + 1)
                    for t in range(QB):
                        last = pe.transpose(acc[s][:, t * P:(t + 1) * P], n_h[:, s, t * P:(t + 1) * P], ident[:])
                    last.then_inc(out_turned[s], 1)

        def norm_root(act, name, cols):
            n, w = NORMS[name], cols.stop - cols.start
            with act.Fori(0, KT // 2) as i:
                for s in range(2):
                    act.wait_ge(n_added[s], i + 4 * n + 1)
                    act.activation(n_sq[:, s:s + 1, 0:w], res[:, bass.ds(2 * i + s, 1), cols], ACT.Square).then_inc(n_squared[s], 1)
            act.wait_ge(n_summed, n + 1)
            act.activation(n_rs[:, 0:w], ps[:, 6 * BANK:6 * BANK + w], ACT.Sqrt, bias=eps_d[:]).then_inc(n_root, 1)

        def norm_gain(act, name, cols, gain, shift):
            n, w = NORMS[name], cols.stop - cols.start
            with act.Fori(0, KT // 2) as i:
                for s in range(2):
                    k = 2 * i + s
                    act.wait_ge(n_times[s], i + (4 * n + 1))
                    to = n_h[:, s:s + 1, 0:w]
                    if name in SPLITS:
                        act.wait_ge(n_low[s], i + 4 * SPLITS[name] + 1)
                    elif name == "out":
                        act.wait_ge(out_turned[s], i + 1)
                    else:
                        to = res[:, bass.ds(k, 1), cols]
                    act.activation(to, n_t[:, s:s + 1, 0:w], ACT.Identity, bias=shift(k), scale=gain(k)).then_inc(n_gained[s], 1)

        def keep(act, name, rows, row0, tiles, cols, func):
            w = cols.stop - cols.start
            with act.Fori(0, tiles // 2) as i:
                for s in range(2):
                    act.wait_ge(w_used[s], i + (W0[name][s] + 1) + 1)
                    act.wait_ge(stored[s], 16 * i + 16 * Z0[name][s] + 16)
                    act.activation(z_out[:, s, 0:w], acc[s][:, 0:w], func).then_inc(acc_free[s], 1)
                    act.wait_ge(acc_free[s], i + (A0[name][s] + 1) + 1)
                    act.dma_start(rows[bass.ds((2 * i + s) * P + row0, P), cols], z_out[:, s, 0:w]).then_inc(stored[s], 16)

        def keep_rotated(act, name, rows, row0, tiles, cols):
            w = cols.stop - cols.start

            def copy(i, s):
                act.wait_ge(w_used[s], i + (W0[name][s] + 1) + 1)
                act.wait_ge(stored[s], 16 * i + 16 * Z0[name][s] + 16)
                act.activation(z_out[:, s, 0:w], acc[s][:, 0:w], ACT.Copy).then_inc(acc_free[s], 1)

            def store(i, s):
                act.wait_ge(r_roped, 2 * i + (R0[name] + s + 1) + 1)
                act.dma_start(rows[bass.ds((2 * i + s) * P + row0, P), cols], z_out[:, s, 0:w]).then_inc(stored[s], 16)

            copy(0, 0)
            copy(0, 1)
            store(0, 0)
            if tiles > 2:
                with act.Fori(1, tiles // 2) as i:
                    copy(i, 0)
                    store(i - 1, 1)
                    copy(i, 1)
                    store(i, 0)
            store(tiles // 2 - 1, 1)

        def vec_gain(at):
            return lambda k: vec32[:, bass.ds(k + at, 1)]

        def no_shift(k):
            return zero[:]

        def mod_gain(layer, v):
            return lambda k: modg[:, layer, v, bass.ds(k, 1)]

        def mod_shift(layer, v):
            return lambda k: mod[:, bass.ds(k + 24 * layer, 1), v]

        @block.scalar
        def _(act):
            act.wait_ge(zeroed, 7)
            act.wait_ge(vec_ready, 2)
            for v in range(2):
                act.activation(cond[:, :, v], vec[:, V_C + v * KT:V_C + (v + 1) * KT], ACT.Silu).then_inc(cond_ready, 1)
            act.wait_ge(lam_step, 2)
            act.activation(lamt[:, 2:4], lamt[:, 0:2], ACT.Exp).then_inc(lam_exp, 1)
            act.wait_ge(modg_ready, 4)
            norm_root(act, "mix", X_COLS)
            norm_gain(act, "mix", X_COLS, vec_gain(V_MIX), no_shift)
            for s in range(2):
                act.wait_ge(n_low[s], 4 * (SPLITS["mix"] + 1) + 1)
            keep(act, "gelu", z1, 0, 8, slice(0, SEQ), ACT.Gelu)
            keep(act, "plain", z1, 8 * P, 12, slice(0, SEQ), ACT.Copy)
            act.wait_ge(w_used[0], W0["forget"][0] + 1 + 1)
            act.activation(f_x[:], acc[0][0:8, 0:SEQ], ACT.Identity, bias=fb[:]).then_inc(acc_free[0], 1)
            act.wait_ge(acc_free[0], A0["forget"][0] + 1 + 1)
            act.activation(f_a[:], f_x[:], ACT.Abs).then_inc(f_soft, 1)
            act.wait_ge(f_soft, 1)
            act.activation(f_a[:], f_a[:], ACT.Exp, scale=-1.0).then_inc(f_soft, 1)
            act.wait_ge(f_soft, 2)
            act.activation(f_a[:], f_a[:], ACT.Ln, bias=one[0:8, :]).then_inc(f_soft, 1)
            act.wait_ge(f_scan, 24)
            for part in range(2):
                act.dma_start(forget_rows[part], f_parts[:, part].bitcast(F32)).then_inc(f_stored, 16)
            with act.Fori(0, 4) as j:
                act.wait_ge(s_turned, j + 1)
                turned = bank(2)[:, 0:2 * P].rearrange("p (e t) -> p e t", e=2)
                act.activation(s_wt[0:64, :, :], turned[0:64], ACT.Copy).then_inc(s_wt_ready, 1)
                act.activation(s_wt[64:P, :, 64:P], turned[64:P, :, 64:P], ACT.Copy).then_inc(s_wt_ready, 1)
                act.wait_ge(s_stats, 6 * j + 3)
                act.activation(s_sq[:], s_ctr[:], ACT.Square).then_inc(s_squared, 1)
                act.wait_ge(s_stats, 6 * j + 4)
                act.activation(s_stat[:, 3], s_stat[:, 2], ACT.Sqrt, bias=eps_1[:], scale=1.0 / DH).then_inc(s_std, 1)
            with act.Fori(0, 4) as j:
                def fa_exp(u):
                    a, i = divmod(u, QB)
                    s, w = u % 3, (i + 1) * P
                    act.wait_ge(fa.maxed, 16 * j + (u + 1))
                    act.activation(a_s[:, s, 0:w], a_s[:, s, 0:w], ACT.Exp, bias=a_low[:, s:s + 1], scale=-1.0,
                                   accum_out=a_sum[:, a, i:i + 1]).then_inc(fa.exped, 1)

                for u in range(LEAD):
                    fa_exp(u)
                act.wait_ge(fa.turned, 18 * j + 1)
                act.wait_ge(fa.mixed, 16 * j + 1)
                act.activation(a_v[:].rearrange("p k d -> p (k d)"), bank(4, 2), ACT.Copy).then_inc(fa.pt_kept, 1)
                for u in range(2 * QB):
                    i = u % QB
                    act.wait_ge(fa.turned, 18 * j + (u + 2))
                    if u >= 2:
                        act.wait_ge(fa.mixed, 16 * j + (u - 1) + 1)
                    act.activation(a_pt[:, u % 2, 0:i + 1, :],
                                   ps[:, 4 * BANK:4 * BANK + (i + 1) * P].rearrange("p (k q) -> p k q", q=P),
                                   ACT.Copy).then_inc(fa.pt_kept, 1)
                    if u + LEAD < 2 * QB:
                        fa_exp(u + LEAD)
            for s in range(2):
                act.wait_ge(acc_free[s], A0["ffn"][s] + 1)
            norm_root(act, "ffn", X_COLS)
            norm_gain(act, "ffn", X_COLS, vec_gain(V_FFN), no_shift)
            for s in range(2):
                act.wait_ge(n_low[s], 4 * (SPLITS["ffn"] + 1) + 1)

            def ffn_up(chunk, e, acc_use):
                for s in range(2):
                    tile = 2 * chunk + (s * FT + e)
                    act.wait_ge(w_used[s], 2 * chunk + (W0["ffn"][s] + e + 1) + 1)
                    act.wait_ge(f_mult, 2 * chunk + e)
                    act.activation(f_y[:, s], acc[s][:, 0:SEQ], ACT.Identity, bias=convv[:, bass.ds(tile + 6 * FT, 1)],
                                   scale=convv[:, bass.ds(tile + 4 * FT, 1)]).then_inc(f_based[s], 1)
                act.wait_ge(acc_free[0], acc_use + (A0["ffn"][0] + 1) + 1)
                act.activation(f_g[:], f_y[:, 0], ACT.Silu).then_inc(f_gate, 1)

            ffn_up(0, 0, 0)
            ffn_up(0, 1, 1)
            with act.Fori(1, CHUNKS) as c:
                ffn_up(c, 0, 6 * c - 4)
                ffn_up(c, 1, 6 * c + 1)
            for s in range(2):
                act.wait_ge(acc_free[s], A0["a_qk"][s] + 1)
            norm_root(act, "fin", X_COLS)
            norm_gain(act, "fin", X_COLS, vec_gain(V_FIN), no_shift)
            for s in range(2):
                act.wait_ge(n_gained[s], 4 * (NORMS["fin"] + 1) + 1)
            for name, cols, v in (("a_x", X_COLS, 0), ("a_ctx", slice(0, CTX), 1)):
                norm_root(act, name, cols)
                norm_gain(act, name, cols, mod_gain(0, v), mod_shift(0, v))
            for s in range(2):
                act.wait_ge(n_low[s], 4 * (SPLITS["a_ctx"] + 1) + 1)
            keep_rotated(act, "a_qk", za, 0, 16, slice(0, TOK))
            keep(act, "a_v", za, 16 * P, 8, slice(0, TOK), ACT.Copy)
            keep(act, "a_gate", za, 24 * P, 8, slice(0, TOK), ACT.Silu)
            def da_exp(h, u):
                w, s = da_tiles(u) * P, u % 3
                for m, (p, at, maxed, done) in enumerate(((d_p0, s, da.maxed, da.exped), (d_p1, u % 2, da_maxed1, da_exped1))):
                    act.wait_ge(maxed, 10 * h + (u + 1) + 1)
                    act.activation(p[:, at, 0:w], p[:, at, 0:w], ACT.Exp, bias=d_low[:, s, m:m + 1], scale=-1.0,
                                   accum_out=d_sum[:, m, u:u + 1]).then_inc(done, 1)

            def da_keep_out(h, u, first):
                act.wait_ge(da.mixed, 10 * h + (u + 1) + 1)
                if u == 0 and not first:
                    act.wait_ge(da.turned, da_turn(h, "o", len(batches(TOK // P)) - 1)[2])
                b, _, _ = da_turn(h, "m", u)
                act.activation(d_o[:, u], bank(6 + b)[:, 0:P], ACT.Copy).then_inc(da.kept, 1)
                act.wait_ge(da.kept, 10 * h + (u + 1))
                act.activation(d_sq[:], d_o[:, u], ACT.Square, accum_out=d_ss[:, u:u + 1]).then_inc(da_free[b], 1)

            def da_root(h):
                act.wait_ge(da.normed, 4 * h - 2)
                act.activation(d_rs[:], d_rs[:], ACT.Sqrt).then_inc(da_rms, 1)

            def da_head(h, first):
                for u in range(LEAD):
                    da_exp(h, u)
                if not first:
                    da_root(h)
                act.wait_ge(da.mixed, 10 * h + 1)
                for n, blocks in enumerate(batches(TOK // P)):
                    b, _, turned = da_turn(h, "v", n)
                    act.wait_ge(da.turned, turned)
                    act.activation(d_v[:, blocks.start:blocks.stop, :],
                                   bank(6 + b)[:, 0:len(blocks) * P].rearrange("p (k d) -> p k d", d=P), ACT.Copy).then_inc(da_free[b], 1)
                for u in range(TOK // P):
                    if u >= 2:
                        act.wait_ge(da.mixed, 10 * h + (u - 1) + 1)
                    for n, blocks in enumerate(batches(da_tiles(u))):
                        if n == 2:
                            da_keep_out(h, u - 1, first)
                        b, _, turned = da_turn(h, "p", u, n)
                        act.wait_ge(da.turned, turned)
                        act.activation(d_pt[:, u % 2, blocks.start:blocks.stop, :],
                                       bank(6 + b)[:, 0:len(blocks) * P].rearrange("p (k q) -> p k q", q=P),
                                       ACT.Copy).then_inc(da_free[b], 1)
                    if u == 1:
                        da_keep_out(h, 0, first)
                    if u + LEAD < TOK // P:
                        da_exp(h, u + LEAD)
                da_keep_out(h, TOK // P - 1, first)

            da_head(0, True)
            with act.Fori(1, DA_HEADS) as h:
                da_head(h, False)
            da_root(DA_HEADS)
            for s in range(2):
                act.wait_ge(acc_free[s], A0["b_q"][s] + 1)
            for name, cols, v in (("b_x", X_COLS, 0), ("b_ctx", slice(0, CTX), 1)):
                norm_root(act, name, cols)
                norm_gain(act, name, cols, mod_gain(1, v), mod_shift(1, v))
            for s in range(2):
                act.wait_ge(n_low[s], 4 * (SPLITS["b_ctx"] + 1) + 1)
            keep_rotated(act, "b_q", zb[:, X_COLS], 0, 8, slice(0, SEQ))
            keep_rotated(act, "b_k", zb, 8 * P, 2, slice(0, TOK))
            keep(act, "b_v", zb, 10 * P, 2, slice(0, TOK), ACT.Copy)
            keep(act, "b_gate", zb[:, X_COLS], 12 * P, 8, slice(0, SEQ), ACT.Silu)
            with act.Fori(0, 4) as h:
                def ba_exp(u):
                    i, a = divmod(u, 4)
                    s, w = u % 3, len(window_tiles(i)) * P
                    act.wait_ge(ba_biased, 32 * h + (u + 1))
                    act.activation(b_s[:, s, 0:w], b_s[:, s, 0:w], ACT.Exp, bias=b_low[:, 1, s:s + 1], scale=-1.0,
                                   accum_out=b_sum[:, i % 2, a:a + 1]).then_inc(ba.exped, 1)
                    act.activation(b_sink[:, i % 2, a:a + 1], sinks[:, bass.ds(4 * h + a, 1)], ACT.Exp,
                                   bias=b_low[:, 1, s:s + 1]).then_inc(ba.exped, 1)

                for u in range(LEAD):
                    ba_exp(u)
                act.wait_ge(ba.turned, 33 * h + 1)
                act.wait_ge(ba.mixed, 32 * h + 1)
                act.activation(b_v[:].rearrange("p n e d -> p (n e d)"), ps[:, 4 * BANK:4 * BANK + TOK // 2], ACT.Copy).then_inc(ba.pt_kept, 1)
                for u in range(4 * QB):
                    nk = len(window_tiles(u // 4))
                    act.wait_ge(ba.turned, 33 * h + (u + 2))
                    if u >= 2:
                        act.wait_ge(ba.mixed, 32 * h + (u - 1) + 1)
                    act.activation(b_pt[:, u % 2, 0:nk, :],
                                   ps[:, 4 * BANK:4 * BANK + nk * P].rearrange("p (k q) -> p k q", q=P),
                                   ACT.Copy).then_inc(ba.pt_kept, 1)
                    if u + LEAD < 4 * QB:
                        ba_exp(u + LEAD)
            for s in range(2):
                act.wait_ge(acc_free[s], A0["b_out"][s] + 4 + 1)
            norm_root(act, "out", X_COLS)
            norm_gain(act, "out", X_COLS, vec_gain(V_FG2), no_shift)

        def norm_scale(dve, name, cols):
            n, w = NORMS[name], cols.stop - cols.start
            dve.memset(n_sum[:, 0:w], 0.0).then_inc(n_zeroed, 1)
            dve.wait_ge(n_zeroed, n + 1)
            with dve.Fori(0, KT // 2) as i:
                for s in range(2):
                    dve.wait_ge(n_squared[s], i + (4 * n + 1))
                    dve.wait_ge(n_added[1 - s], i + (4 * n + s) + 1)
                    dve.tensor_tensor(n_sum[:, 0:w], n_sum[:, 0:w], n_sq[:, s, 0:w], ALU.add).then_inc(n_added[s], 1)
            dve.wait_ge(n_root, n + 1)
            dve.reciprocal(n_rs[:, 0:w], n_rs[:, 0:w]).then_inc(n_scaled, 1)
            dve.wait_ge(n_scaled, n + 1)
            with dve.Fori(0, KT // 2) as i:
                for s in range(2):
                    dve.wait_ge(n_gained[s], i + 4 * n + 1)
                    dve.tensor_tensor(n_t[:, s:s + 1, 0:w], res[:, bass.ds(2 * i + s, 1), cols], n_rs[:, 0:w].unsqueeze(1),
                                      ALU.mult).then_inc(n_times[s], 1)
                if name in SPLITS:
                    for s in range(2):
                        dve.wait_ge(n_gained[s], i + (4 * n + 1) + 1)
                        dve.tensor_copy(hh[:, bass.ds(2 * i + s, 1), cols], n_h[:, s:s + 1, 0:w]).then_inc(n_high[s], 1)
                elif name == "out":
                    for s in range(2):
                        dve.wait_ge(out_turned[s], i + 1 + 1)
                        dve.wait_ge(out_stored[s], 16 * i + 16)
                        dve.tensor_copy(tok_out[:, s], acc[s][:, 0:SEQ].rearrange("p (t n) -> p t n", n=P)).then_inc(out_kept[s], 1)

        def add_to_residual(dve, name, parts):
            with dve.Fori(0, KT // 2) as i:
                for s in range(2):
                    dve.wait_ge(w_used[s], i + (W0[name][s] + 1) + 1)
                    for n, (cols, p0, gate) in enumerate(parts):
                        at = res[:, bass.ds(2 * i + s, 1), cols]
                        got = acc[s][:, p0:p0 + cols.stop - cols.start].unsqueeze(1)
                        if gate is None:
                            ins = dve.tensor_tensor(at, got, at, ALU.add)
                        else:
                            layer, v = gate
                            ins = dve.scalar_tensor_tensor(at, got, mod[:, bass.ds(2 * i + (s + 24 * layer + 16), 1), v], at,
                                                           ALU.mult, ALU.add)
                        if n == len(parts) - 1:
                            ins.then_inc(acc_free[s], 1)

        def rotate(dve, name, tiles, first):
            cols = slice(first, first + SEQ)
            with dve.Fori(0, tiles // 2) as i:
                for s in range(2):
                    n = 2 * i + (R0[name] + s)
                    dve.wait_ge(r_swapped, n + 1)
                    dve.wait_ge(r_roped, n + 1)
                    dve.tensor_tensor(r_rot[:], bank(6, 2), r_sin[:], ALU.mult).then_inc(r_read, 1)
                    dve.tensor_tensor(z_out[:, s, cols], z_out[:, s, cols], r_cos[:], ALU.mult).then_inc(r_turned, 1)
                    dve.wait_ge(r_read, n + 1 + 1)
                    dve.wait_ge(r_turned, n + 1)
                    dve.tensor_tensor(z_out[:, s, cols], z_out[:, s, cols], r_rot[:], ALU.add).then_inc(r_roped, 1)

        @block.vector
        def _(dve):
            def keep_tokens(s, use, col):
                dve.wait_ge(tok_turned[s], use + 1)
                dve.tensor_copy(res[:, :, bass.ds(col, P)],
                                acc[s][:, 0:KT * P].rearrange("p (k t) -> p k t", t=P)).then_inc(tok_kept[s], 1)

            for s in range(2):
                keep_tokens(s, 0, s * P)
            with dve.Fori(0, QB // 2) as i:
                for s in range(2):
                    keep_tokens(s, i + 1, (2 * i + s) * P + CTX)
            dve.wait_ge(rows_turned, 1)
            dve.tensor_copy(vec[:], bank(6)[:, 0:V_END]).then_inc(vec_ready, 1)
            dve.tensor_copy(convv[:], bank(7)[:, 0:4 * 2 * FT]).then_inc(vec_ready, 1)
            dve.wait_ge(consts_in, 16 * 10)
            for n in range(2):
                dve.tensor_tensor_reduce(lamrows[:, 2 * n], lamrows[:, 2 * n], lamrows[:, 2 * n + 1], 1.0, 0.0, ALU.mult,
                                         ALU.add, lamt[:, n:n + 1]).then_inc(lam_step, 1)
            for n, rows_ in enumerate((ident[:], maskrows[:, 0], maskrows[:, 1])):
                dve.tensor_copy(masks[:, n], rows_).then_inc(masks_ready, 1)
            dve.wait_ge(vec_ready, 2)
            dve.tensor_scalar(vec32[:], vec[:, 0:V_BMOD], float(D) ** 0.5, None, ALU.mult).then_inc(vec32_ready, 1)
            dve.tensor_scalar(subg[:], vec[:, V_SUB:V_SUB + 1], 1.0 - LAM_INIT, None, ALU.mult).then_inc(vec32_ready, 1)
            dve.wait_ge(lam_exp, 1)
            dve.scalar_tensor_tensor(neg_lam[:], lamt[:, 3:4], LAM_INIT, lamt[:, 2:3], ALU.subtract, ALU.subtract).then_inc(lam_step, 1)
            for layer in range(2):
                with dve.Fori(0, 6) as i:
                    for s in range(2):
                        dve.wait_ge(mod_summed[s], i + (6 * layer + 1) + 1)
                        for n in range(2):
                            t = 4 * i + (2 * s + n + 24 * layer)
                            dve.tensor_scalar(mod[:, bass.ds(t, 1), :], acc[s][:, 2 * n:2 * n + 2].unsqueeze(1),
                                              vec[:, bass.ds(t + V_BMOD, 1)], None, ALU.add).then_inc(mod_kept[s], 1)
            for s in range(2):
                dve.wait_ge(mod_kept[s], 24 + 1)
            dve.wait_ge(vec32_ready, 2)
            for layer in range(2):
                for v in range(2):
                    dve.scalar_tensor_tensor(modg[:, layer, v], mod[:, 24 * layer + 8:24 * layer + 16, v], 1.0,
                                             vec32[:, V_G2 + KT * layer:V_G2 + KT * (layer + 1)], ALU.add,
                                             ALU.mult).then_inc(modg_ready, 1)
            norm_scale(dve, "mix", X_COLS)
            dve.wait_ge(f_soft, 3)
            dve.scalar_tensor_tensor(f_s[:, 0], f_x[:], 0.0, f_a[:], ALU.min, ALU.subtract).then_inc(f_scan, 1)
            for n in range(10):
                a, b, d = n % 2, 1 - n % 2, 1 << n
                dve.wait_ge(f_scan, 2 * n + 1)
                dve.tensor_copy(f_s[:, b, 0:d], f_s[:, a, 0:d]).then_inc(f_scan, 1)
                dve.tensor_tensor(f_s[:, b, d:], f_s[:, a, d:], f_s[:, a, 0:SEQ - d], ALU.add).then_inc(f_scan, 1)
            dve.wait_ge(f_scan, 21)
            dve.tensor_scalar(f_x[:], f_s[:, 0], -1.0 / SCALE, None, ALU.mult).then_inc(f_scan, 1)
            dve.wait_ge(f_scan, 22)
            dve.tensor_copy(f_parts[:, 0], f_x[:]).then_inc(f_scan, 1)
            dve.wait_ge(f_scan, 23)
            dve.tensor_tensor(f_parts[:, 1], f_x[:], f_parts[:, 0].bitcast(F32), ALU.subtract).then_inc(f_scan, 1)
            with dve.Fori(0, 4) as j:
                v = ps[:, 0:2 * BANK].rearrange("p (g d) -> p g d", d=DH)

                def by_head(n):
                    return s_stat[:, n].unsqueeze(2).broadcast_to([P, 16, DH])

                dve.wait_ge(s_turned, j + 1)
                dve.tensor_reduce(s_stat[:, 0], v, AX, ALU.add).then_inc(s_stats, 1)
                dve.wait_ge(s_stats, 6 * j + 1)
                dve.tensor_scalar(s_stat[:, 1], s_stat[:, 0], 1.0 / DH, None, ALU.mult).then_inc(s_stats, 1)
                dve.wait_ge(s_stats, 6 * j + 2)
                dve.tensor_tensor(s_ctr[:], v, by_head(1), ALU.subtract).then_inc(s_stats, 1)
                dve.wait_ge(s_squared, j + 1)
                dve.tensor_reduce(s_stat[:, 2], s_sq[:], AX, ALU.add).then_inc(s_stats, 1)
                dve.wait_ge(s_std, j + 1)
                dve.reciprocal(s_stat[:, 3], s_stat[:, 3]).then_inc(s_stats, 1)
                dve.wait_ge(s_stats, 6 * j + 5)
                dve.tensor_tensor(s_ctr[:], s_ctr[:], by_head(3), ALU.mult).then_inc(s_stats, 1)
                dve.wait_ge(s_in, 80 * j + 80)
                dve.wait_ge(s_mixed, j + 1)
                dve.wait_ge(s_low, j + 1)
                for e in range(2):
                    r = slice(e * DH, (e + 1) * DH)
                    got = ps[r, 4 * BANK:].rearrange("p (n e t) -> p n e t", e=2, t=P)[:, :, e]
                    dve.scalar_tensor_tensor(s_y[r].rearrange("p (n t) -> p n t", t=P), got, vec[r, bass.ds(j + V_LNG, 1)],
                                             s_b[r].unsqueeze(1).broadcast_to([DH, QB, P]), ALU.mult, ALU.add).then_inc(s_gated, 1)
                dve.wait_ge(s_gated, 4 * j + 2)
                dve.tensor_tensor(s_y[:], s_y[:], s_u[:], ALU.mult).then_inc(s_gated, 1)
                dve.wait_ge(s_gated, 4 * j + 3)
                dve.tensor_copy(hh[:, bass.ds(j, 1), X_COLS], s_y[:].unsqueeze(1)).then_inc(s_gated, 1)
            with dve.Fori(0, 4) as j:
                def fa_max(u):
                    s, at, w = u % 3, 2 * (u % 2) * BANK, (u % QB + 1) * P
                    dve.wait_ge(fa.scored, 16 * j + (u + 1) + 1)
                    if u >= 3:
                        dve.wait_ge(fa.turned, 18 * j + (u - 1))
                    dve.tensor_scalar(a_s[:, s, 0:w], ps[:, at:at + w], -SCALE, HIGHEST, ALU.mult, ALU.min,
                                      accum_out=a_low[:, s:s + 1]).then_inc(fa.maxed, 1)

                for u in range(2 * QB):
                    fa_max(u)
                dve.wait_ge(fa.exped, 16 * j + 16)
                dve.reciprocal(a_rec[:], a_sum[:]).then_inc(fa.normed, 1)
                dve.wait_ge(fa.normed, 2 * j + 1 + 1)
                dve.wait_ge(fa.mixed, 16 * j + 16 + 1)
                dve.tensor_tensor(a_o[:], bank(6, 2).rearrange("p (i a d) -> p i a d", a=2, d=DH),
                                  a_rec[:].rearrange("p a i -> p i a").unsqueeze(3).broadcast_to([P, QB, 2, DH]),
                                  ALU.mult).then_inc(fa.normed, 1)
                to = hh[:, bass.ds(j + 4, 1), X_COLS]
                dve.wait_ge(fa.turned, 18 * j + 18)
                dve.tensor_copy(to, bank(4, 2).unsqueeze(1)).then_inc(fa.kept, 1)
                dve.wait_ge(fa.kept, 2 * j + 1 + 1)
                dve.tensor_tensor(hl[:, bass.ds(j + 4, 1), X_COLS], bank(4, 2).unsqueeze(1), to.bitcast(F32), ALU.subtract).then_inc(fa.kept, 1)
            add_to_residual(dve, "w_out", ((X_COLS, 0, None),))
            norm_scale(dve, "ffn", X_COLS)

            def ffn_taps(chunk, e, acc_use):
                for s in range(2):
                    tile = 2 * chunk + (s * FT + e)
                    dve.wait_ge(f_based[s], 2 * chunk + (e + 1))
                    dve.scalar_tensor_tensor(f_y[:, s, 1:], acc[s][:, 0:SEQ - 1], convv[:, bass.ds(tile + 2 * FT, 1)],
                                             f_y[:, s, 1:], ALU.mult, ALU.add).then_inc(f_tapped[s], 1)
                    dve.wait_ge(f_tapped[s], 2 * chunk + (e + 1))
                    dve.scalar_tensor_tensor(f_y[:, s, 2:], acc[s][:, 0:SEQ - 2], convv[:, bass.ds(tile, 1)],
                                             f_y[:, s, 2:], ALU.mult, ALU.add).then_inc(acc_free[s], 1)
                dve.wait_ge(f_gate, 2 * chunk + (e + 1))
                dve.wait_ge(acc_free[1], acc_use + (A0["ffn"][1] + 1) + 1)
                dve.wait_ge(f_low, 2 * chunk + e)
                dve.tensor_tensor(f_act[:], f_g[:], f_y[:, 1], ALU.mult).then_inc(f_mult, 1)

            def ffn_high(chunk, e):
                dve.wait_ge(f_mult, 2 * chunk + (e + 1))
                dve.wait_ge(d_used, chunk + 1)
                dve.tensor_copy(f_hi[:, e], f_act[:]).then_inc(f_high, 1)

            def ffn_down(chunk):
                for m in range(KT):
                    if m < KT - 1:
                        dve.wait_ge(f_down, 7 * chunk + (m + 1))
                    else:
                        dve.wait_ge(d_used, chunk + 1 + 1)
                    dve.tensor_tensor(res[:, m, X_COLS], acc[m % 2][:, 0:SEQ], res[:, m, X_COLS], ALU.add).then_inc(acc_free[m % 2], 1)

            ffn_taps(0, 0, 0)
            ffn_high(0, 0)
            ffn_taps(0, 1, 1)
            ffn_high(0, 1)
            with dve.Fori(1, CHUNKS) as c:
                ffn_taps(c, 0, 6 * c - 4)
                ffn_down(c - 1)
                ffn_high(c, 0)
                ffn_taps(c, 1, 6 * c + 1)
                ffn_high(c, 1)
            ffn_down(CHUNKS - 1)
            norm_scale(dve, "fin", X_COLS)
            for s in range(2):
                dve.wait_ge(n_gained[s], 4 * (NORMS["fin"] + 1) + 1)
            norm_scale(dve, "a_x", X_COLS)
            norm_scale(dve, "a_ctx", slice(0, CTX))
            for s in range(2):
                dve.wait_ge(n_low[s], 4 * (SPLITS["a_ctx"] + 1) + 1)
            dve.wait_ge(consts_in, 16 * 12)
            rotate(dve, "a_qk", 16, CTX)
            dve.wait_ge(lam_step, 3)

            def da_max(h, u):
                s, w = u % 3, da_tiles(u) * P
                if u >= 3:
                    dve.wait_ge(da.turned, da_turn(h, "p", u - 3, len(batches(da_tiles(u - 3))) - 1)[2])
                dve.wait_ge(da.scored, 10 * h + (u + 1) + 1)
                dve.tensor_scalar(d_p0[:, s, 0:w], acc[0][:, 0:w], -SCALE, HIGHEST, ALU.mult, ALU.min,
                                  accum_out=d_low[:, s, 0:1]).then_inc(da.maxed, 1)
                if u >= 2:
                    dve.wait_ge(da_weighed, 30 * h + (3 * u - 3))
                dve.wait_ge(da_scored1, 10 * h + (u + 1) + 1)
                dve.tensor_scalar(d_p1[:, u % 2, 0:w], acc[1][:, 0:w], -SCALE, HIGHEST, ALU.mult, ALU.min,
                                  accum_out=d_low[:, s, 1:2]).then_inc(da_maxed1, 1)

            def da_weigh(h, u):
                s, w = u % 3, da_tiles(u) * P
                dve.wait_ge(da_exped1, 10 * h + (u + 1))
                dve.reciprocal(d_rec[:, s, 0:1], d_sum[:, 1, u:u + 1]).then_inc(da_weighed, 1)
                dve.wait_ge(da.exped, 10 * h + (u + 1))
                dve.wait_ge(da_weighed, 30 * h + (3 * u + 1))
                dve.scalar_tensor_tensor(d_rec[:, s, 1:2], d_sum[:, 0, u:u + 1], neg_lam[:], d_rec[:, s, 0:1],
                                         ALU.mult, ALU.mult).then_inc(da_weighed, 1)
                dve.wait_ge(da_weighed, 30 * h + (3 * u + 2))
                dve.scalar_tensor_tensor(d_p0[:, s, 0:w], d_p1[:, u % 2, 0:w], d_rec[:, s, 1:2], d_p0[:, s, 0:w], ALU.mult,
                                         ALU.add).then_inc(da_weighed, 1)

            def da_mean(h):
                dve.wait_ge(da.normed, 4 * h - 3)
                b, before, _ = da_turn(h - 1, "m", TOK // P - 1)
                dve.wait_ge(da_free[b], before + 1 + 1)
                dve.scalar_tensor_tensor(d_rs[:], d_ss[:], 1.0 / P, d_eps[:], ALU.mult, ALU.add).then_inc(da.normed, 1)

            def da_norm(h):
                dve.wait_ge(da_rms, h)
                dve.reciprocal(d_rs[:], d_rs[:]).then_inc(da.normed, 1)
                dve.wait_ge(da.normed, 4 * h - 1)
                dve.tensor_tensor(d_o[:], d_o[:], d_rs[:].unsqueeze(2).broadcast_to([P, TOK // P, P]), ALU.mult).then_inc(da.normed, 1)

            def da_gate(h):
                dve.wait_ge(da_gloaded, 16 * h)
                for n, blocks in enumerate(batches(TOK // P)):
                    b, _, turned = da_turn(h, "o", n)
                    cols = slice(blocks.start * P, blocks.stop * P)
                    dve.wait_ge(da.turned, turned)
                    dve.scalar_tensor_tensor(d_g[:, cols], bank(6 + b)[:, 0:len(blocks) * P], subg[:], d_g[:, cols],
                                             ALU.mult, ALU.mult).then_inc(da_free[b], 1)
                for n in range(len(batches(TOK // P)))[-2:]:
                    b, before, _ = da_turn(h, "o", n)
                    dve.wait_ge(da_free[b], before + 1 + 1)
                dve.tensor_copy(hh[:, bass.ds(h - 1, 1)], d_g.unsqueeze(1)).then_inc(da_gated, 1)

            def da_head(h, first):
                da_max(h, 0)
                if not first:
                    da_mean(h)
                da_max(h, 1)
                if not first:
                    da_norm(h)
                for u in range(TOK // P):
                    da_weigh(h, u)
                    if u + LEAD < TOK // P:
                        da_max(h, u + LEAD)
                    if u == 1 and not first:
                        da_gate(h)
                dve.scalar_tensor_tensor(d_eps[:], d_sum[:, 0], SUB_EPS, d_sum[:, 0], ALU.mult, ALU.mult).then_inc(da.normed, 1)

            da_head(0, True)
            with dve.Fori(1, DA_HEADS) as h:
                da_head(h, False)
            da_mean(DA_HEADS)
            da_norm(DA_HEADS)
            da_gate(DA_HEADS)
            add_to_residual(dve, "a_out", ((X_COLS, CTX, (0, 0)), (slice(0, CTX), 0, (0, 1))))
            norm_scale(dve, "b_x", X_COLS)
            norm_scale(dve, "b_ctx", slice(0, CTX))
            for s in range(2):
                dve.wait_ge(n_low[s], 4 * (SPLITS["b_ctx"] + 1) + 1)
            dve.wait_ge(consts_in, 16 * 14)
            rotate(dve, "b_q", 8, 0)
            rotate(dve, "b_k", 2, CTX)
            with dve.Fori(0, 4) as h:
                def ba_max(u):
                    i, a = divmod(u, 4)
                    s, at, w = u % 3, 2 * (u % 2) * BANK, len(window_tiles(i)) * P
                    dve.wait_ge(ba.scored, 32 * h + (u + 1) + 1)
                    if u >= 3:
                        dve.wait_ge(ba.turned, 33 * h + (u - 1))
                    dve.tensor_scalar(b_s[:, s, 0:w], ps[:, at:at + w], -SCALE, HIGHEST, ALU.mult, ALU.min,
                                      accum_out=b_low[:, 0, s:s + 1]).then_inc(ba.maxed, 1)
                    dve.wait_ge(ba.maxed, 32 * h + (u + 1))
                    dve.tensor_scalar(b_low[:, 1, s:s + 1], sinks[:, bass.ds(4 * h + a, 1)], -1.0, b_low[:, 0, s:s + 1],
                                      ALU.mult, ALU.min).then_inc(ba_biased, 1)

                def ba_norm(i):
                    dve.wait_ge(ba.exped, 64 * h + (8 * i + 8))
                    dve.tensor_tensor(b_rec[:, 0], b_sum[:, i % 2], b_sink[:, i % 2], ALU.add).then_inc(ba.normed, 1)
                    dve.wait_ge(ba.normed, 24 * h + (3 * i + 1))
                    dve.reciprocal(b_rec[:, 1], b_rec[:, 0]).then_inc(ba.normed, 1)
                    dve.wait_ge(ba.normed, 24 * h + (3 * i + 2))
                    dve.wait_ge(ba.mixed, 32 * h + (4 * i + 4) + 1)
                    dve.tensor_tensor(b_o[:].rearrange("p (a d) -> p a d", d=DH), bank(6 + i % 2)[:, 0:2 * P].rearrange("p (a d) -> p a d", d=DH),
                                      b_rec[:, 1].unsqueeze(2).broadcast_to([P, 4, DH]), ALU.mult).then_inc(ba.normed, 1)

                def ba_keep(i):
                    cols = slice(CTX + i * P, CTX + (i + 1) * P)
                    dve.wait_ge(ba_gloaded, 16 * h + 16)
                    dve.wait_ge(ba_o_turned, 8 * h + (i + 1))
                    dve.wait_ge(ba.low, 8 * h + i + 1)
                    dve.tensor_tensor(b_y[:], bank(6 + i % 2)[:, 2 * P:4 * P].rearrange("p (t q) -> p t q", t=2),
                                      b_g[:, :, i * P:(i + 1) * P], ALU.mult).then_inc(ba.kept, 1)
                    dve.wait_ge(ba.kept, 16 * h + (2 * i + 1))
                    dve.tensor_copy(hh[:, bass.ds(2 * h, 2), cols], b_y[:]).then_inc(ba.kept, 1)

                for u in range(LEAD):
                    ba_max(u)
                for u in range(4 * QB):
                    i, a = divmod(u, 4)
                    if u + LEAD < 4 * QB:
                        ba_max(u + LEAD)
                    if i and a == 0:
                        ba_norm(i - 1)
                    if i and a == 2:
                        ba_keep(i - 1)
                ba_norm(QB - 1)
                ba_keep(QB - 1)
            add_to_residual(dve, "b_out", ((X_COLS, 0, (1, 0)),))
            norm_scale(dve, "out", X_COLS)


_INS = [
    "x", "norm_mix_g", "w_in", "f_bias", "sg_ln_g", "sg_w", "sg_b", "w_out", "norm_ffn_g", "w_up", "w_conv", "b_conv", "w_down",
    "norm_final_g", "c_2", "ctx_2", "c_ctx_2", "w_mod_2", "b_mod_2", "norm_g_2", "w_o_2", "a_w_in_2", "a_lambda_q1_2",
    "a_lambda_k1_2", "a_lambda_q2_2", "a_lambda_k2_2", "a_subln_g_2", "b_w_in_2", "b_sink_2", "final_g_2",
]


def constants():
    import numpy as np

    n = np.arange(P)
    causal = np.where(n[None, :] <= n[:, None], 0.0, -1e30)
    before = np.where(n[None, :] >= n[:, None], 0.0, -1e30)
    half, grid = DH // 2, 64
    inv = (np.float32(10000.0) ** (-np.arange(0, half, 2, dtype=np.float32) / np.float32(half))).astype(np.float32)
    t = np.arange(SEQ)
    place = np.stack([t // grid, t % grid]).astype(np.float32)
    angle = np.stack([place[(f % DH) // half] * inv[f % 16] for f in range(P)]).astype(np.float32)
    sign = np.where(n % half < 16, -1.0, 1.0)[:, None]
    return {
        "const_ident": np.eye(P, dtype=np.float32), "const_swap": np.eye(P, dtype=np.float32)[n ^ 16],
        "const_causal": causal.astype(np.float32), "const_before": before.astype(np.float32), "const_cos": np.cos(angle).astype(np.float32),
        "const_sin": (sign * np.sin(angle)).astype(np.float32),
    }


def kernel(**inputs):
    import numpy as np
    import concourse.bacc as bacc
    from concourse.bass_utils import run_bass_kernel_spmd

    nc = bacc.Bacc("TRN2", target_bir_lowering=False, num_devices=1)
    arrays = {f"in_{name}": np.ascontiguousarray(inputs[name]) for name in _INS}
    arrays.update(constants())
    args = [nc.dram_tensor(name, a.shape, F32, kind="ExternalInput").ap() for name, a in arrays.items()]
    args.append(nc.dram_tensor("out_rows", (1, SEQ, D), F32, kind="ExternalOutput").ap())
    two_block_kernel(nc, *args)
    got = run_bass_kernel_spmd(nc, [arrays], core_ids=[0])
    return got.results[0]["out_rows"]
```

```python
from contextlib import ExitStack

import concourse.bass as bass
from concourse import mybir

F32 = mybir.dt.float32
F32R = mybir.dt.float32r
ALU = mybir.AluOpType
ACT = mybir.ActivationFunctionType
AX = mybir.AxisListType.X

P = 128
D = 1024
KT = D // P
CTX = 256
SEQ = 1024
TOK = CTX + SEQ
BANK = 512
DH = 64
D_FF = 2816
FT = D_FF // P
CHUNKS = FT // 2
QB = SEQ // P
EPS = 1e-6
MOD_TILES = 3
SUB_EPS = 1e-5
LAM_INIT = 0.8 - 0.6
SCALE = DH ** -0.5

V_MIX, V_FFN, V_FIN, V_G2, V_FG2, V_BMOD, V_SUB, V_LNG, V_C, V_END = 0, 8, 16, 24, 40, 48, 96, 97, 101, 117

X_COLS = slice(CTX, TOK)
ALL_COLS = slice(0, TOK)
DA_HEADS = 8
SPREAD_BANKS = (7, 6, 0)
LEAD = 2
HIGHEST = 3.0e38


def chunks(width):
    return [(c, min(BANK, width - c)) for c in range(0, width, BANK)]


def batches(blocks):
    return [range(n, min(n + 4, blocks)) for n in range(0, blocks, 4)]


def da_tiles(u):
    return CTX // P if u < CTX // P else TOK // P


def da_plan(heads_before):
    turns = [("v", n) for n in range(len(batches(TOK // P)))]
    for u in range(TOK // P):
        weights = [("p", u, n) for n in range(len(batches(da_tiles(u))))]
        output = [("o", n) for n in range(len(batches(TOK // P)))] if u == 1 and heads_before else []
        turns += weights[0:2] + output + [("m", u - 1)] * (u > 0) + weights[2:]
    turns.append(("m", TOK // P - 1))
    return {key: n for n, key in enumerate(turns)}


def da_turn(h, *key):
    mixes = TOK // P
    first, plan = da_plan(False), da_plan(True)
    per_head, short = len(plan), len(plan) - len(first)
    if isinstance(h, int) and h == 0:
        n = first[key]
        mixed = sum(k[0] == "m" for k in first if first[k] < n)
        return n % 2, n // 2, n + 1 - mixed
    last = isinstance(h, int) and h == DA_HEADS
    n = key[1] if last else plan[key]
    mixed = 0 if last else sum(k[0] == "m" for k in plan if plan[k] < n)
    return (n - short) % 2, per_head // 2 * h + (n - short) // 2, (per_head - mixes) * h + (n - short + 1 - mixed)


def window_tiles(i):
    return [2 + i - 1] * (i > 0) + [0, 1, 2 + i] + [2 + i + 1] * (i < QB - 1)


def two_block_kernel(
    nc, x, norm_mix_g, w_in, f_bias, sg_ln_g, sg_w, sg_b, w_out, norm_ffn_g, w_up, w_conv, b_conv, w_down,
    norm_final_g, c_2, ctx_2, c_ctx_2, w_mod_2, b_mod_2, norm_g_2, w_o_2, a_w_in_2, a_lambda_q1_2, a_lambda_k1_2,
    a_lambda_q2_2, a_lambda_k2_2, a_subln_g_2, b_w_in_2, b_sink_2, final_g_2,
    const_ident, const_swap, const_causal, const_before, const_cos, const_sin, out,
):
    z1 = nc.dram_tensor("z1", (20 * P, SEQ), F32, kind="Internal").ap()
    forget_rows = nc.dram_tensor("forget_rows", (2, 8, SEQ), F32, kind="Internal").ap()
    za = nc.dram_tensor("za", (32 * P, TOK), F32, kind="Internal").ap()
    zb = nc.dram_tensor("zb", (20 * P, TOK), F32, kind="Internal").ap()

    with ExitStack() as ctx:
        def alloc(scope, name, shape, dt=F32):
            return scope.enter_context(nc.sbuf_tensor(name, shape, dt))

        def sb(name, shape, dt=F32):
            return alloc(ctx, name, shape, dt)

        def sem(name):
            return ctx.enter_context(nc.semaphore(name))

        def sem2(name):
            return [sem(f"{name}{s}") for s in range(2)]

        res = sb("res", [P, KT, TOK])
        hh = sb("hh", [P, KT, TOK], F32R)
        hl = sb("hl", [P, KT, TOK], F32R)
        w_raw = sb("w_raw", [P, 2, KT * P])
        wh = sb("wh", [P, 2, KT * P], F32R)
        wl = sb("wl", [P, 2, KT * P], F32R)
        ident = sb("ident", [P, P])
        ones = sb("ones", [P, P])
        swap = sb("swap", [P, P])
        masks = sb("masks", [P, 3, P], F32R)
        ones_r = sb("ones_r", [2, P], F32R)
        vec = sb("vec", [P, V_END])
        vec32 = sb("vec32", [P, V_BMOD])
        convv = sb("convv", [P, 4 * 2 * FT])
        mod = sb("mod", [P, 48, 2])
        modg = sb("modg", [P, 2, 2, KT])
        zero = sb("zero", [P, 1])
        eps_d = sb("eps_d", [P, 1])
        one = sb("one", [P, 1])
        eps_1 = sb("eps_1", [P, 1])
        cond = sb("cond", [P, KT, 2])
        neg_lam = sb("neg_lam", [P, 1])
        subg = sb("subg", [P, 1])
        sinks = sb("sinks", [P, 16])
        fb = sb("fb", [8, 1])
        n_col = sb("n_col", [P, TOK // P])
        s_wt = sb("s_wt", [P, 2, P])
        ps = ctx.enter_context(nc.psum_tensor("ps", [P, 8 * BANK], F32))

        def bank(b, n=1):
            return ps[:, b * BANK:(b + n) * BANK]

        acc = [bank(0, 3), bank(3, 3)]

        scope = ExitStack()
        tokrows = alloc(scope, "tokrows", [P, 2, D])
        rows = alloc(scope, "rows", [P, P])
        convrows = alloc(scope, "convrows", [88, 2, P])
        lamrows = alloc(scope, "lamrows", [P, 4, DH])
        maskrows = alloc(scope, "maskrows", [P, 2, P])
        lamt = alloc(scope, "lamt", [P, 4])
        scope.close()
        scope = ExitStack()
        n_sq = alloc(scope, "n_sq", [P, 2, TOK])
        n_sum = alloc(scope, "n_sum", [P, TOK])
        n_rs = alloc(scope, "n_rs", [P, TOK])
        n_t = alloc(scope, "n_t", [P, 2, TOK])
        n_h = alloc(scope, "n_h", [P, 2, TOK])
        tok_out = alloc(scope, "tok_out", [P, 2, KT, P])
        scope.close()
        scope = ExitStack()
        z_out = alloc(scope, "z_out", [P, 2, TOK])
        f_x = alloc(scope, "f_x", [8, SEQ])
        f_a = alloc(scope, "f_a", [8, SEQ])
        inner = ExitStack()
        f_s = alloc(inner, "f_s", [8, 2, SEQ])
        inner.close()
        f_parts = alloc(scope, "f_parts", [8, 2, SEQ], F32R)
        mod_acc = alloc(scope, "mod_acc", [P, 2, 2, MOD_TILES * P])
        f_keep = alloc(scope, "f_keep", [P, SEQ // 4])
        w_mod_sb = alloc(scope, "w_mod_sb", [P, 2, KT, MOD_TILES * P])
        scope.close()
        scope = ExitStack()
        s_keep = alloc(scope, "s_keep", [P, 7 * SEQ])
        s_u = alloc(scope, "s_u", [P, SEQ])
        s_v = alloc(scope, "s_v", [P, SEQ])
        s_w = alloc(scope, "s_w", [P, 2, P])
        s_b = alloc(scope, "s_b", [P, P])
        s_ctr = alloc(scope, "s_ctr", [P, 16, DH])
        s_sq = alloc(scope, "s_sq", [P, 16, DH])
        s_stat = alloc(scope, "s_stat", [P, 4, 16])
        s_y = alloc(scope, "s_y", [P, SEQ])
        scope.close()
        scope = ExitStack()
        a_q = alloc(scope, "a_q", [P, SEQ])
        a_k = alloc(scope, "a_k", [P, SEQ])
        a_vt = alloc(scope, "a_vt", [P, SEQ])
        a_c = alloc(scope, "a_c", [2, 2, SEQ], F32R)
        a_v = alloc(scope, "a_v", [P, QB, P])
        a_s = alloc(scope, "a_s", [P, 3, SEQ])
        a_pt = alloc(scope, "a_pt", [P, 2, QB, P])
        a_o = alloc(scope, "a_o", [P, QB, 2, DH])
        a_low = alloc(scope, "a_low", [P, 3])
        a_sum = alloc(scope, "a_sum", [P, 2, QB])
        a_rec = alloc(scope, "a_rec", [P, 2, QB])
        scope.close()
        scope = ExitStack()
        f_y = alloc(scope, "f_y", [P, 2, SEQ])
        f_g = alloc(scope, "f_g", [P, SEQ])
        f_act = alloc(scope, "f_act", [P, SEQ])
        f_hi = alloc(scope, "f_hi", [P, 2, SEQ], F32R)
        f_lo = alloc(scope, "f_lo", [P, 2, SEQ], F32R)
        d_raw = alloc(scope, "d_raw", [P, 2, D])
        d_hi = alloc(scope, "d_hi", [P, 2, D], F32R)
        d_lo = alloc(scope, "d_lo", [P, 2, D], F32R)
        scope.close()
        scope = ExitStack()
        d_q = alloc(scope, "d_q", [P, TOK])
        d_k = alloc(scope, "d_k", [P, TOK])
        d_g = w_raw[:].rearrange("p s n -> p (s n)")[:, 0:TOK]
        d_v = alloc(scope, "d_v", [P, TOK // P, P])
        d_p0 = alloc(scope, "d_p0", [P, 3, TOK])
        d_p1 = alloc(scope, "d_p1", [P, 2, TOK])
        d_pt = alloc(scope, "d_pt", [P, 2, TOK // P, P])
        d_vt = wh[:].rearrange("p s n -> p (s n)")[:, 0:TOK].bitcast(F32)
        d_o = alloc(scope, "d_o", [P, TOK // P, P])
        d_sq = alloc(scope, "d_sq", [P, P])
        d_low = alloc(scope, "d_low", [P, 3, 2])
        d_sum = alloc(scope, "d_sum", [P, 2, TOK // P])
        d_rec = alloc(scope, "d_rec", [P, 3, 2])
        d_ss = alloc(scope, "d_ss", [P, TOK // P])
        d_eps = alloc(scope, "d_eps", [P, TOK // P])
        d_rs = alloc(scope, "d_rs", [P, TOK // P])
        scope.close()
        scope = ExitStack()
        b_q = alloc(scope, "b_q", [P, 2, SEQ])
        b_k = alloc(scope, "b_k", [P, TOK])
        b_vt = alloc(scope, "b_vt", [P, TOK // 2])
        b_v = alloc(scope, "b_v", [P, TOK // 2 // P, 2, DH])
        b_g = alloc(scope, "b_g", [P, 2, SEQ])
        b_s = alloc(scope, "b_s", [P, 3, 5 * P])
        b_pt = alloc(scope, "b_pt", [P, 2, 5, P])
        b_o = alloc(scope, "b_o", [P, 2 * P])
        b_y = alloc(scope, "b_y", [P, 2, P])
        b_low = alloc(scope, "b_low", [P, 2, 3])
        b_sum = alloc(scope, "b_sum", [P, 2, 4])
        b_sink = alloc(scope, "b_sink", [P, 2, 4])
        b_rec = alloc(scope, "b_rec", [P, 2, 4])
        scope.close()
        scope = ExitStack()
        r_keep = alloc(scope, "r_keep", [P, 2 * TOK])
        r_cos = alloc(scope, "r_cos", [P, SEQ])
        r_sin = alloc(scope, "r_sin", [P, SEQ])
        r_rot = alloc(scope, "r_rot", [P, SEQ])
        scope.close()

        consts_in = sem("consts_in")
        rows_in = sem("rows_in")
        zeroed = sem("zeroed")
        rows_turned, vec_ready = sem("rows_turned"), sem("vec_ready")
        vec32_ready, cond_ready = sem("vec32_ready"), sem("cond_ready")
        tok_in, tok_turned, tok_kept = sem2("tok_in"), sem2("tok_turned"), sem2("tok_kept")
        lam_step = sem("lam_step")
        lam_exp = sem("lam_exp")
        mod_in, mod_mult, mod_done = sem2("mod_in"), sem("mod_mult"), sem2("mod_done")
        mod_summed, mod_kept = sem2("mod_summed"), sem2("mod_kept")
        modg_ready = sem("modg_ready")
        w_landed, w_high, w_split, w_used = sem2("w_landed"), sem2("w_high"), sem2("w_split"), sem2("w_used")
        acc_free, stored = sem2("acc_free"), sem2("stored")
        res_added = sem("res_added")
        n_squared, n_added = sem2("n_squared"), sem2("n_added")
        n_zeroed, n_summed, n_root, n_scaled = sem("n_zeroed"), sem("n_summed"), sem("n_root"), sem("n_scaled")
        n_spread, n_rooted, n_kept = sem("n_spread"), sem("n_rooted"), sem("n_kept")
        n_times, n_gained = sem2("n_times"), sem2("n_gained")
        n_high, n_low = sem2("n_high"), sem2("n_low")
        out_turned, out_kept, out_stored = sem2("out_turned"), sem2("out_kept"), sem2("out_stored")
        f_biased, f_soft, f_scan, f_stored = sem("f_biased"), sem("f_soft"), sem("f_scan"), sem("f_stored")
        s_in, s_given, s_turned, s_stats, s_squared, s_std = sem("s_in"), sem("s_given"), sem("s_turned"), sem("s_stats"), sem("s_squared"), sem("s_std")
        s_wt_ready, s_mixed, s_gated, s_low = sem("s_wt_ready"), sem("s_mixed"), sem("s_gated"), sem("s_low")
        f_based, f_tapped, f_gate, f_mult = sem2("f_based"), sem2("f_tapped"), sem("f_gate"), sem("f_mult")
        f_high, f_low, f_down = sem("f_high"), sem("f_low"), sem("f_down")
        d_landed, d_high, d_split, d_used = sem2("d_landed"), sem2("d_high"), sem2("d_split"), sem("d_used")
        r_swapped, r_read, r_turned, r_roped = sem("r_swapped"), sem("r_read"), sem("r_turned"), sem("r_roped")
        masks_ready = sem("masks_ready")

        class Mixer:
            def __init__(self, name):
                self.loaded, self.scored = sem(name + "_loaded"), sem(name + "_scored")
                self.maxed, self.exped = sem(name + "_maxed"), sem(name + "_exped")
                self.turned, self.pt_kept, self.mixed = sem(name + "_turned"), sem(name + "_pt_kept"), sem(name + "_mixed")
                self.normed, self.kept, self.low = sem(name + "_normed"), sem(name + "_kept"), sem(name + "_low")

        fa, da, ba = Mixer("fa"), Mixer("da"), Mixer("ba")
        da_scored1, da_maxed1, da_exped1 = sem("da_scored1"), sem("da_maxed1"), sem("da_exped1")
        da_vloaded, da_gloaded, ba_gloaded = sem("da_vloaded"), sem("da_gloaded"), sem("ba_gloaded")
        da_weighed, da_rms, da_gated = sem("da_weighed"), sem("da_rms"), sem("da_gated")
        ba_biased, ba_o_turned = sem("ba_biased"), sem("ba_o_turned")
        da_free = sem2("da_free")

        W0, A0, Z0 = {}, {}, {}
        w_n, a_n, z_n = [0, 0], [0, 0], [0, 0]
        for name, w_uses, a_uses, z_uses in (
            ("gelu", (4, 4), (4, 4), (4, 4)), ("forget", (1, 0), (1, 0), (0, 0)), ("plain", (6, 6), (6, 6), (6, 6)),
            ("w_out", (4, 4), (4, 4), (0, 0)),
            ("ffn", (2 * CHUNKS, 2 * CHUNKS), (6 * CHUNKS, 6 * CHUNKS), (0, 0)),
            ("a_qk", (8, 8), (8, 8), (8, 8)), ("a_v", (4, 4), (4, 4), (4, 4)), ("a_gate", (4, 4), (4, 4), (4, 4)), ("a_out", (4, 4), (4, 4), (0, 0)),
            ("b_q", (4, 4), (4, 4), (4, 4)), ("b_k", (1, 1), (1, 1), (1, 1)), ("b_v", (1, 1), (1, 1), (1, 1)), ("b_gate", (4, 4), (4, 4), (4, 4)),
            ("b_out", (4, 4), (4, 4), (0, 0)),
        ):
            W0[name], A0[name], Z0[name] = tuple(w_n), tuple(a_n), tuple(z_n)
            for s in range(2):
                w_n[s] += w_uses[s]
                a_n[s] += a_uses[s]
                z_n[s] += z_uses[s]
        R0 = {"a_qk": 0, "b_q": 16, "b_k": 24}
        NORMS = {name: n for n, name in enumerate(("mix", "ffn", "fin", "a", "b", "out"))}
        SPLITS = {name: n for n, name in enumerate(("mix", "ffn", "a", "b"))}

        LATENT_SEGS = [(CTX, BANK, 0), (CTX + BANK, BANK, BANK)]
        ALL_SEGS = [(0, BANK, 0), (BANK, BANK, BANK), (2 * BANK, TOK - 2 * BANK, 2 * BANK)]

        block = ctx.enter_context(nc.Block())

        def weight_tiles(sp, name, w, col0, tiles, tables=None, mod_layer=None, norm=None):
            view = w.rearrange("(k p) n -> p k n", p=P)

            def mod_tiles(i, s):
                sp.wait_ge(mod_done[s], i + 4 * mod_layer + 1)
                sp.dma_start(w_mod_sb[:, s], w_mod_2[mod_layer].rearrange("(k p) n -> p k n", p=P)[
                    :, :, bass.ds((2 * i + s) * MOD_TILES * P, MOD_TILES * P)]).then_inc(mod_in[s], 16)

            def tile_pair(i):
                for s in range(2):
                    sp.wait_ge(w_split[s], i + W0[name][s] + 1)
                    sp.dma_start(w_raw[:, s].rearrange("p (k n) -> p k n", k=KT),
                                 view[:, :, bass.ds((2 * i + s) * P + col0, P)]).then_inc(w_landed[s], 16)
                if mod_layer is not None:
                    for s in range(2):
                        if norm:
                            sp.wait_ge(n_low[s], 4 * (SPLITS[norm] + 1) + 1)
                    for s in range(2):
                        mod_tiles(i, s)

            tile_pair(0)
            if tables:
                (free, count), *loads = tables
                for s in range(2):
                    sp.wait_ge(free[s], count)
                for dst, src in loads:
                    sp.dma_start(dst[:], src).then_inc(consts_in, 16)
            if tiles > 2:
                with sp.Fori(1, tiles // 2) as i:
                    tile_pair(i)

        @block.sync
        def _(sp):
            for dst, src in ((ident[:], const_ident), (swap[:], const_swap),
                             (maskrows[:, 0], const_causal), (maskrows[:, 1], const_before),
                             (lamrows[:, 0], a_lambda_q1_2.broadcast_to([P, DH])),
                             (lamrows[:, 1], a_lambda_k1_2.broadcast_to([P, DH])),
                             (lamrows[:, 2], a_lambda_q2_2.broadcast_to([P, DH])),
                             (lamrows[:, 3], a_lambda_k2_2.broadcast_to([P, DH])),
                             (sinks[:], b_sink_2.broadcast_to([P, 16])),
                             (fb[:], f_bias.rearrange("o h -> h o"))):
                sp.dma_start(dst, src).then_inc(consts_in, 16)
            for at, v in ((V_MIX, norm_mix_g), (V_FFN, norm_ffn_g), (V_G2, norm_g_2), (V_BMOD, b_mod_2),
                          (V_SUB, a_subln_g_2), (V_C, c_2)):
                n = v.shape[0] * v.shape[1] // P
                sp.dma_start(rows[at:at + n, :], v.rearrange("o (t p) -> (o t) p", p=P)).then_inc(rows_in, 16)
            for at, v in ((V_FIN, norm_final_g), (V_FG2, final_g_2), (V_C + KT, c_ctx_2)):
                sp.dma_start(rows[at:at + KT, :], v.rearrange("(t p) -> t p", p=P)).then_inc(rows_in, 16)
            sp.dma_start(rows[V_LNG:V_LNG + 4, :],
                         sg_ln_g[0].rearrange("(j e) d -> j (e d)", e=2)).then_inc(rows_in, 16)
            for tap, (slot, at) in enumerate(((0, 0), (0, 44), (1, 0))):
                sp.dma_start(convrows[at:at + 2 * FT, slot, :],
                             w_conv[0, tap].rearrange("(t p) -> t p", p=P)).then_inc(rows_in, 16)
            sp.dma_start(convrows[44:88, 1, :], b_conv[0].rearrange("(t p) -> t p", p=P)).then_inc(rows_in, 16)
            for s in range(2):
                sp.dma_start(tokrows[:, s], ctx_2[0, s * P:(s + 1) * P, :]).then_inc(tok_in[s], 16)
            with sp.Fori(0, QB // 2) as i:
                for s in range(2):
                    sp.wait_ge(tok_turned[s], i + 1)
                    sp.dma_start(tokrows[:, s], x[0, bass.ds((2 * i + s) * P, P), :]).then_inc(tok_in[s], 16)
            weight_tiles(sp, "gelu", w_in[0], 0, 8, mod_layer=0, norm="mix")
            sp.wait_ge(w_split[0], W0["forget"][0] + 1)
            with nc.allow_non_contiguous_dma(reason="eight columns"):
                sp.dma_start(w_raw[:, 0].rearrange("p (k n) -> p k n", k=KT)[:, :, 0:8],
                             w_in[0].rearrange("(k p) n -> p k n", p=P)[:, :, 20 * P:20 * P + 8]).then_inc(w_landed[0], 16)
            weight_tiles(sp, "plain", w_in[0], 8 * P, 12)
            for s in range(2):
                sp.wait_ge(stored[s], 16 * (Z0["plain"][s] + 6) + 16)
            with sp.Fori(0, 4) as j:
                sp.wait_ge(s_turned, j + 1)
                sp.dma_start(s_v[:], z1[bass.ds(j * P + 4 * P, P), :]).then_inc(s_in, 16)
                sp.dma_start(s_w[:], sg_w[0, bass.ds(2 * j, 2)].rearrange("h t s -> t h s")).then_inc(s_in, 16)
                sp.wait_ge(s_low, j + 1)
                sp.dma_start(s_u[:], z1[bass.ds(j * P, P), :]).then_inc(s_given, 16)
                for e in range(2):
                    sp.dma_start(s_b[e * DH:(e + 1) * DH, :],
                                 sg_b[0, bass.ds(2 * j + e, 1), :].broadcast_to([DH, P])).then_inc(s_given, 16)
            sp.wait_ge(f_stored, 32)
            sp.wait_ge(s_low, 4 + 1)
            with sp.Fori(0, 4) as j:
                sp.wait_ge(fa.scored, 16 * j + 1)
                sp.dma_start(a_q[:], z1[bass.ds(j * P + 8 * P, P), :]).then_inc(fa.loaded, 16)
                sp.dma_start(a_k[:], z1[bass.ds(j * P + 12 * P, P), :]).then_inc(fa.loaded, 16)
                for part in range(2):
                    sp.dma_start(a_c[part:part + 1].bitcast(F32), forget_rows[part:part + 1, bass.ds(2 * j, 2), :]).then_inc(fa.loaded, 16)
                sp.dma_start(a_vt[:], z1[bass.ds(j * P + 16 * P, P), :]).then_inc(fa.loaded, 16)
            weight_tiles(sp, "w_out", w_out[0], 0, 8)
            up = w_up[0].rearrange("(k p) n -> p k n", p=P)

            def up_tiles(chunk, e):
                for s in range(2):
                    sp.wait_ge(w_split[s], 2 * chunk + (W0["ffn"][s] + e) + 1)
                    sp.dma_start(w_raw[:, s].rearrange("p (k n) -> p k n", k=KT),
                                 up[:, :, bass.ds((2 * chunk + (s * FT + e)) * P, P)]).then_inc(w_landed[s], 16)

            def down_rows(chunk):
                for s in range(2):
                    sp.wait_ge(d_split[s], chunk + 1)
                    sp.dma_start(d_raw[:, s], w_down[0, bass.ds((2 * chunk + s) * P, P), :]).then_inc(d_landed[s], 16)

            up_tiles(0, 0)
            for s in range(2):
                sp.wait_ge(n_low[s], 4 * (SPLITS["ffn"] + 1) + 1)
            with sp.Fori(0, CHUNKS - 1) as c:
                up_tiles(c, 1)
                down_rows(c)
                up_tiles(c + 1, 0)
            up_tiles(CHUNKS - 1, 1)
            down_rows(CHUNKS - 1)
            weight_tiles(sp, "a_qk", a_w_in_2[0], 0, 16, ((n_low, 4 * (SPLITS["a"] + 1) + 1), (r_cos, const_cos), (r_sin, const_sin)))
            weight_tiles(sp, "a_v", a_w_in_2[0], 16 * P, 8, mod_layer=1)
            weight_tiles(sp, "a_gate", a_w_in_2[0], 24 * P, 8)
            for s in range(2):
                sp.wait_ge(stored[s], 16 * (Z0["a_gate"][s] + 4) + 16)
            with sp.Fori(0, DA_HEADS) as h:
                sp.wait_ge(da_scored1, 10 * h + 1)
                sp.dma_start(d_q[:], za[bass.ds(h * P, P), :]).then_inc(da.loaded, 16)
                sp.dma_start(d_k[:], za[bass.ds(h * P + 8 * P, P), :]).then_inc(da.loaded, 16)
                sp.dma_start(d_vt, za[bass.ds(h * P + 16 * P, P), :]).then_inc(da_vloaded, 16)
                sp.wait_ge(da.low, h + 1)
                sp.dma_start(d_g, za[bass.ds(h * P + 24 * P, P), :]).then_inc(da_gloaded, 16)
            sp.wait_ge(da.low, DA_HEADS + 1)
            weight_tiles(sp, "a_out", w_o_2[0], 0, 8)
            weight_tiles(sp, "b_q", b_w_in_2[0], 0, 8, ((n_low, 4 * (SPLITS["b"] + 1) + 1), (r_cos, const_cos), (r_sin, const_sin)))
            weight_tiles(sp, "b_k", b_w_in_2[0], 8 * P, 2)
            weight_tiles(sp, "b_v", b_w_in_2[0], 10 * P, 2)
            weight_tiles(sp, "b_gate", b_w_in_2[0], 12 * P, 8)
            for s in range(2):
                sp.wait_ge(stored[s], 16 * (Z0["b_gate"][s] + 4) + 16)
            with sp.Fori(0, 4) as h:
                sp.wait_ge(ba.scored, 32 * h + 1)
                sp.dma_start(b_q[:], zb[bass.ds(h * 2 * P, 2 * P), X_COLS].rearrange("(t p) n -> p t n", p=P)).then_inc(ba.loaded, 16)
                for e in range(2):
                    sp.dma_start(b_k[e * DH:(e + 1) * DH, :], zb[bass.ds(h * DH + 8 * P, DH), :]).then_inc(ba.loaded, 16)
                    sp.dma_start(b_vt[e * DH:(e + 1) * DH, :],
                                 zb[bass.ds(h * DH + 10 * P, DH), e * TOK // 2:(e + 1) * TOK // 2]).then_inc(ba.loaded, 16)
                sp.wait_ge(ba.low, 8 * h + 1)
                sp.dma_start(b_g[:], zb[bass.ds(h * 2 * P + 12 * P, 2 * P), X_COLS].rearrange("(t p) n -> p t n", p=P)).then_inc(ba_gloaded, 16)
            weight_tiles(sp, "b_out", w_o_2[1], 0, 8)
            rows_of_out = out[0].rearrange("(t p) n -> p t n", p=P)
            with sp.Fori(0, KT // 2) as i:
                for s in range(2):
                    sp.wait_ge(out_kept[s], i + 1 + 1)
                    sp.dma_start(rows_of_out[:, :, bass.ds((2 * i + s) * P, P)], tok_out[:, s]).then_inc(out_stored[s], 16)
            for s in range(2):
                sp.wait_ge(out_stored[s], 16 * (KT // 2) + 16)

        def split(pool, base, use, s):
            pool.wait_ge(w_landed[s], 16 * use + 16 * (base[s] + 1))
            pool.wait_ge(w_used[s], use + base[s] + 1)
            pool.tensor_tensor(wh[:, s], w_raw[:, s], zero[:].broadcast_to([P, KT * P]), ALU.add).then_inc(w_high[s], 1)
            pool.wait_ge(w_high[s], use + (base[s] + 1))
            pool.tensor_tensor(wl[:, s], w_raw[:, s], wh[:, s].bitcast(F32), ALU.subtract).then_inc(w_split[s], 1)

        def split_tiles(pool, name, tiles, norm=None, cols=None):
            first = 0
            if norm:
                first = 1
                for s in range(2):
                    split(pool, W0[name], 0, s)
                norm_rests(pool, norm, cols)
            with pool.Fori(first, tiles // 2) as i:
                for s in range(2):
                    split(pool, W0[name], i, s)

        def norm_rests(pool, name, cols):
            n = 4 * SPLITS[name]
            with pool.Fori(0, KT // 2) as i:
                for s in range(2):
                    pool.wait_ge(n_high[s], i + (n + 1))
                    pool.tensor_tensor(hl[:, bass.ds(2 * i + s, 1), cols], n_h[:, s:s + 1, 0:cols.stop - cols.start],
                                       hh[:, bass.ds(2 * i + s, 1), cols].bitcast(F32), ALU.subtract).then_inc(n_low[s], 1)

        @block.gpsimd
        def _(pool):
            for opened in (*w_split, *w_used, *acc_free, *mod_done, *mod_summed, *mod_kept, *n_added, *n_low, *n_gained, *out_turned, *out_kept,
                           s_turned, s_low, *d_split, d_used, r_read, r_roped, fa.scored, fa.pt_kept, fa.mixed, fa.normed, fa.kept,
                           da.scored, da_scored1, da.maxed, da_maxed1, da.mixed, da.low, *da_free,
                           ba.scored, ba.pt_kept, ba.mixed, ba.low):
                pool.sem_inc(opened, 1)
            for opened in (*stored, *out_stored):
                pool.sem_inc(opened, 16)
            pool.memset(ones[:], 1.0).then_inc(zeroed, 1)
            pool.memset(zero[:], 0.0).then_inc(zeroed, 1)
            pool.memset(ones_r[:].bitcast(F32), 1.0).then_inc(zeroed, 1)
            pool.memset(one[:], 1.0).then_inc(zeroed, 1)
            pool.memset(eps_d[:], D * EPS).then_inc(zeroed, 1)
            pool.memset(eps_1[:], EPS).then_inc(zeroed, 1)
            pool.memset(s_wt[:], 0.0).then_inc(zeroed, 1)
            pool.wait_ge(zeroed, 2)
            split_tiles(pool, "gelu", 8, "mix", X_COLS)
            split(pool, W0["forget"], 0, 0)
            split_tiles(pool, "plain", 12)
            with pool.Fori(0, 4) as j:
                pool.wait_ge(s_gated, 4 * j + 4)
                pool.tensor_tensor(hl[:, bass.ds(j, 1), X_COLS], s_y[:].unsqueeze(1),
                                   hh[:, bass.ds(j, 1), X_COLS].bitcast(F32), ALU.subtract).then_inc(s_low, 1)
            split_tiles(pool, "w_out", 8)

            def split_up(chunk, e):
                for s in range(2):
                    split(pool, W0["ffn"], 2 * chunk + e, s)

            def split_down(chunk):
                for s in range(2):
                    pool.wait_ge(d_landed[s], 16 * chunk + 16)
                    pool.wait_ge(d_used, chunk + 1)
                    pool.tensor_tensor(d_hi[:, s], d_raw[:, s], zero[:].broadcast_to([P, D]), ALU.add).then_inc(d_high[s], 1)
                    pool.wait_ge(d_high[s], chunk + 1)
                    pool.tensor_tensor(d_lo[:, s], d_raw[:, s], d_hi[:, s].bitcast(F32), ALU.subtract).then_inc(d_split[s], 1)

            def act_rest(chunk, e):
                pool.wait_ge(f_high, 2 * chunk + (e + 1))
                pool.tensor_tensor(f_lo[:, e], f_act[:], f_hi[:, e].bitcast(F32), ALU.subtract).then_inc(f_low, 1)

            split_up(0, 0)
            norm_rests(pool, "ffn", X_COLS)
            with pool.Fori(0, CHUNKS - 1) as c:
                split_up(c, 1)
                act_rest(c, 0)
                split_down(c)
                split_up(c + 1, 0)
                act_rest(c, 1)
            split_up(CHUNKS - 1, 1)
            act_rest(CHUNKS - 1, 0)
            split_down(CHUNKS - 1)
            act_rest(CHUNKS - 1, 1)
            split_tiles(pool, "a_qk", 16, "a", ALL_COLS)
            split_tiles(pool, "a_v", 8)
            split_tiles(pool, "a_gate", 8)
            with pool.Fori(0, DA_HEADS) as h:
                pool.wait_ge(da_gated, h + 1)
                pool.tensor_tensor(hl[:, bass.ds(h, 1)], d_g.unsqueeze(1), hh[:, bass.ds(h, 1)].bitcast(F32), ALU.subtract).then_inc(da.low, 1)
            split_tiles(pool, "a_out", 8)
            split_tiles(pool, "b_q", 8, "b", ALL_COLS)
            split_tiles(pool, "b_k", 2)
            split_tiles(pool, "b_v", 2)
            split_tiles(pool, "b_gate", 8)
            with pool.Fori(0, 4) as h:
                for i in range(QB):
                    cols = slice(CTX + i * P, CTX + (i + 1) * P)
                    pool.wait_ge(ba.kept, 16 * h + (2 * i + 2))
                    pool.tensor_tensor(hl[:, bass.ds(2 * h, 2), cols], b_y[:], hh[:, bass.ds(2 * h, 2), cols].bitcast(F32),
                                       ALU.subtract).then_inc(ba.low, 1)
            split_tiles(pool, "b_out", 8)

        def product(pe, out_, w_hi, w_lo, x_hi, x_lo, start, stop):
            pe.matmul(out_, w_hi, x_hi, start=start, stop=False)
            pe.matmul(out_, w_hi, x_lo, start=False, stop=False)
            return pe.matmul(out_, w_lo, x_hi, start=False, stop=stop)

        def project_tile(pe, name, i, s, segs):
            pe.wait_ge(w_split[s], i + (W0[name][s] + 1) + 1)
            pe.wait_ge(acc_free[s], i + A0[name][s] + 1)
            for k in range(KT):
                wk = slice(k * P, (k + 1) * P)
                for c0, w, p0 in segs:
                    last = product(pe, acc[s][:, p0:p0 + w], wh[:, s, wk], wl[:, s, wk],
                                   hh[:, k, c0:c0 + w], hl[:, k, c0:c0 + w], k == 0, k == KT - 1)
            last.then_inc(w_used[s], 1)

        def project_first(pe, name, segs, norm):
            lag = 3
            for s in range(2):
                pe.wait_ge(w_split[s], W0[name][s] + 1 + 1)
                pe.wait_ge(acc_free[s], A0[name][s] + 1)
            for n in range(KT + lag):
                for s, k in enumerate((n, n - lag)):
                    if not 0 <= k < KT:
                        continue
                    if s == 0:
                        pe.wait_ge(n_low[k % 2], 4 * SPLITS[norm] + k // 2 + 1 + 1)
                    wk = slice(k * P, (k + 1) * P)
                    for c0, w, p0 in segs:
                        last = product(pe, acc[s][:, p0:p0 + w], wh[:, s, wk], wl[:, s, wk],
                                       hh[:, k, c0:c0 + w], hl[:, k, c0:c0 + w], k == 0, k == KT - 1)
                    if k == KT - 1:
                        last.then_inc(w_used[s], 1)

        def project(pe, name, tiles, segs, mod_layer=None, norm=None):
            def mod_sums(i, s):
                pe.wait_ge(mod_done[s], i + (4 * mod_layer + 1) + 1)
                pe.wait_ge(mod_kept[s], i + 4 * mod_layer + 1)
                for n in range(MOD_TILES):
                    for v in range(2):
                        last = pe.matmul(bank(6 + s)[:, 2 * n + v:2 * n + v + 1], mod_acc[:, s, v, n * P:(n + 1) * P],
                                         ones[:, 0:1], start=True, stop=True)
                last.then_inc(mod_summed[s], 1)

            if norm:
                project_first(pe, name, segs, norm)
                if mod_layer is not None:
                    for s in range(2):
                        mod_sums(0, s)
            with pe.Fori(1 if norm else 0, tiles // 2) as i:
                for s in range(2):
                    project_tile(pe, name, i, s, segs)
                    if mod_layer is not None:
                        mod_sums(i, s)

        def project_rotated(pe, name, tiles, segs, norm=None):
            def swap_tile(i, s):
                pe.wait_ge(acc_free[s], i + A0[name][s] + 1 + 1)
                pe.wait_ge(r_read, 2 * i + (R0[name] + s) + 1)
                first = segs[-1][2] + segs[-1][1] - SEQ
                for c in range(0, SEQ, BANK):
                    last = pe.matmul(ps[:, 6 * BANK + c:7 * BANK + c], swap[:], z_out[:, s, first + c:first + c + BANK], start=True, stop=True)
                last.then_inc(r_swapped, 1)

            if norm:
                project_first(pe, name, segs, norm)
            else:
                project_tile(pe, name, 0, 0, segs)
                project_tile(pe, name, 0, 1, segs)
            swap_tile(0, 0)
            if tiles > 2:
                with pe.Fori(1, tiles // 2) as i:
                    project_tile(pe, name, i, 0, segs)
                    swap_tile(i - 1, 1)
                    project_tile(pe, name, i, 1, segs)
                    swap_tile(i, 0)
            swap_tile(tiles // 2 - 1, 1)

        def norm_sum(pe, name, cols):
            n, w = NORMS[name], cols.stop - cols.start
            for s in range(2):
                pe.wait_ge(n_added[s], 4 * (n + 1) + 1)
            for t in range(w // P):
                last = pe.matmul(bank(6)[:, t:t + 1], n_sum[:, t * P:(t + 1) * P], ones[:, 0:1], start=True, stop=True)
            last.then_inc(n_summed, 1)
            pe.wait_ge(n_spread, n + 1)
            for (c, size), b in zip(chunks(w), SPREAD_BANKS):
                last = pe.matmul(bank(b)[:, 0:size], ones[:], n_t[:].rearrange("p s n -> p (s n)")[:, c:c + size], start=True, stop=True)
            last.then_inc(n_rooted, 1)

        @block.tensor
        def _(pe):
            def turn_tile(out_, tile, product):
                if product:
                    return pe.matmul(out_, tile, ident[:], start=True, stop=True)
                return pe.transpose(out_, tile, ident[:])

            pe.wait_ge(consts_in, 16 * 10)

            def turn_tokens(s, use):
                pe.wait_ge(tok_in[s], 16 * use + 16)
                pe.wait_ge(tok_kept[s], use)
                for k in range(KT):
                    last = pe.transpose(acc[s][:, k * P:(k + 1) * P], tokrows[:, s, k * P:(k + 1) * P], ident[:])
                last.then_inc(tok_turned[s], 1)

            for s in range(2):
                turn_tokens(s, 0)
            with pe.Fori(0, QB // 2) as i:
                for s in range(2):
                    turn_tokens(s, i + 1)
            pe.wait_ge(rows_in, 16 * 14)
            pe.transpose(bank(6)[:, 0:V_END], rows[0:V_END, :], ident[0:V_END, 0:V_END])
            for n in range(2):
                last = pe.transpose(bank(7)[:, n * 88:(n + 1) * 88], convrows[:, n, :], ident[0:88, 0:88])
            last.then_inc(rows_turned, 1)
            norm_sum(pe, "mix", X_COLS)
            project(pe, "gelu", 8, LATENT_SEGS, 0, "mix")
            project_tile(pe, "forget", 0, 0, LATENT_SEGS)
            project(pe, "plain", 12, LATENT_SEGS)
            for s in range(2):
                pe.wait_ge(acc_free[s], A0["w_out"][s] + 1)
            with pe.Fori(0, 4) as j:
                pe.wait_ge(s_in, 32 * j + 32)
                for n in range(QB):
                    pe.transpose(ps[:, n * P:(n + 1) * P], s_v[:, n * P:(n + 1) * P], ident[:])
                for e in range(2):
                    last = pe.transpose(bank(2)[:, e * P:(e + 1) * P], s_w[:, e], ident[:])
                last.then_inc(s_turned, 1)
                pe.wait_ge(s_wt_ready, 2 * j + 2)
                pe.wait_ge(s_stats, 6 * j + 6)
                for n in range(QB):
                    last = pe.matmul(ps[:, 4 * BANK + n * 2 * P:4 * BANK + (n + 1) * 2 * P],
                                     s_ctr[:].rearrange("p (n e) d -> p n (e d)", e=2)[:, n],
                                     s_wt[:].rearrange("p e t -> p (e t)"), start=True, stop=True)
                last.then_inc(s_mixed, 1)
            pe.wait_ge(masks_ready, 3)
            pe.wait_ge(s_low, 4 + 1)
            with pe.Fori(0, 4) as j:
                pe.wait_ge(fa.loaded, 80 * j + 80)

                def fa_scores(u):
                    a, i = divmod(u, QB)
                    h, at, width = slice(a * DH, (a + 1) * DH), 2 * (u % 2) * BANK, (i + 1) * P
                    if u >= 2:
                        pe.wait_ge(fa.maxed, 16 * j + (u - 1))
                    for c in range(0, width, BANK):
                        w = min(BANK, width - c)
                        got = ps[:, at + c:at + c + w]
                        pe.matmul(got, a_q[h, i * P:(i + 1) * P], a_k[h, c:c + w], start=True, stop=False)
                        last = pe.matmul(got, ones_r[:], a_c[:, a, c:c + w], start=False, stop=(c + w < width))
                    last = pe.matmul(ps[:, at + i * P:at + width], masks[:, 0], masks[:, 1], start=False, stop=True)
                    last.then_inc(fa.scored, 1)

                def fa_mix(u):
                    a, i = divmod(u, QB)
                    pe.wait_ge(fa.pt_kept, 17 * j + (u + 2) + 1)
                    if u == 0:
                        pe.wait_ge(fa.normed, 2 * j + 1)
                    got = ps[:, 6 * BANK + i * P + a * DH:6 * BANK + i * P + (a + 1) * DH]
                    for kt in range(i + 1):
                        last = pe.matmul(got, a_pt[:, u % 2, kt], a_v[:, kt, a * DH:(a + 1) * DH], start=(kt == 0), stop=(kt == i))
                    last.then_inc(fa.mixed, 1)

                for u in range(LEAD):
                    fa_scores(u)
                pe.wait_ge(fa.pt_kept, 17 * j + 1)
                pe.wait_ge(fa.kept, 2 * j + 1)
                for n in range(QB):
                    last = turn_tile(ps[:, 4 * BANK + n * P:4 * BANK + (n + 1) * P], a_vt[:, n * P:(n + 1) * P], True)
                last.then_inc(fa.turned, 1)
                for u in range(2 * QB):
                    if u + LEAD < 2 * QB:
                        fa_scores(u + LEAD)
                    pe.wait_ge(fa.exped, 16 * j + (u + 1))
                    pe.wait_ge(fa.pt_kept, 17 * j + (u + 1) + 1)
                    for kt in range(u % QB + 1):
                        last = turn_tile(ps[:, 4 * BANK + kt * P:4 * BANK + (kt + 1) * P],
                                         a_s[:, u % 3, kt * P:(kt + 1) * P], False)
                    last.then_inc(fa.turned, 1)
                    if u:
                        fa_mix(u - 1)
                fa_mix(2 * QB - 1)
                pe.wait_ge(fa.normed, 2 * j + 2 + 1)
                for i in range(QB):
                    last = turn_tile(ps[:, 4 * BANK + i * P:4 * BANK + (i + 1) * P], a_o[:, i].rearrange("p a d -> p (a d)"), True)
                last.then_inc(fa.turned, 1)
            pe.wait_ge(fa.kept, 8 + 1)
            project(pe, "w_out", 8, LATENT_SEGS)
            norm_sum(pe, "ffn", X_COLS)

            def ffn_up(chunk, e, acc_use):
                for s in range(2):
                    pe.wait_ge(w_split[s], 2 * chunk + (W0["ffn"][s] + e + 1) + 1)
                    pe.wait_ge(acc_free[s], acc_use + A0["ffn"][s] + 1)
                    for k in range(KT):
                        wk = slice(k * P, (k + 1) * P)
                        for c0, w, p0 in LATENT_SEGS:
                            last = product(pe, acc[s][:, p0:p0 + w], wh[:, s, wk], wl[:, s, wk],
                                           hh[:, k, c0:c0 + w], hl[:, k, c0:c0 + w], k == 0, k == KT - 1)
                    last.then_inc(w_used[s], 1)

            def ffn_down(chunk, acc_use):
                pe.wait_ge(f_low, 2 * chunk + 2)
                for s in range(2):
                    pe.wait_ge(d_split[s], chunk + 1 + 1)
                for m in range(KT):
                    s, wm = m % 2, slice(m * P, (m + 1) * P)
                    pe.wait_ge(acc_free[s], acc_use + (A0["ffn"][s] + m // 2) + 1)
                    for e in range(2):
                        for c in range(0, SEQ, BANK):
                            last = product(pe, acc[s][:, c:c + BANK], d_hi[:, e, wm], d_lo[:, e, wm],
                                           f_hi[:, e, c:c + BANK], f_lo[:, e, c:c + BANK], e == 0, e == 1)
                    last.then_inc(f_down if m < KT - 1 else d_used, 1)

            project_first(pe, "ffn", LATENT_SEGS, "ffn")
            ffn_up(0, 1, 1)
            with pe.Fori(1, CHUNKS) as c:
                ffn_up(c, 0, 6 * c - 4)
                ffn_down(c - 1, 6 * c - 3)
                ffn_up(c, 1, 6 * c + 1)
            ffn_down(CHUNKS - 1, 6 * CHUNKS - 4)
            norm_sum(pe, "fin", X_COLS)
            norm_sum(pe, "a", ALL_COLS)
            project_rotated(pe, "a_qk", 16, ALL_SEGS, "a")
            pe.wait_ge(r_read, R0["b_q"] + 1)
            project(pe, "a_v", 8, ALL_SEGS, 1)
            project(pe, "a_gate", 8, ALL_SEGS)
            for s in range(2):
                pe.wait_ge(acc_free[s], A0["a_out"][s] + 1)
            def da_turn_tiles(h, src, blocks, *key):
                b, before, _ = da_turn(h, *key)
                pe.wait_ge(da_free[b], before + 1)
                for n, kt in enumerate(blocks):
                    last = turn_tile(bank(6 + b)[:, n * P:(n + 1) * P], src(kt), key[0] != "p")
                last.then_inc(da.turned, 1)

            def da_scores(h, u, m):
                done, read = ((da.scored, da.maxed), (da_scored1, da_maxed1))[m]
                pe.wait_ge(read, 10 * h + u + 1)
                r, width = slice(m * DH, (m + 1) * DH), da_tiles(u) * P
                for c in range(0, width, BANK):
                    w = min(BANK, width - c)
                    last = pe.matmul(acc[m][:, c:c + w], d_q[r, u * P:(u + 1) * P], d_k[r, c:c + w], start=True, stop=True)
                last.then_inc(done, 1)

            def da_mix(h, u):
                nk = da_tiles(u)
                for n in range(len(batches(nk)))[-2:]:
                    b, before, _ = da_turn(h, "p", u, n)
                    pe.wait_ge(da_free[b], before + 1 + 1)
                b, before, _ = da_turn(h, "m", u)
                pe.wait_ge(da_free[b], before + 1)
                for kt in range(nk):
                    last = pe.matmul(bank(6 + b)[:, 0:P], d_pt[:, u % 2, kt, :], d_v[:, kt, :], start=(kt == 0), stop=(kt == nk - 1))
                last.then_inc(da.mixed, 1)

            def da_turn_output(h):
                pe.wait_ge(da.normed, 4 * h)
                for n, blocks in enumerate(batches(TOK // P)):
                    da_turn_tiles(h, lambda u: d_o[:, u], blocks, "o", n)

            def da_head(h, first):
                pe.wait_ge(da.loaded, 32 * h + 32)
                for u in range(LEAD):
                    for m in range(2):
                        da_scores(h, u, m)
                pe.wait_ge(da_vloaded, 16 * h + 16)
                for n, blocks in enumerate(batches(TOK // P)):
                    da_turn_tiles(h, lambda kt: d_vt[:, kt * P:(kt + 1) * P], blocks, "v", n)
                for u in range(TOK // P):
                    ahead = [m for m in range(2) if u + LEAD < TOK // P]
                    if ahead:
                        da_scores(h, u + LEAD, ahead.pop(0))
                    pe.wait_ge(da_weighed, 30 * h + (3 * u + 3))
                    for n, blocks in enumerate(batches(da_tiles(u))):
                        if n == 2:
                            da_mix(h, u - 1)
                        da_turn_tiles(h, lambda kt: d_p0[:, u % 3, kt * P:(kt + 1) * P], blocks, "p", u, n)
                        if ahead:
                            da_scores(h, u + LEAD, ahead.pop(0))
                    if u == 1 and not first:
                        da_turn_output(h)
                    if u == 1:
                        da_mix(h, 0)
                da_mix(h, TOK // P - 1)

            da_head(0, True)
            with pe.Fori(1, DA_HEADS) as h:
                da_head(h, False)
            da_turn_output(DA_HEADS)
            pe.wait_ge(da.low, DA_HEADS + 1)
            project(pe, "a_out", 8, ALL_SEGS)
            norm_sum(pe, "b", ALL_COLS)
            project_rotated(pe, "b_q", 8, LATENT_SEGS, "b")
            project_rotated(pe, "b_k", 2, ALL_SEGS)
            project(pe, "b_v", 2, ALL_SEGS)
            project(pe, "b_gate", 8, LATENT_SEGS)
            for s in range(2):
                pe.wait_ge(acc_free[s], A0["b_out"][s] + 1)
            with pe.Fori(0, 4) as h:
                def ba_scores(u):
                    i, a = divmod(u, 4)
                    r, t, at = slice((a % 2) * DH, (a % 2 + 1) * DH), a // 2, 2 * (u % 2) * BANK
                    if u >= 2:
                        pe.wait_ge(ba.maxed, 32 * h + (u - 1))
                    for n, kt in enumerate(window_tiles(i)):
                        if kt == 1:
                            continue
                        w, side = CTX if kt == 0 else P, kt - (2 + i) if kt else 0
                        got = ps[:, at + n * P:at + n * P + w]
                        last = pe.matmul(got, b_q[r, t, i * P:(i + 1) * P], b_k[r, kt * P:kt * P + w], start=True, stop=(side == 0))
                        if side:
                            last = pe.matmul(got, masks[:, 0], masks[:, 2 if side < 0 else 1], start=False, stop=True)
                    last.then_inc(ba.scored, 1)

                def ba_mix(u):
                    i, a = divmod(u, 4)
                    tiles = window_tiles(i)
                    pe.wait_ge(ba.pt_kept, 33 * h + (u + 2) + 1)
                    for n, kt in enumerate(tiles):
                        last = pe.matmul(bank(6 + i % 2)[:, a * DH:(a + 1) * DH], b_pt[:, u % 2, n, :], b_v[:, kt % 5, kt // 5, :],
                                         start=(n == 0), stop=(n == len(tiles) - 1))
                    last.then_inc(ba.mixed, 1)

                def ba_turn_output(i):
                    pe.wait_ge(ba.normed, 24 * h + (3 * i + 3))
                    for t in range(2):
                        last = turn_tile(bank(6 + i % 2)[:, (2 + t) * P:(3 + t) * P], b_o[:, t * P:(t + 1) * P], True)
                    last.then_inc(ba_o_turned, 1)

                pe.wait_ge(ba.loaded, 80 * h + 80)
                for u in range(LEAD):
                    ba_scores(u)
                pe.wait_ge(ba.pt_kept, 33 * h + 1)
                for n in range(TOK // 2 // P):
                    last = turn_tile(ps[:, 4 * BANK + n * P:4 * BANK + (n + 1) * P], b_vt[:, n * P:(n + 1) * P], True)
                last.then_inc(ba.turned, 1)
                for u in range(4 * QB):
                    i, a = divmod(u, 4)
                    if u + LEAD < 4 * QB:
                        ba_scores(u + LEAD)
                    pe.wait_ge(ba.exped, 64 * h + (2 * u + 1))
                    pe.wait_ge(ba.pt_kept, 33 * h + (u + 1) + 1)
                    for n in range(len(window_tiles(i))):
                        last = turn_tile(ps[:, 4 * BANK + n * P:4 * BANK + (n + 1) * P], b_s[:, u % 3, n * P:(n + 1) * P], n % 2 == 1)
                    last.then_inc(ba.turned, 1)
                    if i and a == 1:
                        ba_turn_output(i - 1)
                    if u:
                        ba_mix(u - 1)
                ba_mix(4 * QB - 1)
                ba_turn_output(QB - 1)
            pe.wait_ge(ba.low, 32 + 1)
            project(pe, "b_out", 8, LATENT_SEGS)
            norm_sum(pe, "out", X_COLS)
            with pe.Fori(0, KT // 2) as i:
                for s in range(2):
                    pe.wait_ge(n_gained[s], i + 4 * NORMS["out"] + 1 + 1)
                    pe.wait_ge(out_kept[s], i + 1)
                    for t in range(QB):
                        last = pe.transpose(acc[s][:, t * P:(t + 1) * P], n_h[:, s, t * P:(t + 1) * P], ident[:])
                    last.then_inc(out_turned[s], 1)

        def norm_root(act, name, cols, before=None):
            n, w = NORMS[name], cols.stop - cols.start
            with act.Fori(0, KT // 2) as i:
                for s in range(2):
                    if before is not None:
                        act.wait_ge(acc_free[s], i + (before[s] + 1) + 1)
                    act.wait_ge(n_added[s], i + 4 * n + 1)
                    act.activation(n_sq[:, s:s + 1, 0:w], res[:, bass.ds(2 * i + s, 1), cols], ACT.Square).then_inc(n_squared[s], 1)
            act.wait_ge(n_summed, n + 1)
            act.activation(n_col[:, 0:w // P], bank(6)[:, 0:w // P], ACT.Sqrt, bias=eps_d[:]).then_inc(n_root, 1)

        def norm_gain(act, name, parts):
            n, first = NORMS[name], parts[0][0].start
            with act.Fori(0, KT // 2) as i:
                for s in range(2):
                    k = 2 * i + s
                    act.wait_ge(n_times[s], i + (4 * n + 1))
                    if name in SPLITS:
                        act.wait_ge(n_low[s], i + 4 * SPLITS[name] + 1)
                    elif name == "out":
                        act.wait_ge(out_turned[s], i + 1)
                    for cols, gain, shift in parts:
                        at = slice(cols.start - first, cols.stop - first)
                        to = res[:, bass.ds(k, 1), cols] if name == "fin" else n_h[:, s:s + 1, at]
                        ins = act.activation(to, n_t[:, s:s + 1, at], ACT.Identity, bias=shift(k), scale=gain(k))
                    ins.then_inc(n_gained[s], 1)

        def keep(act, name, rows, row0, tiles, cols, func):
            w = cols.stop - cols.start
            with act.Fori(0, tiles // 2) as i:
                for s in range(2):
                    act.wait_ge(w_used[s], i + (W0[name][s] + 1) + 1)
                    act.wait_ge(stored[s], 16 * i + 16 * Z0[name][s] + 16)
                    act.activation(z_out[:, s, 0:w], acc[s][:, 0:w], func).then_inc(acc_free[s], 1)
                    act.wait_ge(acc_free[s], i + (A0[name][s] + 1) + 1)
                    act.dma_start(rows[bass.ds((2 * i + s) * P + row0, P), cols], z_out[:, s, 0:w]).then_inc(stored[s], 16)

        def keep_rotated(act, name, rows, row0, tiles, cols):
            w = cols.stop - cols.start

            def copy(i, s):
                act.wait_ge(w_used[s], i + (W0[name][s] + 1) + 1)
                act.wait_ge(stored[s], 16 * i + 16 * Z0[name][s] + 16)
                act.activation(z_out[:, s, 0:w], acc[s][:, 0:w], ACT.Copy).then_inc(acc_free[s], 1)

            def store(i, s):
                act.wait_ge(r_roped, 2 * i + (R0[name] + s + 1) + 1)
                act.dma_start(rows[bass.ds((2 * i + s) * P + row0, P), cols], z_out[:, s, 0:w]).then_inc(stored[s], 16)

            copy(0, 0)
            copy(0, 1)
            store(0, 0)
            if tiles > 2:
                with act.Fori(1, tiles // 2) as i:
                    copy(i, 0)
                    store(i - 1, 1)
                    copy(i, 1)
                    store(i, 0)
            store(tiles // 2 - 1, 1)

        def vec_gain(at):
            return lambda k: vec32[:, bass.ds(k + at, 1)]

        def no_shift(k):
            return zero[:]

        def mod_gain(layer, v):
            return lambda k: modg[:, layer, v, bass.ds(k, 1)]

        def mod_shift(layer, v):
            return lambda k: mod[:, bass.ds(k + 24 * layer, 1), v]

        @block.scalar
        def _(act):
            act.wait_ge(zeroed, 7)
            act.wait_ge(vec_ready, 2)
            for v in range(2):
                act.activation(cond[:, :, v], vec[:, V_C + v * KT:V_C + (v + 1) * KT], ACT.Silu).then_inc(cond_ready, 1)
            act.wait_ge(lam_step, 2)
            act.activation(lamt[:, 2:4], lamt[:, 0:2], ACT.Exp).then_inc(lam_exp, 1)
            for s in range(2):
                act.wait_ge(tok_kept[s], 5)
            act.wait_ge(masks_ready, 3)
            act.wait_ge(lam_step, 3)
            act.wait_ge(vec32_ready, 2)
            norm_root(act, "mix", X_COLS)
            norm_gain(act, "mix", ((X_COLS, vec_gain(V_MIX), no_shift),))
            for s in range(2):
                act.wait_ge(n_low[s], 4 * (SPLITS["mix"] + 1) + 1)
            keep(act, "gelu", z1, 0, 8, slice(0, SEQ), ACT.Gelu)
            act.wait_ge(w_used[0], W0["forget"][0] + 1 + 1)
            act.activation(f_x[:], acc[0][0:8, 0:SEQ], ACT.Identity, bias=fb[:]).then_inc(acc_free[0], 1)
            act.wait_ge(acc_free[0], A0["forget"][0] + 1 + 1)
            act.activation(f_a[:], f_x[:], ACT.Abs).then_inc(f_soft, 1)
            act.wait_ge(f_soft, 1)
            act.activation(f_a[:], f_a[:], ACT.Exp, scale=-1.0).then_inc(f_soft, 1)
            act.wait_ge(f_soft, 2)
            act.activation(f_a[:], f_a[:], ACT.Ln, bias=one[0:8, :]).then_inc(f_soft, 1)
            keep(act, "plain", z1, 8 * P, 12, slice(0, SEQ), ACT.Copy)
            act.wait_ge(f_scan, 24)
            for part in range(2):
                act.dma_start(forget_rows[part], f_parts[:, part].bitcast(F32)).then_inc(f_stored, 16)
            with act.Fori(0, 4) as j:
                act.wait_ge(s_turned, j + 1 + 1)
                turned = bank(2)[:, 0:2 * P].rearrange("p (e t) -> p e t", e=2)
                act.activation(s_wt[0:64, :, :], turned[0:64], ACT.Copy).then_inc(s_wt_ready, 1)
                act.activation(s_wt[64:P, :, 64:P], turned[64:P, :, 64:P], ACT.Copy).then_inc(s_wt_ready, 1)
                act.wait_ge(s_stats, 6 * j + 3)
                act.activation(s_sq[:], s_ctr[:], ACT.Square).then_inc(s_squared, 1)
                act.wait_ge(s_stats, 6 * j + 4)
                act.activation(s_stat[:, 3], s_stat[:, 2], ACT.Sqrt, bias=eps_1[:], scale=1.0 / DH).then_inc(s_std, 1)
            with act.Fori(0, 4) as j:
                def fa_exp(u):
                    a, i = divmod(u, QB)
                    s, w = u % 3, (i + 1) * P
                    act.wait_ge(fa.maxed, 16 * j + (u + 1))
                    act.activation(a_s[:, s, 0:w], a_s[:, s, 0:w], ACT.Exp, bias=a_low[:, s:s + 1], scale=-1.0,
                                   accum_out=a_sum[:, a, i:i + 1]).then_inc(fa.exped, 1)

                for u in range(LEAD):
                    fa_exp(u)
                act.wait_ge(fa.turned, 18 * j + 1)
                act.wait_ge(fa.mixed, 16 * j + 1)
                act.activation(a_v[:].rearrange("p k d -> p (k d)"), bank(4, 2), ACT.Copy).then_inc(fa.pt_kept, 1)
                for u in range(2 * QB):
                    i = u % QB
                    act.wait_ge(fa.turned, 18 * j + (u + 2))
                    if u >= 2:
                        act.wait_ge(fa.mixed, 16 * j + (u - 1) + 1)
                    act.activation(a_pt[:, u % 2, 0:i + 1, :],
                                   ps[:, 4 * BANK:4 * BANK + (i + 1) * P].rearrange("p (k q) -> p k q", q=P),
                                   ACT.Copy).then_inc(fa.pt_kept, 1)
                    if u + LEAD < 2 * QB:
                        fa_exp(u + LEAD)
            norm_root(act, "ffn", X_COLS, A0["w_out"])
            norm_gain(act, "ffn", ((X_COLS, vec_gain(V_FFN), no_shift),))
            for s in range(2):
                act.wait_ge(n_low[s], 4 * (SPLITS["ffn"] + 1) + 1)

            def ffn_up(chunk, e, acc_use):
                for s in range(2):
                    tile = 2 * chunk + (s * FT + e)
                    act.wait_ge(w_used[s], 2 * chunk + (W0["ffn"][s] + e + 1) + 1)
                    act.wait_ge(f_mult, 2 * chunk + e)
                    act.activation(f_y[:, s], acc[s][:, 0:SEQ], ACT.Identity, bias=convv[:, bass.ds(tile + 6 * FT, 1)],
                                   scale=convv[:, bass.ds(tile + 4 * FT, 1)]).then_inc(f_based[s], 1)
                act.wait_ge(acc_free[0], acc_use + (A0["ffn"][0] + 1) + 1)
                act.activation(f_g[:], f_y[:, 0], ACT.Silu).then_inc(f_gate, 1)

            ffn_up(0, 0, 0)
            ffn_up(0, 1, 1)
            with act.Fori(1, CHUNKS) as c:
                ffn_up(c, 0, 6 * c - 4)
                ffn_up(c, 1, 6 * c + 1)
            norm_root(act, "fin", X_COLS, [n - KT // 2 for n in A0["a_qk"]])
            norm_gain(act, "fin", ((X_COLS, vec_gain(V_FIN), no_shift),))
            for s in range(2):
                act.wait_ge(n_gained[s], 4 * (NORMS["fin"] + 1) + 1)
            act.wait_ge(modg_ready, 2)
            norm_root(act, "a", ALL_COLS)
            norm_gain(act, "a", ((slice(0, CTX), mod_gain(0, 1), mod_shift(0, 1)), (X_COLS, mod_gain(0, 0), mod_shift(0, 0))))
            for s in range(2):
                act.wait_ge(n_low[s], 4 * (SPLITS["a"] + 1) + 1)
            keep_rotated(act, "a_qk", za, 0, 16, slice(0, TOK))
            keep(act, "a_v", za, 16 * P, 8, slice(0, TOK), ACT.Copy)
            keep(act, "a_gate", za, 24 * P, 8, slice(0, TOK), ACT.Silu)
            def da_exp(h, u):
                w, s = da_tiles(u) * P, u % 3
                for m, (p, at, maxed, done) in enumerate(((d_p0, s, da.maxed, da.exped), (d_p1, u % 2, da_maxed1, da_exped1))):
                    act.wait_ge(maxed, 10 * h + (u + 1) + 1)
                    act.activation(p[:, at, 0:w], p[:, at, 0:w], ACT.Exp, bias=d_low[:, s, m:m + 1], scale=-1.0,
                                   accum_out=d_sum[:, m, u:u + 1]).then_inc(done, 1)

            def da_keep_out(h, u, first):
                act.wait_ge(da.mixed, 10 * h + (u + 1) + 1)
                if u == 0 and not first:
                    act.wait_ge(da.turned, da_turn(h, "o", len(batches(TOK // P)) - 1)[2])
                b, _, _ = da_turn(h, "m", u)
                act.activation(d_o[:, u], bank(6 + b)[:, 0:P], ACT.Copy).then_inc(da.kept, 1)
                act.wait_ge(da.kept, 10 * h + (u + 1))
                act.activation(d_sq[:], d_o[:, u], ACT.Square, accum_out=d_ss[:, u:u + 1]).then_inc(da_free[b], 1)

            def da_root(h):
                act.wait_ge(da.normed, 4 * h - 2)
                act.activation(d_rs[:], d_rs[:], ACT.Sqrt).then_inc(da_rms, 1)

            def da_head(h, first):
                for u in range(LEAD):
                    da_exp(h, u)
                if not first:
                    da_root(h)
                act.wait_ge(da.mixed, 10 * h + 1)
                for n, blocks in enumerate(batches(TOK // P)):
                    b, _, turned = da_turn(h, "v", n)
                    act.wait_ge(da.turned, turned)
                    act.activation(d_v[:, blocks.start:blocks.stop, :],
                                   bank(6 + b)[:, 0:len(blocks) * P].rearrange("p (k d) -> p k d", d=P), ACT.Copy).then_inc(da_free[b], 1)
                for u in range(TOK // P):
                    if u >= 2:
                        act.wait_ge(da.mixed, 10 * h + (u - 1) + 1)
                    for n, blocks in enumerate(batches(da_tiles(u))):
                        if n == 2:
                            da_keep_out(h, u - 1, first)
                        b, _, turned = da_turn(h, "p", u, n)
                        act.wait_ge(da.turned, turned)
                        act.activation(d_pt[:, u % 2, blocks.start:blocks.stop, :],
                                       bank(6 + b)[:, 0:len(blocks) * P].rearrange("p (k q) -> p k q", q=P),
                                       ACT.Copy).then_inc(da_free[b], 1)
                    if u == 1:
                        da_keep_out(h, 0, first)
                    if u + LEAD < TOK // P:
                        da_exp(h, u + LEAD)
                da_keep_out(h, TOK // P - 1, first)

            da_head(0, True)
            with act.Fori(1, DA_HEADS) as h:
                da_head(h, False)
            da_root(DA_HEADS)
            act.wait_ge(modg_ready, 4)
            norm_root(act, "b", ALL_COLS, A0["a_out"])
            norm_gain(act, "b", ((slice(0, CTX), mod_gain(1, 1), mod_shift(1, 1)), (X_COLS, mod_gain(1, 0), mod_shift(1, 0))))
            for s in range(2):
                act.wait_ge(n_low[s], 4 * (SPLITS["b"] + 1) + 1)
            keep_rotated(act, "b_q", zb[:, X_COLS], 0, 8, slice(0, SEQ))
            keep_rotated(act, "b_k", zb, 8 * P, 2, slice(0, TOK))
            keep(act, "b_v", zb, 10 * P, 2, slice(0, TOK), ACT.Copy)
            keep(act, "b_gate", zb[:, X_COLS], 12 * P, 8, slice(0, SEQ), ACT.Silu)
            with act.Fori(0, 4) as h:
                def ba_exp(u):
                    i, a = divmod(u, 4)
                    s, w = u % 3, len(window_tiles(i)) * P
                    act.wait_ge(ba_biased, 32 * h + (u + 1))
                    act.activation(b_s[:, s, 0:w], b_s[:, s, 0:w], ACT.Exp, bias=b_low[:, 1, s:s + 1], scale=-1.0,
                                   accum_out=b_sum[:, i % 2, a:a + 1]).then_inc(ba.exped, 1)
                    act.activation(b_sink[:, i % 2, a:a + 1], sinks[:, bass.ds(4 * h + a, 1)], ACT.Exp,
                                   bias=b_low[:, 1, s:s + 1]).then_inc(ba.exped, 1)

                for u in range(LEAD):
                    ba_exp(u)
                act.wait_ge(ba.turned, 33 * h + 1)
                act.wait_ge(ba.mixed, 32 * h + 1)
                act.activation(b_v[:].rearrange("p n e d -> p (n e d)"), ps[:, 4 * BANK:4 * BANK + TOK // 2], ACT.Copy).then_inc(ba.pt_kept, 1)
                for u in range(4 * QB):
                    nk = len(window_tiles(u // 4))
                    act.wait_ge(ba.turned, 33 * h + (u + 2))
                    if u >= 2:
                        act.wait_ge(ba.mixed, 32 * h + (u - 1) + 1)
                    act.activation(b_pt[:, u % 2, 0:nk, :],
                                   ps[:, 4 * BANK:4 * BANK + nk * P].rearrange("p (k q) -> p k q", q=P),
                                   ACT.Copy).then_inc(ba.pt_kept, 1)
                    if u + LEAD < 4 * QB:
                        ba_exp(u + LEAD)
            norm_root(act, "out", X_COLS, A0["b_out"])
            norm_gain(act, "out", ((X_COLS, vec_gain(V_FG2), no_shift),))

        def norm_start(dve, name, cols):
            dve.memset(n_sum[:, 0:cols.stop - cols.start], 0.0).then_inc(n_zeroed, 1)

        def norm_add(dve, name, cols, i, s):
            n, w = NORMS[name], cols.stop - cols.start
            dve.wait_ge(n_zeroed, n + 1)
            dve.wait_ge(n_squared[s], i + (4 * n + 1))
            dve.wait_ge(n_added[1 - s], i + (4 * n + s) + 1)
            dve.tensor_tensor(n_sum[:, 0:w], n_sum[:, 0:w], n_sq[:, s, 0:w], ALU.add).then_inc(n_added[s], 1)

        def norm_add_all(dve, name, cols):
            norm_start(dve, name, cols)
            with dve.Fori(0, KT // 2) as i:
                for s in range(2):
                    norm_add(dve, name, cols, i, s)

        def norm_scale(dve, name, cols):
            n, w = NORMS[name], cols.stop - cols.start
            dve.wait_ge(n_root, n + 1)
            dve.reciprocal(n_col[:, 0:w // P], n_col[:, 0:w // P]).then_inc(n_scaled, 1)
            dve.wait_ge(n_scaled, n + 1)
            dve.tensor_tensor(n_t[:].rearrange("p s n -> p (s n)")[:, 0:w].rearrange("p (t n) -> p t n", n=P),
                              ident[:].unsqueeze(1).broadcast_to([P, w // P, P]),
                              n_col[:, 0:w // P].unsqueeze(2).broadcast_to([P, w // P, P]), ALU.mult).then_inc(n_spread, 1)
            dve.wait_ge(n_rooted, n + 1)
            for (c, size), b in zip(chunks(w), SPREAD_BANKS):
                last = dve.tensor_copy(n_rs[:, c:c + size], bank(b)[:, 0:size])
            last.then_inc(n_kept, 1)
            dve.wait_ge(n_kept, n + 1)
            with dve.Fori(0, KT // 2) as i:
                for s in range(2):
                    dve.wait_ge(n_gained[s], i + 4 * n + 1)
                    dve.tensor_tensor(n_t[:, s:s + 1, 0:w], res[:, bass.ds(2 * i + s, 1), cols], n_rs[:, 0:w].unsqueeze(1),
                                      ALU.mult).then_inc(n_times[s], 1)
                if name in SPLITS:
                    for s in range(2):
                        dve.wait_ge(n_gained[s], i + (4 * n + 1) + 1)
                        dve.tensor_copy(hh[:, bass.ds(2 * i + s, 1), cols], n_h[:, s:s + 1, 0:w]).then_inc(n_high[s], 1)
                elif name == "out":
                    for s in range(2):
                        dve.wait_ge(out_turned[s], i + 1 + 1)
                        dve.wait_ge(out_stored[s], 16 * i + 16)
                        dve.tensor_copy(tok_out[:, s], acc[s][:, 0:SEQ].rearrange("p (t n) -> p t n", n=P)).then_inc(out_kept[s], 1)

        def add_to_residual(dve, name, parts, norm, norm_cols):
            norm_start(dve, norm, norm_cols)
            with dve.Fori(0, KT // 2) as i:
                for s in range(2):
                    dve.wait_ge(w_used[s], i + (W0[name][s] + 1) + 1)
                    for n, (cols, p0, gate) in enumerate(parts):
                        at = res[:, bass.ds(2 * i + s, 1), cols]
                        got = acc[s][:, p0:p0 + cols.stop - cols.start].unsqueeze(1)
                        if gate is None:
                            ins = dve.tensor_tensor(at, got, at, ALU.add)
                        else:
                            layer, v = gate
                            ins = dve.scalar_tensor_tensor(at, got, mod[:, bass.ds(2 * i + (s + 24 * layer + 16), 1), v], at,
                                                           ALU.mult, ALU.add)
                        if n == len(parts) - 1:
                            ins.then_inc(acc_free[s], 1)
                    norm_add(dve, norm, norm_cols, i, s)

        def rotate(dve, name, tiles, first):
            cols = slice(first, first + SEQ)
            with dve.Fori(0, tiles // 2) as i:
                for s in range(2):
                    n = 2 * i + (R0[name] + s)
                    dve.wait_ge(r_swapped, n + 1)
                    dve.wait_ge(r_roped, n + 1)
                    dve.tensor_tensor(r_rot[:], bank(6, 2), r_sin[:], ALU.mult).then_inc(r_read, 1)
                    dve.tensor_tensor(z_out[:, s, cols], z_out[:, s, cols], r_cos[:], ALU.mult).then_inc(r_turned, 1)
                    dve.wait_ge(r_read, n + 1 + 1)
                    dve.wait_ge(r_turned, n + 1)
                    dve.tensor_tensor(z_out[:, s, cols], z_out[:, s, cols], r_rot[:], ALU.add).then_inc(r_roped, 1)

        def keep_modulation(dve, layer):
            dve.wait_ge(cond_ready, 2)
            with dve.Fori(0, 4) as i:
                for s in range(2):
                    done = 30 * i + (15 * s + 120 * layer)
                    dve.wait_ge(mod_in[s], 16 * i + 16 * (4 * layer + 1))
                    dve.wait_ge(mod_summed[s], i + 4 * layer + 1)
                    for k in range(KT):
                        for v in range(2):
                            to, w = mod_acc[:, s, v], w_mod_sb[:, s, k]
                            if k == 0:
                                dve.tensor_scalar(to, w, cond[:, k, v:v + 1], None, ALU.mult).then_inc(mod_mult, 1)
                            else:
                                dve.wait_ge(mod_mult, done + (2 * k + v - 1))
                                dve.scalar_tensor_tensor(to, w, cond[:, k, v:v + 1], to, ALU.mult, ALU.add).then_inc(
                                    *((mod_mult, 1) if k < KT - 1 or v == 0 else (mod_done[s], 1)))
                for s in range(2):
                    t = 2 * MOD_TILES * i + (MOD_TILES * s + 24 * layer)
                    dve.wait_ge(mod_summed[s], i + (4 * layer + 1) + 1)
                    dve.tensor_tensor(mod[:, bass.ds(t, MOD_TILES), :], bank(6 + s)[:, 0:2 * MOD_TILES].rearrange("p (t v) -> p t v", v=2),
                                      vec[:, bass.ds(t + V_BMOD, MOD_TILES)].unsqueeze(2).broadcast_to([P, MOD_TILES, 2]),
                                      ALU.add).then_inc(mod_kept[s], 1)
            for s in range(2):
                dve.wait_ge(mod_kept[s], 4 * layer + 4 + 1)
            for v in range(2):
                dve.scalar_tensor_tensor(modg[:, layer, v], mod[:, 24 * layer + 8:24 * layer + 16, v], 1.0,
                                         vec32[:, V_G2 + KT * layer:V_G2 + KT * (layer + 1)], ALU.add,
                                         ALU.mult).then_inc(modg_ready, 1)

        @block.vector
        def _(dve):
            def keep_tokens(s, use, col):
                dve.wait_ge(tok_turned[s], use + 1)
                dve.tensor_copy(res[:, :, bass.ds(col, P)],
                                acc[s][:, 0:KT * P].rearrange("p (k t) -> p k t", t=P)).then_inc(tok_kept[s], 1)

            for s in range(2):
                keep_tokens(s, 0, s * P)
            with dve.Fori(0, QB // 2) as i:
                for s in range(2):
                    keep_tokens(s, i + 1, (2 * i + s) * P + CTX)
            dve.wait_ge(rows_turned, 1)
            dve.tensor_copy(vec[:], bank(6)[:, 0:V_END]).then_inc(vec_ready, 1)
            dve.tensor_copy(convv[:], bank(7)[:, 0:4 * 2 * FT]).then_inc(vec_ready, 1)
            dve.wait_ge(consts_in, 16 * 10)
            for n in range(2):
                dve.tensor_tensor_reduce(lamrows[:, 2 * n], lamrows[:, 2 * n], lamrows[:, 2 * n + 1], 1.0, 0.0, ALU.mult,
                                         ALU.add, lamt[:, n:n + 1]).then_inc(lam_step, 1)
            for n, rows_ in enumerate((ident[:], maskrows[:, 0], maskrows[:, 1])):
                dve.tensor_copy(masks[:, n], rows_).then_inc(masks_ready, 1)
            dve.wait_ge(vec_ready, 2)
            dve.tensor_scalar(vec32[:], vec[:, 0:V_BMOD], float(D) ** 0.5, None, ALU.mult).then_inc(vec32_ready, 1)
            dve.tensor_scalar(subg[:], vec[:, V_SUB:V_SUB + 1], 1.0 - LAM_INIT, None, ALU.mult).then_inc(vec32_ready, 1)
            dve.wait_ge(lam_exp, 1)
            dve.scalar_tensor_tensor(neg_lam[:], lamt[:, 3:4], LAM_INIT, lamt[:, 2:3], ALU.subtract, ALU.subtract).then_inc(lam_step, 1)
            for s in range(2):
                dve.wait_ge(tok_kept[s], 5)
            dve.wait_ge(masks_ready, 3)
            dve.wait_ge(lam_step, 3)
            norm_add_all(dve, "mix", X_COLS)
            norm_scale(dve, "mix", X_COLS)
            dve.wait_ge(vec32_ready, 2)
            for s in range(2):
                dve.wait_ge(n_low[s], 4 * (SPLITS["mix"] + 1) + 1)
            keep_modulation(dve, 0)
            dve.wait_ge(f_soft, 3)
            dve.scalar_tensor_tensor(f_s[:, 0], f_x[:], 0.0, f_a[:], ALU.min, ALU.subtract).then_inc(f_scan, 1)
            for n in range(10):
                a, b, d = n % 2, 1 - n % 2, 1 << n
                dve.wait_ge(f_scan, 2 * n + 1)
                dve.tensor_copy(f_s[:, b, 0:d], f_s[:, a, 0:d]).then_inc(f_scan, 1)
                dve.tensor_tensor(f_s[:, b, d:], f_s[:, a, d:], f_s[:, a, 0:SEQ - d], ALU.add).then_inc(f_scan, 1)
            dve.wait_ge(f_scan, 21)
            dve.tensor_scalar(f_x[:], f_s[:, 0], -1.0 / SCALE, None, ALU.mult).then_inc(f_scan, 1)
            dve.wait_ge(f_scan, 22)
            dve.tensor_copy(f_parts[:, 0], f_x[:]).then_inc(f_scan, 1)
            dve.wait_ge(f_scan, 23)
            dve.tensor_tensor(f_parts[:, 1], f_x[:], f_parts[:, 0].bitcast(F32), ALU.subtract).then_inc(f_scan, 1)
            with dve.Fori(0, 4) as j:
                v = ps[:, 0:2 * BANK].rearrange("p (g d) -> p g d", d=DH)

                def by_head(n):
                    return s_stat[:, n].unsqueeze(2).broadcast_to([P, 16, DH])

                dve.wait_ge(s_turned, j + 1 + 1)
                dve.tensor_reduce(s_stat[:, 0], v, AX, ALU.add).then_inc(s_stats, 1)
                dve.wait_ge(s_stats, 6 * j + 1)
                dve.tensor_scalar(s_stat[:, 1], s_stat[:, 0], 1.0 / DH, None, ALU.mult).then_inc(s_stats, 1)
                dve.wait_ge(s_stats, 6 * j + 2)
                dve.tensor_tensor(s_ctr[:], v, by_head(1), ALU.subtract).then_inc(s_stats, 1)
                dve.wait_ge(s_squared, j + 1)
                dve.tensor_reduce(s_stat[:, 2], s_sq[:], AX, ALU.add).then_inc(s_stats, 1)
                dve.wait_ge(s_std, j + 1)
                dve.reciprocal(s_stat[:, 3], s_stat[:, 3]).then_inc(s_stats, 1)
                dve.wait_ge(s_stats, 6 * j + 5)
                dve.tensor_tensor(s_ctr[:], s_ctr[:], by_head(3), ALU.mult).then_inc(s_stats, 1)
                dve.wait_ge(s_given, 48 * j + 48)
                dve.wait_ge(s_mixed, j + 1)
                dve.wait_ge(s_low, j + 1)
                for e in range(2):
                    r = slice(e * DH, (e + 1) * DH)
                    got = ps[r, 4 * BANK:].rearrange("p (n e t) -> p n e t", e=2, t=P)[:, :, e]
                    dve.scalar_tensor_tensor(s_y[r].rearrange("p (n t) -> p n t", t=P), got, vec[r, bass.ds(j + V_LNG, 1)],
                                             s_b[r].unsqueeze(1).broadcast_to([DH, QB, P]), ALU.mult, ALU.add).then_inc(s_gated, 1)
                dve.wait_ge(s_gated, 4 * j + 2)
                dve.tensor_tensor(s_y[:], s_y[:], s_u[:], ALU.mult).then_inc(s_gated, 1)
                dve.wait_ge(s_gated, 4 * j + 3)
                dve.tensor_copy(hh[:, bass.ds(j, 1), X_COLS], s_y[:].unsqueeze(1)).then_inc(s_gated, 1)
            with dve.Fori(0, 4) as j:
                def fa_max(u):
                    s, at, w = u % 3, 2 * (u % 2) * BANK, (u % QB + 1) * P
                    dve.wait_ge(fa.scored, 16 * j + (u + 1) + 1)
                    if u >= 3:
                        dve.wait_ge(fa.turned, 18 * j + (u - 1))
                    dve.tensor_scalar(a_s[:, s, 0:w], ps[:, at:at + w], -SCALE, HIGHEST, ALU.mult, ALU.min,
                                      accum_out=a_low[:, s:s + 1]).then_inc(fa.maxed, 1)

                for u in range(2 * QB):
                    fa_max(u)
                dve.wait_ge(fa.exped, 16 * j + 16)
                dve.reciprocal(a_rec[:], a_sum[:]).then_inc(fa.normed, 1)
                dve.wait_ge(fa.normed, 2 * j + 1 + 1)
                dve.wait_ge(fa.mixed, 16 * j + 16 + 1)
                dve.tensor_tensor(a_o[:], bank(6, 2).rearrange("p (i a d) -> p i a d", a=2, d=DH),
                                  a_rec[:].rearrange("p a i -> p i a").unsqueeze(3).broadcast_to([P, QB, 2, DH]),
                                  ALU.mult).then_inc(fa.normed, 1)
                to = hh[:, bass.ds(j + 4, 1), X_COLS]
                dve.wait_ge(fa.turned, 18 * j + 18)
                dve.tensor_copy(to, bank(4, 2).unsqueeze(1)).then_inc(fa.kept, 1)
                dve.wait_ge(fa.kept, 2 * j + 1 + 1)
                dve.tensor_tensor(hl[:, bass.ds(j + 4, 1), X_COLS], bank(4, 2).unsqueeze(1), to.bitcast(F32), ALU.subtract).then_inc(fa.kept, 1)
            add_to_residual(dve, "w_out", ((X_COLS, 0, None),), "ffn", X_COLS)
            norm_scale(dve, "ffn", X_COLS)

            def ffn_taps(chunk, e, acc_use):
                for s in range(2):
                    tile = 2 * chunk + (s * FT + e)
                    dve.wait_ge(f_based[s], 2 * chunk + (e + 1))
                    dve.scalar_tensor_tensor(f_y[:, s, 1:], acc[s][:, 0:SEQ - 1], convv[:, bass.ds(tile + 2 * FT, 1)],
                                             f_y[:, s, 1:], ALU.mult, ALU.add).then_inc(f_tapped[s], 1)
                    dve.wait_ge(f_tapped[s], 2 * chunk + (e + 1))
                    dve.scalar_tensor_tensor(f_y[:, s, 2:], acc[s][:, 0:SEQ - 2], convv[:, bass.ds(tile, 1)],
                                             f_y[:, s, 2:], ALU.mult, ALU.add).then_inc(acc_free[s], 1)
                dve.wait_ge(f_gate, 2 * chunk + (e + 1))
                dve.wait_ge(acc_free[1], acc_use + (A0["ffn"][1] + 1) + 1)
                dve.wait_ge(f_low, 2 * chunk + e)
                dve.tensor_tensor(f_act[:], f_g[:], f_y[:, 1], ALU.mult).then_inc(f_mult, 1)

            def ffn_high(chunk, e):
                dve.wait_ge(f_mult, 2 * chunk + (e + 1))
                dve.wait_ge(d_used, chunk + 1)
                dve.tensor_copy(f_hi[:, e], f_act[:]).then_inc(f_high, 1)

            def ffn_down(chunk, norm=None):
                for m in range(KT):
                    if m < KT - 1:
                        dve.wait_ge(f_down, 7 * chunk + (m + 1))
                    else:
                        dve.wait_ge(d_used, chunk + 1 + 1)
                    dve.tensor_tensor(res[:, m, X_COLS], acc[m % 2][:, 0:SEQ], res[:, m, X_COLS], ALU.add).then_inc(acc_free[m % 2], 1)
                    if norm and m == 0:
                        norm_start(dve, norm, X_COLS)
                    if norm and m:
                        norm_add(dve, norm, X_COLS, (m - 1) // 2, (m - 1) % 2)
                if norm:
                    norm_add(dve, norm, X_COLS, KT // 2 - 1, 1)

            ffn_taps(0, 0, 0)
            ffn_high(0, 0)
            ffn_taps(0, 1, 1)
            ffn_high(0, 1)
            with dve.Fori(1, CHUNKS) as c:
                ffn_taps(c, 0, 6 * c - 4)
                ffn_down(c - 1)
                ffn_high(c, 0)
                ffn_taps(c, 1, 6 * c + 1)
                ffn_high(c, 1)
            ffn_down(CHUNKS - 1, "fin")
            norm_scale(dve, "fin", X_COLS)
            for s in range(2):
                dve.wait_ge(n_gained[s], 4 * (NORMS["fin"] + 1) + 1)
            norm_add_all(dve, "a", ALL_COLS)
            norm_scale(dve, "a", ALL_COLS)
            for s in range(2):
                dve.wait_ge(n_low[s], 4 * (SPLITS["a"] + 1) + 1)
            dve.wait_ge(consts_in, 16 * 12)
            rotate(dve, "a_qk", 16, CTX)
            keep_modulation(dve, 1)
            dve.wait_ge(lam_step, 3)

            def da_max(h, u):
                s, w = u % 3, da_tiles(u) * P
                if u >= 3:
                    dve.wait_ge(da.turned, da_turn(h, "p", u - 3, len(batches(da_tiles(u - 3))) - 1)[2])
                dve.wait_ge(da.scored, 10 * h + (u + 1) + 1)
                dve.tensor_scalar(d_p0[:, s, 0:w], acc[0][:, 0:w], -SCALE, HIGHEST, ALU.mult, ALU.min,
                                  accum_out=d_low[:, s, 0:1]).then_inc(da.maxed, 1)
                if u >= 2:
                    dve.wait_ge(da_weighed, 30 * h + (3 * u - 3))
                dve.wait_ge(da_scored1, 10 * h + (u + 1) + 1)
                dve.tensor_scalar(d_p1[:, u % 2, 0:w], acc[1][:, 0:w], -SCALE, HIGHEST, ALU.mult, ALU.min,
                                  accum_out=d_low[:, s, 1:2]).then_inc(da_maxed1, 1)

            def da_weigh(h, u):
                s, w = u % 3, da_tiles(u) * P
                dve.wait_ge(da_exped1, 10 * h + (u + 1))
                dve.reciprocal(d_rec[:, s, 0:1], d_sum[:, 1, u:u + 1]).then_inc(da_weighed, 1)
                dve.wait_ge(da.exped, 10 * h + (u + 1))
                dve.wait_ge(da_weighed, 30 * h + (3 * u + 1))
                dve.scalar_tensor_tensor(d_rec[:, s, 1:2], d_sum[:, 0, u:u + 1], neg_lam[:], d_rec[:, s, 0:1],
                                         ALU.mult, ALU.mult).then_inc(da_weighed, 1)
                dve.wait_ge(da_weighed, 30 * h + (3 * u + 2))
                dve.scalar_tensor_tensor(d_p0[:, s, 0:w], d_p1[:, u % 2, 0:w], d_rec[:, s, 1:2], d_p0[:, s, 0:w], ALU.mult,
                                         ALU.add).then_inc(da_weighed, 1)

            def da_mean(h):
                dve.wait_ge(da.normed, 4 * h - 3)
                b, before, _ = da_turn(h - 1, "m", TOK // P - 1)
                dve.wait_ge(da_free[b], before + 1 + 1)
                dve.scalar_tensor_tensor(d_rs[:], d_ss[:], 1.0 / P, d_eps[:], ALU.mult, ALU.add).then_inc(da.normed, 1)

            def da_norm(h):
                dve.wait_ge(da_rms, h)
                dve.reciprocal(d_rs[:], d_rs[:]).then_inc(da.normed, 1)
                dve.wait_ge(da.normed, 4 * h - 1)
                dve.tensor_tensor(d_o[:], d_o[:], d_rs[:].unsqueeze(2).broadcast_to([P, TOK // P, P]), ALU.mult).then_inc(da.normed, 1)

            def da_gate(h):
                dve.wait_ge(da_gloaded, 16 * h)
                for n, blocks in enumerate(batches(TOK // P)):
                    b, _, turned = da_turn(h, "o", n)
                    cols = slice(blocks.start * P, blocks.stop * P)
                    dve.wait_ge(da.turned, turned)
                    dve.scalar_tensor_tensor(d_g[:, cols], bank(6 + b)[:, 0:len(blocks) * P], subg[:], d_g[:, cols],
                                             ALU.mult, ALU.mult).then_inc(da_free[b], 1)
                for n in range(len(batches(TOK // P)))[-2:]:
                    b, before, _ = da_turn(h, "o", n)
                    dve.wait_ge(da_free[b], before + 1 + 1)
                dve.tensor_copy(hh[:, bass.ds(h - 1, 1)], d_g.unsqueeze(1)).then_inc(da_gated, 1)

            def da_head(h, first):
                da_max(h, 0)
                if not first:
                    da_mean(h)
                da_max(h, 1)
                if not first:
                    da_norm(h)
                for u in range(TOK // P):
                    da_weigh(h, u)
                    if u + LEAD < TOK // P:
                        da_max(h, u + LEAD)
                    if u == 1 and not first:
                        da_gate(h)
                dve.scalar_tensor_tensor(d_eps[:], d_sum[:, 0], SUB_EPS, d_sum[:, 0], ALU.mult, ALU.mult).then_inc(da.normed, 1)

            da_head(0, True)
            with dve.Fori(1, DA_HEADS) as h:
                da_head(h, False)
            da_mean(DA_HEADS)
            da_norm(DA_HEADS)
            da_gate(DA_HEADS)
            add_to_residual(dve, "a_out", ((X_COLS, CTX, (0, 0)), (slice(0, CTX), 0, (0, 1))), "b", ALL_COLS)
            norm_scale(dve, "b", ALL_COLS)
            for s in range(2):
                dve.wait_ge(n_low[s], 4 * (SPLITS["b"] + 1) + 1)
            dve.wait_ge(consts_in, 16 * 14)
            rotate(dve, "b_q", 8, 0)
            rotate(dve, "b_k", 2, CTX)
            with dve.Fori(0, 4) as h:
                def ba_max(u):
                    i, a = divmod(u, 4)
                    s, at, w = u % 3, 2 * (u % 2) * BANK, len(window_tiles(i)) * P
                    dve.wait_ge(ba.scored, 32 * h + (u + 1) + 1)
                    if u >= 3:
                        dve.wait_ge(ba.turned, 33 * h + (u - 1))
                    dve.tensor_scalar(b_s[:, s, 0:w], ps[:, at:at + w], -SCALE, HIGHEST, ALU.mult, ALU.min,
                                      accum_out=b_low[:, 0, s:s + 1]).then_inc(ba.maxed, 1)
                    dve.wait_ge(ba.maxed, 32 * h + (u + 1))
                    dve.tensor_scalar(b_low[:, 1, s:s + 1], sinks[:, bass.ds(4 * h + a, 1)], -1.0, b_low[:, 0, s:s + 1],
                                      ALU.mult, ALU.min).then_inc(ba_biased, 1)

                def ba_norm(i):
                    dve.wait_ge(ba.exped, 64 * h + (8 * i + 8))
                    dve.tensor_tensor(b_rec[:, 0], b_sum[:, i % 2], b_sink[:, i % 2], ALU.add).then_inc(ba.normed, 1)
                    dve.wait_ge(ba.normed, 24 * h + (3 * i + 1))
                    dve.reciprocal(b_rec[:, 1], b_rec[:, 0]).then_inc(ba.normed, 1)
                    dve.wait_ge(ba.normed, 24 * h + (3 * i + 2))
                    dve.wait_ge(ba.mixed, 32 * h + (4 * i + 4) + 1)
                    dve.tensor_tensor(b_o[:].rearrange("p (a d) -> p a d", d=DH), bank(6 + i % 2)[:, 0:2 * P].rearrange("p (a d) -> p a d", d=DH),
                                      b_rec[:, 1].unsqueeze(2).broadcast_to([P, 4, DH]), ALU.mult).then_inc(ba.normed, 1)

                def ba_keep(i):
                    cols = slice(CTX + i * P, CTX + (i + 1) * P)
                    dve.wait_ge(ba_gloaded, 16 * h + 16)
                    dve.wait_ge(ba_o_turned, 8 * h + (i + 1))
                    dve.wait_ge(ba.low, 8 * h + i + 1)
                    dve.tensor_tensor(b_y[:], bank(6 + i % 2)[:, 2 * P:4 * P].rearrange("p (t q) -> p t q", t=2),
                                      b_g[:, :, i * P:(i + 1) * P], ALU.mult).then_inc(ba.kept, 1)
                    dve.wait_ge(ba.kept, 16 * h + (2 * i + 1))
                    dve.tensor_copy(hh[:, bass.ds(2 * h, 2), cols], b_y[:]).then_inc(ba.kept, 1)

                for u in range(LEAD):
                    ba_max(u)
                for u in range(4 * QB):
                    i, a = divmod(u, 4)
                    if u + LEAD < 4 * QB:
                        ba_max(u + LEAD)
                    if i and a == 0:
                        ba_norm(i - 1)
                    if i and a == 2:
                        ba_keep(i - 1)
                ba_norm(QB - 1)
                ba_keep(QB - 1)
            add_to_residual(dve, "b_out", ((X_COLS, 0, (1, 0)),), "out", X_COLS)
            norm_scale(dve, "out", X_COLS)


_INS = [
    "x", "norm_mix_g", "w_in", "f_bias", "sg_ln_g", "sg_w", "sg_b", "w_out", "norm_ffn_g", "w_up", "w_conv", "b_conv", "w_down",
    "norm_final_g", "c_2", "ctx_2", "c_ctx_2", "w_mod_2", "b_mod_2", "norm_g_2", "w_o_2", "a_w_in_2", "a_lambda_q1_2",
    "a_lambda_k1_2", "a_lambda_q2_2", "a_lambda_k2_2", "a_subln_g_2", "b_w_in_2", "b_sink_2", "final_g_2",
]


def constants():
    import numpy as np

    n = np.arange(P)
    causal = np.where(n[None, :] <= n[:, None], 0.0, -1e30)
    before = np.where(n[None, :] >= n[:, None], 0.0, -1e30)
    half, grid = DH // 2, 64
    inv = (np.float32(10000.0) ** (-np.arange(0, half, 2, dtype=np.float32) / np.float32(half))).astype(np.float32)
    t = np.arange(SEQ)
    place = np.stack([t // grid, t % grid]).astype(np.float32)
    angle = np.stack([place[(f % DH) // half] * inv[f % 16] for f in range(P)]).astype(np.float32)
    sign = np.where(n % half < 16, -1.0, 1.0)[:, None]
    return {
        "const_ident": np.eye(P, dtype=np.float32), "const_swap": np.eye(P, dtype=np.float32)[n ^ 16],
        "const_causal": causal.astype(np.float32), "const_before": before.astype(np.float32), "const_cos": np.cos(angle).astype(np.float32),
        "const_sin": (sign * np.sin(angle)).astype(np.float32),
    }


def kernel(**inputs):
    import numpy as np
    import concourse.bacc as bacc
    from concourse.bass_utils import run_bass_kernel_spmd

    nc = bacc.Bacc("TRN2", target_bir_lowering=False, num_devices=1)
    arrays = {f"in_{name}": np.ascontiguousarray(inputs[name]) for name in _INS}
    arrays.update(constants())
    args = [nc.dram_tensor(name, a.shape, F32, kind="ExternalInput").ap() for name, a in arrays.items()]
    args.append(nc.dram_tensor("out_rows", (1, SEQ, D), F32, kind="ExternalOutput").ap())
    two_block_kernel(nc, *args)
    got = run_bass_kernel_spmd(nc, [arrays], core_ids=[0])
    return got.results[0]["out_rows"]
```
